# Optimizing a Trainium2 kernel written in Bass

```python
import math
import jax
import jax.numpy as jnp
from jax import lax
import numpy as np
import jax, jax.numpy as jnp

D_MODEL = 1024
BATCH = 1
SEQ = 256
DEPTH = 2

A_HEADS = 4
A_DK = 64
A_DV = 64
B_HEADS = 8
B_GROUPS = 2
B_HPG = B_HEADS // B_GROUPS
B_DH = 64
C_HEADS = 4
C_DH = 64
MIX_WIDTH = A_HEADS * A_DV + B_HEADS * B_DH + C_HEADS * C_DH
D_FF = 4 * D_MODEL
ROPE_THETA = 500000.0
ROT_DIM = B_DH // 4
EPS = 1e-6
NEG_BIG = -1e30
POS_BIG = 1e30
TINY = 1e-30
HGRN_CHUNK = 64
CMP_BLOCK = 32
CMP_STRIDE = 16
CMP_HIDDEN = 128
SEL_BLOCK = 64
SEL_TOPK = 16
WINDOW = 512
NSA_QBLOCK = 64
FOX_QBLOCK = 128

IN_SPLIT = (
    A_HEADS * A_DK, A_HEADS * A_DK, A_HEADS * A_DV, A_HEADS * A_DV,
    B_HEADS * B_DH,
    B_GROUPS * B_DH, B_GROUPS * B_DH,
    B_GROUPS * B_DH, B_GROUPS * B_DH,
    B_GROUPS * B_DH, B_GROUPS * B_DH,
    3 * B_HEADS,
    C_HEADS * C_DH, C_HEADS * C_DH, C_HEADS * C_DH, C_HEADS,
)
IN_WIDTH = sum(IN_SPLIT)


def _rmsnorm(x, g):
    xf = x.astype(jnp.float32)
    var = jnp.mean(xf * xf, axis=-1, keepdims=True)
    return xf * lax.rsqrt(var + EPS) * g.astype(jnp.float32)

def _rope_partial(x, pos):
    half = ROT_DIM // 2
    inv_freq = jnp.power(jnp.float32(ROPE_THETA), -jnp.arange(0, ROT_DIM, 2, dtype=jnp.float32) / ROT_DIM)
    ang = pos.astype(jnp.float32)[:, None] * inv_freq[None, :]
    ang = ang.reshape((1, pos.shape[0]) + (1,) * (x.ndim - 3) + (half,))
    cos, sin = jnp.cos(ang), jnp.sin(ang)
    x1 = x[..., :half]
    x2 = x[..., half:ROT_DIM]
    return jnp.concatenate([x1 * cos - x2 * sin, x2 * cos + x1 * sin, x[..., ROT_DIM:]], axis=-1)

def _masked_softmax(logits, mask):
    logits = jnp.where(mask, logits.astype(jnp.float32), NEG_BIG)
    m = jnp.max(logits, axis=-1, keepdims=True)
    p = jnp.where(mask, jnp.exp(logits - m), 0.0)
    return p / jnp.maximum(jnp.sum(p, axis=-1, keepdims=True), TINY)

def _hgrn2(q, f_logit, i_val, g_out, lb, onorm_g):
    bsz, seq = q.shape[0], q.shape[1]
    lb = lb.reshape(A_HEADS, A_DK)
    z = f_logit.astype(jnp.float32).reshape(bsz, seq, A_HEADS, A_DK)
    f = lb + (1.0 - lb) * jax.nn.sigmoid(z)
    log_f = jnp.log(jnp.maximum(f, TINY))
    k = (1.0 - lb) * jax.nn.sigmoid(-z)
    qf = q.astype(jnp.float32).reshape(bsz, seq, A_HEADS, A_DK) * (A_DK ** -0.5)
    v = i_val.astype(jnp.float32).reshape(bsz, seq, A_HEADS, A_DV)
    n_chunks = seq // HGRN_CHUNK

    def to_chunks(t):
        return t.reshape(bsz, n_chunks, HGRN_CHUNK, A_HEADS, -1).transpose(1, 0, 3, 2, 4)

    causal = jnp.tril(jnp.ones((HGRN_CHUNK, HGRN_CHUNK), dtype=bool))

    def step(state, inp):
        qc, kc, vc, gc = inp
        G = jnp.cumsum(gc, axis=2)
        o_inter = jnp.einsum('bhtk,bhkv->bhtv', qc * jnp.exp(G), state)
        diff = G[:, :, :, None, :] - G[:, :, None, :, :]
        decay = jnp.exp(jnp.where(causal[:, :, None], diff, NEG_BIG))
        scores = jnp.einsum('bhtk,bhsk,bhtsk->bhts', qc, kc, decay)
        o_intra = jnp.einsum('bhts,bhsv->bhtv', scores, vc)
        g_last = G[:, :, -1:, :]
        k_dec = kc * jnp.exp(g_last - G)
        state = state * jnp.exp(g_last[:, :, 0, :])[..., None] + jnp.einsum('bhsk,bhsv->bhkv', k_dec, vc)
        return state, o_inter + o_intra

    state0 = jnp.zeros((bsz, A_HEADS, A_DK, A_DV), jnp.float32)
    _, o = lax.scan(step, state0, (to_chunks(qf), to_chunks(k), to_chunks(v), to_chunks(log_f)))
    o = o.transpose(1, 0, 3, 2, 4).reshape(bsz, seq, A_HEADS, A_DV)
    gate = jax.nn.silu(g_out.astype(jnp.float32)).reshape(bsz, seq, A_HEADS, A_DV)
    o = _rmsnorm(o, onorm_g) * gate
    return o.reshape(bsz, seq, A_HEADS * A_DV)

def _nsa(q, k_cmp, v_cmp, k_slc, v_slc, k_win, v_win, gates, qn_g, kn_g, cmp_pos, cmp_w1, cmp_w2):
    bsz, seq = q.shape[0], q.shape[1]
    pos = jnp.arange(seq)
    qh = _rope_partial(_rmsnorm(q.reshape(bsz, seq, B_GROUPS, B_HPG, B_DH), qn_g), pos) * (B_DH ** -0.5)
    ks = _rope_partial(_rmsnorm(k_slc.reshape(bsz, seq, B_GROUPS, B_DH), kn_g), pos)
    kw = _rope_partial(_rmsnorm(k_win.reshape(bsz, seq, B_GROUPS, B_DH), kn_g), pos)
    vs = v_slc.astype(jnp.float32).reshape(bsz, seq, B_GROUPS, B_DH)
    vw = v_win.astype(jnp.float32).reshape(bsz, seq, B_GROUPS, B_DH)

    n_sub = CMP_BLOCK // CMP_STRIDE
    n_cmp = seq // CMP_STRIDE - n_sub + 1

    def compress(t, which):
        sub = t.astype(jnp.float32).reshape(bsz, seq // CMP_STRIDE, CMP_STRIDE, B_GROUPS, B_DH)
        blocks = jnp.concatenate([sub[:, m:m + n_cmp] for m in range(n_sub)], axis=2)
        blocks = blocks + cmp_pos[which][None, None, :, None, :]
        flat = blocks.transpose(0, 1, 3, 2, 4).reshape(bsz, n_cmp, B_GROUPS, CMP_BLOCK * B_DH)
        hidden = jax.nn.gelu(flat @ cmp_w1[which])
        return hidden @ cmp_w2[which]

    cmp_end = jnp.arange(n_cmp) * CMP_STRIDE + CMP_BLOCK - 1
    kc = _rope_partial(_rmsnorm(compress(k_cmp.reshape(bsz, seq, B_GROUPS, B_DH), 0), kn_g), cmp_end)
    vc = compress(v_cmp.reshape(bsz, seq, B_GROUPS, B_DH), 1)

    n_sel = seq // SEL_BLOCK
    ci = np.arange(n_cmp)[:, None]
    sj = np.arange(n_sel)[None, :]
    c_start = ci * CMP_STRIDE
    overlap = jnp.asarray(((c_start <= sj * SEL_BLOCK + SEL_BLOCK - 1)
                           & (c_start + CMP_BLOCK - 1 >= sj * SEL_BLOCK)).astype(np.float32))
    topk = min(SEL_TOPK, n_sel)
    kb = ks.reshape(bsz, n_sel, SEL_BLOCK, B_GROUPS, B_DH).transpose(0, 3, 1, 2, 4)
    vb = vs.reshape(bsz, n_sel, SEL_BLOCK, B_GROUPS, B_DH).transpose(0, 3, 1, 2, 4)
    kw_pad = jnp.pad(kw, ((0, 0), (WINDOW, 0), (0, 0), (0, 0)))
    vw_pad = jnp.pad(vw, ((0, 0), (WINDOW, 0), (0, 0), (0, 0)))
    gate = jax.nn.sigmoid(gates.astype(jnp.float32)).reshape(bsz, seq, 3, B_GROUPS, B_HPG)
    b_idx = jnp.arange(bsz)[:, None, None, None]
    g_idx = jnp.arange(B_GROUPS)[None, :, None, None]
    sel_off = jnp.arange(SEL_BLOCK)
    win_off = jnp.arange(WINDOW + NSA_QBLOCK)
    blk_ids = jnp.arange(n_sel)

    def block_fn(blk):
        q0 = blk * NSA_QBLOCK
        t = q0 + jnp.arange(NSA_QBLOCK)
        qb = lax.dynamic_slice_in_dim(qh, q0, NSA_QBLOCK, axis=1)
        s_c = jnp.einsum('bqghd,bngd->bghqn', qb, kc)
        p_c = _masked_softmax(s_c, cmp_end[None, :] <= t[:, None])
        o_c = jnp.einsum('bghqn,bngd->bqghd', p_c, vc)
        imp = jnp.einsum('bghqn,nj->bgqj', p_c, overlap)
        cur = (t // SEL_BLOCK)[:, None]
        forced = (blk_ids[None, :] == 0) | (blk_ids[None, :] == cur) | (blk_ids[None, :] == cur - 1)
        imp = jnp.where(forced, POS_BIG, imp)
        imp = jnp.where(blk_ids[None, :] * SEL_BLOCK > t[:, None], NEG_BIG, imp)
        vals, idx = lax.top_k(imp, topk)
        k_sel = kb[b_idx, g_idx, idx]
        v_sel = vb[b_idx, g_idx, idx]
        s_s = jnp.einsum('bqghd,bgqkld->bghqkl', qb, k_sel).reshape(bsz, B_GROUPS, B_HPG, NSA_QBLOCK, topk * SEL_BLOCK)
        key_pos = idx[..., None] * SEL_BLOCK + sel_off
        m_s = (key_pos <= t[None, None, :, None, None]) & (vals > NEG_BIG * 0.5)[..., None]
        m_s = m_s.reshape(bsz, B_GROUPS, 1, NSA_QBLOCK, topk * SEL_BLOCK)
        p_s = _masked_softmax(s_s, m_s).reshape(bsz, B_GROUPS, B_HPG, NSA_QBLOCK, topk, SEL_BLOCK)
        o_s = jnp.einsum('bghqkl,bgqkld->bqghd', p_s, v_sel)
        kwb = lax.dynamic_slice_in_dim(kw_pad, q0, WINDOW + NSA_QBLOCK, axis=1)
        vwb = lax.dynamic_slice_in_dim(vw_pad, q0, WINDOW + NSA_QBLOCK, axis=1)
        kpos = q0 - WINDOW + win_off
        m_w = (kpos[None, :] >= 0) & (kpos[None, :] <= t[:, None]) & (kpos[None, :] > t[:, None] - WINDOW)
        s_w = jnp.einsum('bqghd,bkgd->bghqk', qb, kwb)
        p_w = _masked_softmax(s_w, m_w)
        o_w = jnp.einsum('bghqk,bkgd->bqghd', p_w, vwb)
        gb = lax.dynamic_slice_in_dim(gate, q0, NSA_QBLOCK, axis=1)
        return gb[:, :, 0, :, :, None] * o_c + gb[:, :, 1, :, :, None] * o_s + gb[:, :, 2, :, :, None] * o_w

    out = lax.map(block_fn, jnp.arange(seq // NSA_QBLOCK))
    return out.transpose(1, 0, 2, 3, 4, 5).reshape(bsz, seq, B_HEADS * B_DH)

def _fox(q, k, v, f_logit, qn_g, kn_g, fb):
    bsz, seq = q.shape[0], q.shape[1]
    qh = _rmsnorm(q.reshape(bsz, seq, C_HEADS, C_DH), qn_g) * (C_DH ** -0.5)
    kh = _rmsnorm(k.reshape(bsz, seq, C_HEADS, C_DH), kn_g)
    vh = v.astype(jnp.float32).reshape(bsz, seq, C_HEADS, C_DH)
    log_f = jax.nn.log_sigmoid(f_logit.astype(jnp.float32) + fb.astype(jnp.float32))
    c = jnp.cumsum(log_f, axis=1).transpose(0, 2, 1)
    kpos = jnp.arange(seq)

    def block_fn(blk):
        q0 = blk * FOX_QBLOCK
        t = q0 + jnp.arange(FOX_QBLOCK)
        qb = lax.dynamic_slice_in_dim(qh, q0, FOX_QBLOCK, axis=1)
        cq = lax.dynamic_slice_in_dim(c, q0, FOX_QBLOCK, axis=2)
        s = jnp.einsum('bqhd,bkhd->bhqk', qb, kh) + cq[..., None] - c[:, :, None, :]
        p = _masked_softmax(s, kpos[None, :] <= t[:, None])
        return jnp.einsum('bhqk,bkhd->bqhd', p, vh)

    out = lax.map(block_fn, jnp.arange(seq // FOX_QBLOCK))
    return out.transpose(1, 0, 2, 3, 4).reshape(bsz, seq, C_HEADS * C_DH)

def first_inputs(seed: int = 0) -> dict:
    key = jax.random.key(seed)
    ks = jax.random.split(key, 17)

    def nrm(k, shape, scale):
        return jax.random.normal(k, shape, jnp.float32) * scale

    return {
        'x': nrm(ks[0], (BATCH, SEQ, D_MODEL), 1.0),
        'norm1_g': 1.0 + nrm(ks[1], (DEPTH, D_MODEL), 0.02),
        'w_in': nrm(ks[2], (DEPTH, D_MODEL, IN_WIDTH), D_MODEL ** -0.5),
        'hgrn_lb_logits': nrm(ks[3], (DEPTH, A_HEADS * A_DK), 0.1),
        'hgrn_onorm_g': 1.0 + nrm(ks[4], (DEPTH, A_DV), 0.02),
        'nsa_qn_g': 1.0 + nrm(ks[5], (DEPTH, B_DH), 0.02),
        'nsa_kn_g': 1.0 + nrm(ks[6], (DEPTH, B_DH), 0.02),
        'nsa_cmp_pos': nrm(ks[7], (DEPTH, 2, CMP_BLOCK, B_DH), 0.02),
        'nsa_cmp_w1': nrm(ks[8], (DEPTH, 2, CMP_BLOCK * B_DH, CMP_HIDDEN), (CMP_BLOCK * B_DH) ** -0.5),
        'nsa_cmp_w2': nrm(ks[9], (DEPTH, 2, CMP_HIDDEN, B_DH), CMP_HIDDEN ** -0.5),
        'fox_qn_g': 1.0 + nrm(ks[10], (DEPTH, C_DH), 0.02),
        'fox_kn_g': 1.0 + nrm(ks[11], (DEPTH, C_DH), 0.02),
        'fox_fb': 2.0 + nrm(ks[12], (DEPTH, C_HEADS), 0.1),
        'w_o': nrm(ks[13], (DEPTH, MIX_WIDTH, D_MODEL), MIX_WIDTH ** -0.5),
        'norm2_g': 1.0 + nrm(ks[14], (DEPTH, D_MODEL), 0.02),
        'w_up': nrm(ks[15], (DEPTH, D_MODEL, D_FF), D_MODEL ** -0.5),
        'w_down': nrm(ks[16], (DEPTH, D_FF, D_MODEL), D_FF ** -0.5),
    }

def first_block(x, norm1_g, w_in, hgrn_lb_logits, hgrn_onorm_g, nsa_qn_g, nsa_kn_g, nsa_cmp_pos,
              nsa_cmp_w1, nsa_cmp_w2, fox_qn_g, fox_kn_g, fox_fb, w_o, norm2_g, w_up, w_down):
    lb_p = jax.nn.softmax(hgrn_lb_logits.astype(jnp.float32), axis=0)
    lb_all = jnp.cumsum(lb_p, axis=0) - lb_p[0:1]
    split_at = [int(v) for v in np.cumsum(IN_SPLIT)[:-1]]
    for layer in range(DEPTH):
        h = _rmsnorm(x, norm1_g[layer]).astype(x.dtype)
        proj = h @ w_in[layer]
        (aq, af, ai, ag, bq, bkc, bvc, bks, bvs, bkw, bvw, bg,
         cq, ck, cv, cf) = jnp.split(proj, split_at, axis=-1)
        o_a = _hgrn2(aq, af, ai, ag, lb_all[layer], hgrn_onorm_g[layer])
        o_b = _nsa(bq, bkc, bvc, bks, bvs, bkw, bvw, bg, nsa_qn_g[layer], nsa_kn_g[layer],
                   nsa_cmp_pos[layer], nsa_cmp_w1[layer], nsa_cmp_w2[layer])
        o_c = _fox(cq, ck, cv, cf, fox_qn_g[layer], fox_kn_g[layer], fox_fb[layer])
        mix = jnp.concatenate([o_a, o_b, o_c], axis=-1).astype(x.dtype)
        x = x + (mix @ w_o[layer]).astype(x.dtype)
        h2 = _rmsnorm(x, norm2_g[layer]).astype(x.dtype)
        x = x + (jnp.square(jax.nn.relu(h2 @ w_up[layer])) @ w_down[layer]).astype(x.dtype)
    return x


CTX_LEN = 256
GRID_W = 64
HALF = 0.5
D_FF_2 = 2816
N_ADA = 9
CONV_CH = 384
CONV_K = 31
N_HEADS = 8
Q_LORA = 384
KV_LORA = 256
QK_NOPE = 64
QK_ROPE = 32
V_DIM = 64
ROPE_AXIS = QK_ROPE // 2
ROPE_BASE = 10000.0
ATTN_SCALE = (QK_NOPE + QK_ROPE) ** -0.5
Q_BLOCK = 128
FOURIER_GROUPS = 4
FOURIER_GROUP_CH = 128
FOURIER_WIDTH = FOURIER_GROUPS * FOURIER_GROUP_CH
MIX_WIDTH_2 = 2 * CONV_CH + Q_LORA + KV_LORA + QK_ROPE + FOURIER_WIDTH
N_BRANCH = 3


def rms_norm(x, g):
    xf = x.astype(jnp.float32)
    y = xf * lax.rsqrt(jnp.mean(xf * xf, axis=-1, keepdims=True) + EPS)
    return (y * g.astype(jnp.float32)).astype(x.dtype)

def layer_norm(x, g, b):
    xf = x.astype(jnp.float32)
    mu = jnp.mean(xf, axis=-1, keepdims=True)
    var = jnp.mean(jnp.square(xf - mu), axis=-1, keepdims=True)
    y = (xf - mu) * lax.rsqrt(var + EPS)
    return (y * g.astype(jnp.float32) + b.astype(jnp.float32)).astype(x.dtype)

def ada_norm(h, g, shift, scale):
    return rms_norm(h, g) * (1 + scale) + shift

def swiglu(x, w1, w3, w2):
    return (jax.nn.silu(x @ w1) * (x @ w3)) @ w2

def axial_rope_tables(n_tok, dtype):
    rows = n_tok // GRID_W
    row = jnp.broadcast_to(jnp.arange(rows, dtype=jnp.float32)[:, None], (rows, GRID_W)).reshape(-1)
    col = jnp.broadcast_to(jnp.arange(GRID_W, dtype=jnp.float32)[None, :], (rows, GRID_W)).reshape(-1)
    inv = 1.0 / (ROPE_BASE ** (jnp.arange(ROPE_AXIS // 2, dtype=jnp.float32) * 2.0 / ROPE_AXIS))
    ar = row[:, None] * inv
    ac = col[:, None] * inv
    ang = jnp.concatenate([ar, ar, ac, ac], axis=-1)
    return jnp.cos(ang).astype(dtype), jnp.sin(ang).astype(dtype)

def rotate_half_axial(x):
    xr = x.reshape(x.shape[:-1] + (2, 2, ROPE_AXIS // 2))
    xr = jnp.concatenate([-xr[..., 1:2, :], xr[..., 0:1, :]], axis=-2)
    return xr.reshape(x.shape)

def apply_rope(x, cos, sin):
    return x * cos + rotate_half_axial(x) * sin

def split_mixing(z):
    o1 = 2 * CONV_CH
    o2 = o1 + Q_LORA
    o3 = o2 + KV_LORA
    o4 = o3 + QK_ROPE
    return z[..., :o1], z[..., o1:o2], z[..., o2:o3], z[..., o3:o4], z[..., o4:]

def conv_module(zc, w_dw, b_dw, ln_g, ln_b, w_pw, b_pw):
    a, gt = jnp.split(zc, 2, axis=-1)
    v = a * jax.nn.sigmoid(gt)
    v = lax.conv_general_dilated(v, w_dw[:, None, :].astype(v.dtype), window_strides=(1,),
                                 padding=[(CONV_K // 2, CONV_K // 2)],
                                 dimension_numbers=('NWC', 'WIO', 'NWC'),
                                 feature_group_count=CONV_CH) + b_dw
    v = layer_norm(v, ln_g, ln_b)
    return jax.nn.silu(v) @ w_pw + b_pw

def fourier_mix(zf, w, b):
    bsz, t, _ = zf.shape
    g = zf.reshape(bsz, t, FOURIER_GROUPS, FOURIER_GROUP_CH).astype(jnp.float32)
    f = jnp.fft.fftn(g, axes=(1, 3), norm='ortho').real.astype(zf.dtype)
    return f.reshape(bsz, t, FOURIER_WIDTH) @ w + b

def mla_q(cq, g_qn, w_uq, cos, sin):
    bsz, t, _ = cq.shape
    q = (rms_norm(cq, g_qn) @ w_uq).reshape(bsz, t, N_HEADS, QK_NOPE + QK_ROPE)
    if cos is None:
        return q
    q_nope, q_rope = q[..., :QK_NOPE], q[..., QK_NOPE:]
    return jnp.concatenate([q_nope, apply_rope(q_rope, cos[:, None, :], sin[:, None, :])], axis=-1)

def mla_kv(ckv, kr, g_kvn, w_ukv, cos, sin):
    bsz, t, _ = ckv.shape
    kv = (rms_norm(ckv, g_kvn) @ w_ukv).reshape(bsz, t, N_HEADS, QK_NOPE + V_DIM)
    k_nope, v = kv[..., :QK_NOPE], kv[..., QK_NOPE:]
    if cos is not None:
        kr = apply_rope(kr, cos, sin)
    k = jnp.concatenate([k_nope, jnp.broadcast_to(kr[:, :, None, :], (bsz, t, N_HEADS, QK_ROPE))], axis=-1)
    return k, v

def attend_dense(q, k, v):
    s = jnp.einsum('bqhd,bkhd->bhqk', q, k, preferred_element_type=jnp.float32) * ATTN_SCALE
    p = jax.nn.softmax(s, axis=-1).astype(v.dtype)
    o = jnp.einsum('bhqk,bkhd->bqhd', p, v)
    return o.reshape(o.shape[0], o.shape[1], N_HEADS * V_DIM)

def attend_blocked(q, k, v):
    bsz, s, _, dk = q.shape
    nb = s // Q_BLOCK
    qb = q.reshape(bsz, nb, Q_BLOCK, N_HEADS, dk).transpose(1, 0, 2, 3, 4)
    o = lax.map(lambda blk: attend_dense(blk, k, v), qb)
    return o.transpose(1, 0, 2, 3).reshape(bsz, s, N_HEADS * V_DIM)

def merge_branches(u, y_conv, y_mla, y_four, w_bg, b_bg, w_out):
    g = jax.nn.sigmoid(u @ w_bg + b_bg)
    g0, g1, g2 = jnp.split(g, N_BRANCH, axis=-1)
    return (g0 * y_conv + g1 * y_mla + g2 * y_four) @ w_out

def second_inputs(seed: int = 0) -> dict:
    key = jax.random.key(seed)
    ks = jax.random.split(key, 40)
    L, D = DEPTH, D_MODEL

    def nrm(k, shape, std):
        return jax.random.normal(k, shape, jnp.float32) * std

    def gain(k, shape):
        return 1.0 + nrm(k, shape, 0.02)

    return {
        'x': nrm(ks[0], (BATCH, SEQ, D), 1.0),
        'c': nrm(ks[1], (BATCH, D), 1.0),
        'ctx': nrm(ks[2], (BATCH, CTX_LEN, D), 1.0),
        'c_ctx': nrm(ks[3], (D,), 1.0),
        'w_ada': nrm(ks[4], (L, D, N_ADA * D), 0.5 * D ** -0.5),
        'b_ada': nrm(ks[5], (L, N_ADA * D), 0.02),
        'g_ffn1': gain(ks[6], (L, D)),
        'w1_ffn1': nrm(ks[7], (L, D, D_FF_2), D ** -0.5),
        'w3_ffn1': nrm(ks[8], (L, D, D_FF_2), D ** -0.5),
        'w2_ffn1': nrm(ks[9], (L, D_FF_2, D), D_FF_2 ** -0.5),
        'g_mix': gain(ks[10], (L, D)),
        'w_in': nrm(ks[11], (L, D, MIX_WIDTH_2), D ** -0.5),
        'w_dw': nrm(ks[12], (L, CONV_K, CONV_CH), CONV_K ** -0.5),
        'b_dw': nrm(ks[13], (L, CONV_CH), 0.02),
        'ln_g_conv': gain(ks[14], (L, CONV_CH)),
        'ln_b_conv': nrm(ks[15], (L, CONV_CH), 0.02),
        'w_pw_conv': nrm(ks[16], (L, CONV_CH, D), CONV_CH ** -0.5),
        'b_pw_conv': nrm(ks[17], (L, D), 0.02),
        'g_qnorm': gain(ks[18], (L, Q_LORA)),
        'w_uq': nrm(ks[19], (L, Q_LORA, N_HEADS * (QK_NOPE + QK_ROPE)), Q_LORA ** -0.5),
        'g_kvnorm': gain(ks[20], (L, KV_LORA)),
        'w_ukv': nrm(ks[21], (L, KV_LORA, N_HEADS * (QK_NOPE + V_DIM)), KV_LORA ** -0.5),
        'w_o_mla': nrm(ks[22], (L, N_HEADS * V_DIM, D), (N_HEADS * V_DIM) ** -0.5),
        'w_fourier': nrm(ks[23], (L, FOURIER_WIDTH, D), FOURIER_WIDTH ** -0.5),
        'b_fourier': nrm(ks[24], (L, D), 0.02),
        'w_bgate': nrm(ks[25], (L, D, N_BRANCH * D), D ** -0.5),
        'b_bgate': nrm(ks[26], (L, N_BRANCH * D), 0.02),
        'w_out': nrm(ks[27], (L, D, D), D ** -0.5),
        'g_ffn2': gain(ks[28], (L, D)),
        'w1_ffn2': nrm(ks[29], (L, D, D_FF_2), D ** -0.5),
        'w3_ffn2': nrm(ks[30], (L, D, D_FF_2), D ** -0.5),
        'w2_ffn2': nrm(ks[31], (L, D_FF_2, D), D_FF_2 ** -0.5),
        'g_final': gain(ks[32], (D,)),
    }

def second_block(x, c, ctx, c_ctx, w_ada, b_ada, g_ffn1, w1_ffn1, w3_ffn1, w2_ffn1, g_mix, w_in,
              w_dw, b_dw, ln_g_conv, ln_b_conv, w_pw_conv, b_pw_conv, g_qnorm, w_uq, g_kvnorm,
              w_ukv, w_o_mla, w_fourier, b_fourier, w_bgate, b_bgate, w_out, g_ffn2, w1_ffn2,
              w3_ffn2, w2_ffn2, g_final):
    cos, sin = axial_rope_tables(x.shape[1], x.dtype)
    h, hc = x, ctx
    for l in range(DEPTH):
        last = l == DEPTH - 1
        mod = jax.nn.silu(c) @ w_ada[l] + b_ada[l]
        sh1, sc1, gt1, sh2, sc2, gt2, sh3, sc3, gt3 = [m[:, None, :] for m in jnp.split(mod, N_ADA, axis=-1)]
        modc = jax.nn.silu(c_ctx) @ w_ada[l] + b_ada[l]
        csh1, csc1, cgt1, csh2, csc2, cgt2, csh3, csc3, cgt3 = jnp.split(modc, N_ADA, axis=-1)

        h = h + HALF * gt1 * swiglu(ada_norm(h, g_ffn1[l], sh1, sc1), w1_ffn1[l], w3_ffn1[l], w2_ffn1[l])
        hc = hc + HALF * cgt1 * swiglu(ada_norm(hc, g_ffn1[l], csh1, csc1), w1_ffn1[l], w3_ffn1[l], w2_ffn1[l])

        u = ada_norm(h, g_mix[l], sh2, sc2)
        uc = ada_norm(hc, g_mix[l], csh2, csc2)
        z_conv, z_cq, z_ckv, z_kr, z_four = split_mixing(u @ w_in[l])
        zc_conv, zc_cq, zc_ckv, zc_kr, zc_four = split_mixing(uc @ w_in[l])

        k_lat, v_lat = mla_kv(z_ckv, z_kr, g_kvnorm[l], w_ukv[l], cos, sin)
        k_ctx, v_ctx = mla_kv(zc_ckv, zc_kr, g_kvnorm[l], w_ukv[l], None, None)
        q_lat = mla_q(z_cq, g_qnorm[l], w_uq[l], cos, sin)
        attn = attend_blocked(q_lat, jnp.concatenate([k_ctx, k_lat], axis=1),
                              jnp.concatenate([v_ctx, v_lat], axis=1))
        y = merge_branches(u,
                           conv_module(z_conv, w_dw[l], b_dw[l], ln_g_conv[l], ln_b_conv[l], w_pw_conv[l], b_pw_conv[l]),
                           attn @ w_o_mla[l],
                           fourier_mix(z_four, w_fourier[l], b_fourier[l]),
                           w_bgate[l], b_bgate[l], w_out[l])
        h = h + gt2 * y
        if not last:
            q_ctx = mla_q(zc_cq, g_qnorm[l], w_uq[l], None, None)
            attn_c = attend_dense(q_ctx, k_ctx, v_ctx)
            yc = merge_branches(uc,
                                conv_module(zc_conv, w_dw[l], b_dw[l], ln_g_conv[l], ln_b_conv[l], w_pw_conv[l], b_pw_conv[l]),
                                attn_c @ w_o_mla[l],
                                fourier_mix(zc_four, w_fourier[l], b_fourier[l]),
                                w_bgate[l], b_bgate[l], w_out[l])
            hc = hc + cgt2 * yc

        h = h + HALF * gt3 * swiglu(ada_norm(h, g_ffn2[l], sh3, sc3), w1_ffn2[l], w3_ffn2[l], w2_ffn2[l])
        if not last:
            hc = hc + HALF * cgt3 * swiglu(ada_norm(hc, g_ffn2[l], csh3, csc3), w1_ffn2[l], w3_ffn2[l], w2_ffn2[l])
    return rms_norm(h, g_final)


def setup_inputs(seed=0):
    out = dict(first_inputs(seed))
    for name, value in second_inputs(seed + 1).items():
        if name != "x":
            out[name + "_2"] = value
    return out


def reference(
    x, norm1_g, w_in, hgrn_lb_logits, hgrn_onorm_g, nsa_qn_g, nsa_kn_g, nsa_cmp_pos, nsa_cmp_w1,
    nsa_cmp_w2, fox_qn_g, fox_kn_g, fox_fb, w_o, norm2_g, w_up, w_down, c_2, ctx_2, c_ctx_2,
    w_ada_2, b_ada_2, g_ffn1_2, w1_ffn1_2, w3_ffn1_2, w2_ffn1_2, g_mix_2, w_in_2, w_dw_2,
    b_dw_2, ln_g_conv_2, ln_b_conv_2, w_pw_conv_2, b_pw_conv_2, g_qnorm_2, w_uq_2, g_kvnorm_2,
    w_ukv_2, w_o_mla_2, w_fourier_2, b_fourier_2, w_bgate_2, b_bgate_2, w_out_2, g_ffn2_2,
    w1_ffn2_2, w3_ffn2_2, w2_ffn2_2, g_final_2,
):
    x = first_block(
        x, norm1_g, w_in, hgrn_lb_logits, hgrn_onorm_g, nsa_qn_g, nsa_kn_g, nsa_cmp_pos,
        nsa_cmp_w1, nsa_cmp_w2, fox_qn_g, fox_kn_g, fox_fb, w_o, norm2_g, w_up, w_down,
    )
    return second_block(
        x, c_2, ctx_2, c_ctx_2, w_ada_2, b_ada_2, g_ffn1_2, w1_ffn1_2, w3_ffn1_2, w2_ffn1_2,
        g_mix_2, w_in_2, w_dw_2, b_dw_2, ln_g_conv_2, ln_b_conv_2, w_pw_conv_2, b_pw_conv_2,
        g_qnorm_2, w_uq_2, g_kvnorm_2, w_ukv_2, w_o_mla_2, w_fourier_2, b_fourier_2, w_bgate_2,
        b_bgate_2, w_out_2, g_ffn2_2, w1_ffn2_2, w3_ffn2_2, w2_ffn2_2, g_final_2,
    )


_drawn_inputs = setup_inputs


def setup_inputs(seed=0):
    import zlib

    import numpy as np

    out = dict(_drawn_inputs(seed))
    spreads = {}
    factors = {'norm1_g': 2.701,
     'hgrn_lb_logits': 4.128,
     'hgrn_onorm_g': 7.458,
     'nsa_qn_g': 8.0,
     'nsa_kn_g': 8.0,
     'nsa_cmp_pos': 8.0,
     'fox_qn_g': 8.0,
     'fox_kn_g': 8.0,
     'fox_fb': 54.104,
     'ctx_2': 8.0,
     'c_ctx_2': 3.484,
     'b_ada_2': 5.036,
     'g_ffn1_2': 8.0,
     'g_mix_2': 8.0,
     'b_dw_2': 63.257,
     'ln_g_conv_2': 64.0,
     'ln_b_conv_2': 64.0,
     'b_pw_conv_2': 50.68,
     'g_qnorm_2': 8.0,
     'w_uq_2': 4.855,
     'g_kvnorm_2': 8.0,
     'b_fourier_2': 57.067,
     'b_bgate_2': 41.358,
     'g_ffn2_2': 8.0,
     'g_final_2': 7.745}
    for name, (base, spread) in spreads.items():
        noise = np.random.default_rng([zlib.crc32(name.encode()), seed]).standard_normal(out[name].shape)
        drawn = base * np.exp(spread * noise) if base else spread * noise
        out[name] = jnp.asarray(drawn.astype(out[name].dtype))
    for name, factor in factors.items():
        out[name] = (out[name] * factor).astype(out[name].dtype)
    return out
```

```python
from contextlib import ExitStack

import numpy as np

import concourse.bass as bass
from concourse import mybir

F32 = mybir.dt.float32
U32 = mybir.dt.uint32
ALU = mybir.AluOpType
ACT = mybir.ActivationFunctionType
AX_X = mybir.AxisListType.X

P = 128
D = 1024
KT = D // P
T = 256
TT = T // P
DEPTH = 2
EPS = 1e-6
NEG_BIG = -1e30
TINY = 1e-30
DH = 64
LN_SPLIT = 2.0 ** 60

N_CMP = 15
CMP_L = 32
HG_CHUNK = 64
HG_LEVELS = (32, 16, 8, 4, 2, 1)

FF1 = 4 * D // P
FF2 = 22
CONV_K = 31
PAD = CONV_K // 2
TP = T + 2 * PAD
CT = 3
QH = 8
NOPE = 64
ROPE = 32
QK = NOPE + ROPE
ATTN_SCALE = float(QK) ** -0.5
G4 = 4


class Product:

    def __init__(self, chunk, group, n, tiles):
        self.chunk, self.group, self.n, self.tiles, self.cpg = chunk, group, n, tiles, len(tiles)


class Segment:

    def __init__(self, pattern, chunk, times, at):
        self.pattern, self.chunk, self.times, self.at = pattern, chunk, times, at


class Group:

    def __init__(self, m, at, i, per):
        self.m, self.at, self.i, self.per = m, at, i, per


class Unit:

    def __init__(self, kind, tt, h=0, g=0, hh=0, tile0=0, first=True, last=True):
        self.kind, self.tt, self.h, self.g, self.hh, self.tile0 = kind, tt, h, g, hh, tile0
        self.first, self.last, self.lo = first, last, hh * DH


SLOTS = 8
SLOT_TILES = 11


def stream_plan():
    plan, chunk, group = {}, 0, 0
    order = []
    for l in range(DEPTH):
        order += [("in_t", l, 18, (8,)), ("in_a", l, 7, (8,)), ("cmp", l, 2, (8,) * 4), ("ada", l, 72, (8,)), ("wo", l, 8, (8,)),
                  ("up", l, FF1, (8,)), ("down", l, 8, (8,) * 4)]
    for l in range(DEPTH):
        order += [("ffn1", l, FF2, (8, 8)), ("ffn1_out", l, 8, (11, 11)),
                  ("conv_in", l, CT, (8, 8)), ("lat_in", l, 10, (8,)),
                  ("uq", l, QH, (3,)), ("uk", l, QH, (2,)), ("uv", l, 1, (8,)),
                  ("mrg_conv", l, 8, (11,)), ("mrg_four", l, 8, (4, 8)), ("mrg_mla", l, 8, (4, 8)),
                  ("mix_out", l, 8, (8,)), ("ffn2", l, FF2, (8, 8)), ("ffn2_out", l, 8, (11, 11))]
    for name, l, n, tiles in order:
        lin = name not in ("ada", "uv")
        plan[name, l] = Product(chunk, group, n, tiles)
        chunk += n * len(tiles)
        if lin:
            group += n
    return plan


PLAN = stream_plan()


def groups_per_turn(lin):
    per = SLOTS // lin.cpg
    return per if SLOTS % lin.cpg == 0 else None


def segments():
    out, seen, pos = [], {}, 0
    for lin in PLAN.values():
        pattern = lin.tiles if len(set(lin.tiles)) > 1 else lin.tiles[:1]
        times = lin.n * lin.cpg // len(pattern)
        if out and out[-1].pattern == pattern:
            out[-1].times += times
        else:
            out.append(Segment(pattern, pos, times, dict(seen)))
        for w in pattern:
            seen[w] = seen.get(w, 0) + times
        pos += times * len(pattern)
    return out, seen


SEGMENTS, WIDTHS = segments()

CONST_ALL = [("ident", P), ("ones_d", P)]
CONST_1 = [("blk64", P), ("rot", P), ("dup", 2 * P), ("rotdup", 2 * P), ("cos", T), ("sin", T),
           ("ccos", 2 * N_CMP), ("csin", 2 * N_CMP), ("causal", TT * T), ("cmask", TT * 2 * N_CMP),
           ("cneg", TT * 2 * N_CMP), ("tri", TT * T), ("gtk", TT * T), ("reset", 2 * T), ("lvl", 8 * P)]
CONST_2 = [("ones_ct", P), ("ones_kv", P), ("rot96", P), ("dft_c", 2 * P), ("dft_t", TT * 2 * T), ("mcos", T),
           ("msin", T)]


def columns(items):
    at, out = 0, {}
    for name, n in items:
        out[name] = (at, n)
        at += n
    return out, at


CONST_SETS = [columns(c) for c in (CONST_ALL, CONST_1, CONST_2)]
PARAM_L1 = [("norm1", 8), ("norm2", 8), ("onorm", 1), ("qkg", 10), ("pos", 2 * CMP_L), ("w2k", P), ("w2v", DH),
            ("kng", 1), ("fb", 4)]
PARAM_L2 = [("g1", 8), ("gm", 8), ("g2", 8), ("dw", CT * CONV_K), ("bdw", CT), ("lng", CT), ("lnb", CT),
            ("bpw", 8), ("gq", 3), ("gkv", 2), ("bfour", 8), ("bbg", 24)]
PARAM_ALL = [("lb", 4), ("cvec", 16), ("gfin", 8), ("bada", 72 * DEPTH)]
PARAM_SETS = [columns(PARAM_ALL), columns([(f"{n}@{l}", c) for l in range(DEPTH) for n, c in PARAM_L1]),
              columns([(f"{n}@@{l}", c) for l in range(DEPTH) for n, c in PARAM_L2])]


def shape_constants():
    c = {}
    i = np.arange(P)
    eye = np.eye(P)
    c["ident"] = eye
    c["ones_d"] = np.full((P, P), 1.0 / D)
    c["ones_ct"] = np.full((P, P), 1.0 / (CT * P))
    c["ones_kv"] = np.full((P, P), 1.0 / 256)
    c["blk64"] = (i[:, None] // DH == i[None, :] // DH) / float(DH)
    rot = np.zeros((P, P))
    for b in (0, DH):
        for d in range(8):
            rot[b + 8 + d, b + d] = -1.0
            rot[b + d, b + 8 + d] = 1.0
    c["rot"] = rot
    dup = np.zeros((P, 2, P))
    for g in range(2):
        for h in range(2):
            dup[g * DH + np.arange(DH), g, h * DH + np.arange(DH)] = 1.0
    c["dup"] = dup
    c["rotdup"] = np.stack([rot @ dup[:, g] for g in range(2)], 1)
    inv = np.float32(500000.0) ** (-np.arange(0, 16, 2, dtype=np.float32) / np.float32(16))

    def rope(pos):
        ang = (pos.astype(np.float32)[None, :] * inv[:, None]).astype(np.float32)
        cs, sn = np.ones((P, len(pos))), np.zeros((P, len(pos)))
        for b in (0, 8, DH, DH + 8):
            cs[b:b + 8], sn[b:b + 8] = np.cos(ang), np.sin(ang)
        return cs, sn

    c["cos"], c["sin"] = rope(np.arange(T))
    cc, cs = rope(np.arange(N_CMP) * 16 + 31)
    c["ccos"], c["csin"] = np.tile(cc, (1, 2)), np.tile(cs, (1, 2))
    q = np.arange(T).reshape(TT, P)
    k = np.arange(T)
    c["causal"] = np.where(k[None, None] <= q.T[:, :, None], 0.0, NEG_BIG)
    end = np.arange(N_CMP) * 16 + 31
    seen = (end[None, None] <= q.T[:, :, None])
    c["cmask"] = np.tile(seen[:, :, None, :], (1, 1, 2, 1)).astype(float)
    c["cneg"] = np.where(np.tile(seen[:, :, None, :], (1, 1, 2, 1)), 0.0, NEG_BIG)
    c["tri"] = (q.T[:, :, None] <= k[None, None]).astype(float)
    c["gtk"] = (q.T[:, :, None] > k[None, None]).astype(float)
    c["reset"] = np.tile((np.arange(2 * T) % HG_CHUNK != 0).astype(float), (P, 1))
    lv = np.zeros((P, 8, P))
    for n, L in enumerate(HG_LEVELS + (64,)):
        s, t = i[:, None], i[None, :]
        lv[:, n] = (s // (2 * L) == t // (2 * L)) & (s // L % 2 == 0) & (t // L % 2 == 1)
    lv[:, 7] = eye
    c["lvl"] = lv
    a = 2 * np.pi * np.outer(i, i) / P
    c["dft_c"] = np.concatenate([np.cos(a), np.sin(a)], 1)
    a = 2 * np.pi * np.outer(k, k) % (2 * np.pi * T) / T
    n = 1.0 / np.sqrt(float(T * P))
    a = np.stack([np.cos(a) * n, -np.sin(a) * n], 1).reshape(TT, P, 2, T)
    c["dft_t"] = a.transpose(1, 0, 2, 3)
    r96 = np.zeros((P, P))
    for ax in (NOPE, NOPE + 16):
        for d in range(8):
            r96[ax + 8 + d, ax + d] = -1.0
            r96[ax + d, ax + 8 + d] = 1.0
    c["rot96"] = r96
    inv = 1.0 / (np.float32(10000.0) ** (np.arange(8, dtype=np.float32) * 2.0 / 16))
    row, col = np.repeat(np.arange(T // 64), 64), np.tile(np.arange(64), T // 64)
    ang = np.concatenate([row[None] * inv[:, None]] * 2 + [col[None] * inv[:, None]] * 2, 0).astype(np.float32)
    mc, ms = np.ones((P, T)), np.zeros((P, T))
    mc[NOPE:QK], ms[NOPE:QK] = np.cos(ang), np.sin(ang)
    c["mcos"], c["msin"] = mc, ms
    packed = []
    for at_of, width in CONST_SETS:
        out = np.zeros((P, width), np.float32)
        for name, (at, n) in at_of.items():
            out[:, at:at + n] = c[name].reshape(P, n)
        packed.append(out)
    return packed


def chan(v):
    return v.reshape(-1, P).T


def pack_params(a):
    rows = {}

    def rep(v):
        return np.tile(v.reshape(1, -1), (P, 1))

    lb = a["hgrn_lb_logits"]
    rows["lb"] = np.concatenate([chan(lb[0]), chan(lb[1])], 1)
    rows["cvec"] = np.stack([chan(a["c_2"][0]), chan(a["c_ctx_2"])], 2)
    rows["bada"] = np.concatenate([chan(a["b_ada_2"][l]) for l in range(DEPTH)], 1)
    rows["gfin"] = chan(a["g_final_2"])
    for l in range(DEPTH):
        twice = lambda v: np.tile(v.reshape(-1, 1), (2, 1))
        qn, kn = twice(a["nsa_qn_g"][l]), twice(a["nsa_kn_g"][l])
        fq, fk = twice(a["fox_qn_g"][l]), twice(a["fox_kn_g"][l])
        r = {"norm1": chan(a["norm1_g"][l]), "norm2": chan(a["norm2_g"][l]), "onorm": twice(a["hgrn_onorm_g"][l]),
             "qkg": np.concatenate([kn, kn, qn, qn, qn, qn, fq, fq, fk, fk], 1),
             "pos": np.tile(a["nsa_cmp_pos"][l].transpose(2, 0, 1).reshape(DH, -1), (2, 1)),
             "w2k": np.concatenate([a["nsa_cmp_w2"][l, 0]] * 2, 1), "w2v": a["nsa_cmp_w2"][l, 1],
             "kng": kn, "fb": rep(a["fox_fb"][l])}
        rows.update({f"{n}@{l}": v for n, v in r.items()})
        r = {"g1": chan(a["g_ffn1_2"][l]), "gm": chan(a["g_mix_2"][l]),
             "g2": chan(a["g_ffn2_2"][l]),
             "dw": a["w_dw_2"][l].T.reshape(CT, P, CONV_K).transpose(1, 0, 2),
             "bdw": chan(a["b_dw_2"][l]), "lng": chan(a["ln_g_conv_2"][l]), "lnb": chan(a["ln_b_conv_2"][l]),
             "bpw": chan(a["b_pw_conv_2"][l]), "gq": chan(a["g_qnorm_2"][l]), "gkv": chan(a["g_kvnorm_2"][l]),
             "bfour": chan(a["b_fourier_2"][l]), "bbg": chan(a["b_bgate_2"][l])}
        rows.update({f"{n}@@{l}": v for n, v in r.items()})
    packed = []
    for at_of, width in PARAM_SETS:
        out = np.zeros((P, width), np.float32)
        for name, (at, n) in at_of.items():
            out[:, at:at + n] = rows[name].reshape(P, n)
        packed.append(out)
    return packed


def tiles(w):
    k, n = w.shape
    m = -(-n // P)
    if n % P:
        w = np.concatenate([w, np.zeros((k, m * P - n), w.dtype)], 1)
    return w.reshape(k // P, P, m, P).transpose(2, 1, 0, 3)


def place(w, at):
    out = np.zeros((w.shape[0], P), w.dtype)
    out[:, at:at + w.shape[1]] = w
    return out


def pack_stream(a):
    out = {w: [] for w in WIDTHS}

    def put(t):
        t = np.ascontiguousarray(t)
        out[t.shape[1]].append(t.reshape(P, -1))

    def halves(t, w):
        for m in range(t.shape[0]):
            for c in range(0, t.shape[2], w):
                put(t[m][:, c:c + w])

    for l in range(DEPTH):
        w = a["w_in"][l]
        for lo, hi in ((256, 512), (0, 256), (1792, 1920), (2048, 2176), (1024, 1536), (2328, 2840),
                       (1536, 1792), (768, 1024)):
            halves(tiles(w[:, lo:hi]), 8)
        halves(tiles(np.concatenate([w[:, 2304:2328], w[:, 3096:3100]], 1)), 8)
        for lo, hi in ((512, 768), (1920, 2048), (2176, 2304), (2840, 3096)):
            halves(tiles(w[:, lo:hi]), 8)
        for which in range(2):
            t = a["nsa_cmp_w1"][l, which].reshape(CMP_L, DH, P).transpose(1, 0, 2)
            t = np.concatenate([t, t], 0)
            for c in range(4):
                put(t[:, 8 * c:8 * c + 8])
        halves(tiles(a["w_ada_2"][l]), 8)
        halves(tiles(a["w_o"][l]), 8)
        halves(tiles(a["w_up"][l]), 8)
        halves(tiles(a["w_down"][l]), 8)

    def pairs(x, y):
        for m in range(x.shape[0]):
            put(x[m])
            put(y[m])

    for l in range(DEPTH):
        pairs(tiles(a["w1_ffn1_2"][l]), tiles(a["w3_ffn1_2"][l]))
        halves(tiles(a["w2_ffn1_2"][l]), 11)
        w = a["w_in_2"][l]
        pairs(tiles(w[:, 0:384]), tiles(w[:, 384:768]))
        halves(tiles(w[:, 1152:1408]), 8)
        halves(tiles(place(w[:, 1408:1440], NOPE)), 8)
        halves(tiles(w[:, 768:1152]), 8)
        halves(tiles(w[:, 1440:1952]), 8)
        uq = a["w_uq_2"][l].reshape(384, QH, QK)
        ukv = a["w_ukv_2"][l].reshape(256, QH, NOPE + 64)
        for h in range(QH):
            halves(tiles(place(uq[:, h], 0)), 3)
        for h in range(QH):
            halves(tiles(place(ukv[:, h, :NOPE], 0)), 2)
        v = ukv[:, :, NOPE:].reshape(2, P, 4, P).transpose(1, 0, 2, 3)
        put(v.reshape(P, 8, P))
        gate = tiles(a["w_bgate_2"][l])
        pw, four, om = (tiles(a[n][l]) for n in ("w_pw_conv_2", "w_fourier_2", "w_o_mla_2"))
        for m in range(8):
            put(np.concatenate([pw[m], gate[m]], 1))
        pairs(four, gate[16:24])
        pairs(om, gate[8:16])
        halves(tiles(a["w_out_2"][l]), 8)
        pairs(tiles(a["w1_ffn2_2"][l]), tiles(a["w3_ffn2_2"][l]))
        halves(tiles(a["w2_ffn2_2"][l]), 11)
    return {w: np.stack(c) for w, c in out.items()}


def channel_major(x):
    return np.ascontiguousarray(x.T.reshape(-1, P, x.shape[0]).transpose(1, 0, 2))


class Semaphores:

    def __init__(self, sem):
        self.consts = sem("consts")
        self.consts2 = sem("consts2")
        self.x_in = sem("x_in")
        self.ctx_in = sem("ctx_in")
        self.squares = sem("squares")
        self.mean_sq = sem("mean_sq")
        self.rstd = sem("rstd")
        self.normed = sem("normed")
        self.hn_sq = sem("hn_sq")
        self.hn_ms = sem("hn_ms")
        self.hn_ln = sem("hn_ln")
        self.hn_rs = sem("hn_rs")
        self.qkn = sem("qkn")
        self.rotated = sem("rotated")
        self.rope = sem("rope")
        self.sig = sem("sig")
        self.lb = sem("lb")
        self.fa = sem("fa")
        self.fox_in = sem("fox_in")
        self.fox_e = sem("fox_e")
        self.hg_f = sem("hg_f")
        self.hg_ln = sem("hg_ln")
        self.hg_g = sem("hg_g")
        self.hg_e = sem("hg_e")
        self.hg_qk = sem("hg_qk")
        self.hg_x = sem("hg_x")
        self.hg_sc = sem("hg_sc")
        self.hg_o = sem("hg_o")
        self.hg_osq = sem("hg_osq")
        self.hg_oms = sem("hg_oms")
        self.hg_ors = sem("hg_ors")
        self.mixa = sem("mixa")
        self.zeroed = sem("zeroed")
        self.cleared = sem("cleared")
        self.blocks = sem("blocks")
        self.cmp_raw = sem("cmp_raw")
        self.kc_sq = sem("kc_sq")
        self.kc_ms = sem("kc_ms")
        self.kc_rs = sem("kc_rs")
        self.kc_n = sem("kc_n")
        self.kc_rot = sem("kc_rot")
        self.kc_done = sem("kc_done")
        self.vc_done = sem("vc_done")
        self.att_s = sem("att_s")
        self.att_m = sem("att_m")
        self.att_e = sem("att_e")
        self.att_p = sem("att_p")
        self.att_t = sem("att_t")
        self.att_c = sem("att_c")
        self.att_v = sem("att_v")
        self.att_o = sem("att_o")
        self.stored = sem("stored")
        self.csilu = sem("csilu")
        self.cv_in = sem("cv_in")
        self.cv_done = sem("cv_done")
        self.ln_ms = sem("ln_ms")
        self.ln_cen = sem("ln_cen")
        self.ln_sq = sem("ln_sq")
        self.ln_rs = sem("ln_rs")
        self.ln_n = sem("ln_n")
        self.ln_out = sem("ln_out")
        self.c_sq = sem("c_sq")
        self.c_ms = sem("c_ms")
        self.c_rs = sem("c_rs")
        self.c_n = sem("c_n")
        self.q_rot = sem("q_rot")
        self.q_done = sem("q_done")
        self.kr_rot = sem("kr_rot")
        self.kr_done = sem("kr_done")
        self.v_done = sem("v_done")
        self.f_mm = sem("f_mm")
        self.f_sb = sem("f_sb")
        self.sig_g = sem("sig_g")
        self.silu = sem("silu")
        self.padded = sem("padded")
        self.final = sem("final")
        self.ada_row = sem("ada_row")
        self.ada_t = sem("ada_t")
        self.ada_out = sem("ada_out")


def kernel_program(nc, streams, consts, params, x_cm, ctx_cm, out_cm, blocks=(1, 2)):
    with ExitStack() as stack:
        def sb(name, shape, dt=F32):
            return stack.enter_context(nc.sbuf_tensor(name, shape, dt))

        def sem(name):
            return stack.enter_context(nc.semaphore(name))

        ring = sb("ring", [P, SLOTS, SLOT_TILES * P])
        res = sb("res", [P, KT, 2 * T])
        hn = sb("hn", [P, KT, 2 * T])
        hid = sb("hid", [P, FF2 * 2 * T])
        work = sb("work", [P, 16052])
        con0 = sb("con0", [P, CONST_SETS[0][1]])
        con12 = sb("con12", [P, max(CONST_SETS[1][1], CONST_SETS[2][1])])
        par0 = sb("par0", [P, PARAM_SETS[0][1]])
        par12 = sb("par12", [P, max(PARAM_SETS[1][1], PARAM_SETS[2][1])])
        mods = sb("mods", [P, DEPTH, 2 * 72])
        conds = sb("conds", [P, 16])
        small = sb("small", [P, 404])
        bank = [stack.enter_context(nc.psum_tensor(f"bank{b}", [P, 512], F32)) for b in range(8)]

        def carve(buffer, sizes):
            at, out = 0, []
            for n in sizes:
                out.append(buffer[:, at:at + n])
                at += n
            return out

        def const(k, name, **dims):
            at, n = CONST_SETS[k][0][name]
            v = (con0 if k == 0 else con12)[:, at:at + n]
            return v

        def param(name):
            k = 2 if "@@" in name else 1 if "@" in name else 0
            at, n = PARAM_SETS[k][0][name]
            return (par12 if k else par0)[:, at:at + n]

        limit = sum(x.n * x.cpg for x in PLAN.values()) if 2 in blocks else PLAN["ffn1", 0].chunk
        ident, ones_d = const(0, "ident"), const(0, "ones_d")
        blk64, rot = const(1, "blk64"), const(1, "rot")
        dup = const(1, "dup").rearrange("p (g m) -> p g m", g=2)
        rotdup = const(1, "rotdup").rearrange("p (g m) -> p g m", g=2)
        cos, sin = const(1, "cos"), const(1, "sin")
        causal = const(1, "causal").rearrange("p (t k) -> p t k", t=TT)
        cmask = const(1, "cmask").rearrange("p (t k) -> p t k", t=TT)
        cneg = const(1, "cneg").rearrange("p (t k) -> p t k", t=TT)
        tri = const(1, "tri").rearrange("p (t k) -> p t k", t=TT)
        gtk = const(1, "gtk").rearrange("p (t k) -> p t k", t=TT)
        lvl_u = const(1, "lvl").bitcast(U32).rearrange("p (n t) -> p n t", n=8)
        dft_c = const(2, "dft_c")
        dft_t = const(2, "dft_t").rearrange("p (t c k) -> p t c k", t=TT, c=2)

        HT = 2 * T
        proj_b, qkn_b, sq_b, sc_b, sc2_b = carve(hid, [18 * T, 10 * T, 10 * T, 4 * T, 2 * T])
        proj = proj_b.rearrange("p (m t) -> p m t", t=T)
        qkn = qkn_b.rearrange("p (m t) -> p m t", t=T)
        sqh = sq_b.rearrange("p (m t) -> p m t", t=T)
        scores_hg = sc_b.rearrange("p (h b t) -> p h b t", h=2, b=4)
        scores_far = sc2_b.rearrange("p (h b t) -> p h b t", h=2, b=2)
        hid1 = hid[:, 0:FF1 * T].rearrange("p (m t) -> p m t", t=T)
        hid2 = hid[:, :].rearrange("p (m t) -> p m t", t=HT)
        qr = sqh[:, 0:4, :]
        kd = sq_b[:, 4 * T:8 * T].rearrange("p (g s t) -> p g s t", g=2, s=2)
        (sm_b, pr_b, pt_b, rstd, lnb, vtok_b, bc_b, sg, kc, gg, ee, qk, q8, sga, fa_b, mix_b, ada_row) = carve(
            work, [1024, 1024, 1024, 512, 512, 1792, 1920, 512, 512, 512, 512, 512, 512, 512, 2048, 2048, 512])
        sm = sm_b.rearrange("p (u k) -> p u k", u=2)
        pr = pr_b.rearrange("p (u k) -> p u k", u=2)
        pt = pt_b.rearrange("p (u k) -> p u k", u=2)
        vtok = vtok_b.rearrange("p (t c) -> p t c", t=TT)
        bc = bc_b.rearrange("p (w l g n) -> p w l g n", w=2, l=CMP_L, g=2)
        fa = fa_b.rearrange("p (s h q) -> p s h q", s=TT, h=4)
        mixt = mix_b.rearrange("p (m t) -> p m t", t=T)
        (mx, negmx, smu, rcp, lb, lb_t, lb_u, gate_b, lf, lx, ly, lz, qkg, hk, hv, kcn, kcb, krot, vc_b, eps_col,
         one_col) = carve(small, [4, 4, 4, 4, 4, 4, 4, 48, 8, 8, 8, 8, 10, 30, 30, 30, 30, 30, 128, 1, 1])
        gate = gate_b.rearrange("p (t c) -> p t c", t=TT)
        vc = vc_b.rearrange("p (g d) -> p g d", g=2)

        z = hid[:, 0:10 * HT].rearrange("p (m t) -> p m t", t=HT)
        q2 = hid[:, 10 * HT:18 * HT].rearrange("p (h t) -> p h t", t=HT)
        cvo = hid[:, 18 * HT:21 * HT].rearrange("p (m t) -> p m t", t=HT)
        att = z[:, 0:4, :]
        four = z[:, 6:10, :]
        (sm2_b, pr2_b, pt2_b, rstd2, lnb2, k2_b, v2_b, f1_b, cvp_b) = carve(
            work, [1024, 1024, 1024, 512, 512, 4096, 2048, 4096, CT * 2 * TP])
        k2 = k2_b.rearrange("p (h t) -> p h t", t=HT)
        v2 = v2_b.rearrange("p (t c) -> p t c", t=4)
        f1 = f1_b.rearrange("p (s t g c) -> p s t g c", s=2, t=TT, g=G4)
        mrg = f1_b.rearrange("p (m t) -> p m t", t=HT)
        cvp = cvp_b.rearrange("p (m s t) -> p m s t", m=CT, s=2)

        landed = [sem(f"landed{s}") for s in range(SLOTS)]
        used = [sem(f"used{s}") for s in range(SLOTS)]
        drained = [sem(f"drained{p}") for p in range(2)]
        s = Semaphores(sem)

        def turns(eng, lin):
            per = SLOTS // lin.cpg if SLOTS % lin.cpg == 0 else lin.n
            first = per if lin.chunk < SLOTS else 0
            if (lin.n - first) // per < 2 or per % 2:
                for m in range(lin.n):
                    yield Group(m, m, 0, per)
                return
            for m in range(first):
                yield Group(m, m, 0, per)
            end = lin.n // per
            with eng.Fori(first // per, end) as i:
                for j in range(per):
                    yield Group(i * per + j, j, i, per)
            for m in range(end * per, lin.n):
                yield Group(m, m, 0, per)

        def slot_of(lin, g, c):
            return (lin.chunk + g.at * lin.cpg + c) % SLOTS

        def turn_of(lin, g, c):
            return (lin.chunk + g.at * lin.cpg + c) // SLOTS + g.i * (g.per * lin.cpg // SLOTS)

        def wait_weights(pe, lin, g, c):
            pe.wait_ge(landed[slot_of(lin, g, c)], (turn_of(lin, g, c) + 1) * 16)

        def parity(lin, g):
            return (lin.group + g.at) % 2

        def wait_banks(pe, lin, g):
            before = (lin.group + g.at) // 2 + g.i * (g.per // 2)
            if not (isinstance(before, int) and before == 0):
                pe.wait_ge(drained[parity(lin, g)], before)

        def wait_products(eng, lin, g):
            c = lin.cpg - 1
            eng.wait_ge(used[slot_of(lin, g, c)], turn_of(lin, g, c) + 1)

        def wait_drained(eng, lin, m):
            n = lin.group + m
            eng.wait_ge(drained[n % 2], n // 2 + 1)

        def wait_all_drained(eng, lin):
            for m in range(max(lin.n - 2, 0), lin.n):
                wait_drained(eng, lin, m)

        cs = conds[:, :].rearrange("p (k c) -> p k c", c=2)
        ADA_QUADS = 72 // 4

        def modulation(l):
            return mods[:, l, :].rearrange("p (n k c) -> p n k c", n=9, k=8)

        def ada_bank(l, q):
            return bank[1 + 2 * ((ADA_QUADS * l + q) % 2)]

        def ada_pe(pe, l, step):
            lin = PLAN["ada", l]
            for m in range(2 * step, min(2 * step + 2, lin.n)):
                g, q = Group(m, m, 0, lin.n), m // 4
                if m % 4 == 0 and ADA_QUADS * l + q >= 2:
                    pe.wait_ge(s.ada_out, ADA_QUADS * l + q - 1)
                wait_weights(pe, lin, g, 0)
                for k in range(KT):
                    mm = pe.matmul(ada_bank(l, q)[0:2, (m % 4) * P:(m % 4 + 1) * P], cs[:, k, :],
                                   ring[:, slot_of(lin, g, 0), k * P:(k + 1) * P], start=(k == 0), stop=(k == KT - 1))
                mm.then_inc(used[slot_of(lin, g, 0)], 1)
            q = (step - 3) // 2
            if step % 2 == 1 and 0 <= q < ADA_QUADS:
                pe.wait_ge(s.ada_row, ADA_QUADS * l + q + 1)
                for j in range(4):
                    mm = pe.transpose(ada_bank(l, q)[:, 2 * j:2 * j + 2], ada_row[0:2, j * P:(j + 1) * P], ident[0:2, 0:2])
                mm.then_inc(s.ada_t, 1)

        def ada_act(act, l, step):
            q = (step - 2) // 2
            if step % 2 == 0 and 0 <= q < ADA_QUADS:
                lin = PLAN["ada", l]
                wait_products(act, lin, Group(4 * q + 3, 4 * q + 3, 0, lin.n))
                if ADA_QUADS * l + q >= 1:
                    act.wait_ge(s.ada_t, ADA_QUADS * l + q)
                act.activation(ada_row[0:2, :], ada_bank(l, q)[0:2, :], ACT.Copy).then_inc(s.ada_row, 1)

        def ada_dve(dve, l, step):
            q = (step - 4) // 2
            if step % 2 == 0 and 0 <= q < ADA_QUADS:
                dve.wait_ge(s.ada_t, ADA_QUADS * l + q + 1)
                c0 = 72 * l + 4 * q
                dve.tensor_tensor(mods[:, l, 8 * q:8 * q + 8].rearrange("p (m c) -> p m c", c=2),
                                  ada_bank(l, q)[:, 0:8].rearrange("p (m c) -> p m c", c=2),
                                  param("bada")[:, c0:c0 + 4].unsqueeze(2).broadcast_to([P, 4, 2]),
                                  ALU.add).then_inc(s.ada_out, 1)

        LAST_NORM = 5 * DEPTH
        OUT_LINS = [(a, l) for l in range(DEPTH) for a in ("wo", "down")] + [
            (a, l) for l in range(DEPTH) for a in ("ffn1_out", "mix_out", "ffn2_out")]

        def norm_width(n):
            return T if n < 2 * DEPTH or n >= LAST_NORM - 1 else 2 * T

        def norm_act(act, n):
            w = norm_width(n)
            if n == 0:
                act.wait_ge(s.x_in, 16)
            if n == 2 * DEPTH:
                act.wait_ge(s.ctx_in, 16)
            for k in range(KT):
                if n >= 1:
                    wait_drained(act, PLAN[OUT_LINS[n - 1]], k)
                act.activation(hn[:, k, 0:w], res[:, k, 0:w], ACT.Square).then_inc(s.squares, 1)
            act.wait_ge(s.mean_sq, n + 1)
            act.activation(lnb[:, 0:w], bank[7][:, 0:w], ACT.Ln, bias=eps_col)
            act.drain()
            act.activation(rstd[:, 0:w], lnb[:, 0:w], ACT.Exp, scale=-0.5).then_inc(s.rstd, 1)

        def norm_pe(pe, n):
            w = norm_width(n)
            for k in range(KT):
                pe.wait_ge(s.squares, KT * n + k + 1)
                mm = pe.matmul(bank[7][:, 0:w], ones_d, hn[:, k, 0:w], start=(k == 0), stop=(k == KT - 1))
            mm.then_inc(s.mean_sq, 1)

        def wait_normed(pe, n, k):
            pe.wait_ge(s.normed, KT * n + k + 1)

        def units_block1(l):
            out = []
            for tt in range(TT):
                for g in range(2):
                    for hh in range(2):
                        tile0 = 2 * g
                        for kind in ("cmp", "slc", "win"):
                            out.append(Unit(kind, tt, g=g, hh=hh, tile0=tile0,
                                                       first=kind == "cmp", last=kind == "win"))
                for hh in range(2):
                    out.append(Unit("fox", tt, hh=hh))
            base, obase = l * len(out), l * sum(x.last for x in out)
            o = 0
            for n, x in enumerate(out):
                x.u, x.o, x.l = base + n, obase + o, l
                x.keys = N_CMP if x.kind == "cmp" else T
                o += x.last
            return out

        N_UNITS1 = DEPTH * len(units_block1(0))
        N_OUTS1 = DEPTH * sum(x.last for x in units_block1(0))

        def scores(x):
            return bank[4 + x.u % 2]

        def head_cols(x):
            return slice(x.lo, x.lo + DH)

        def unit_scores(pe, x):
            if x.u >= 2:
                pe.wait_ge(s.att_m, x.u - 1)
            q0 = x.tt * P
            rows = slice(x.lo, x.lo + DH)
            for j in range(2):
                if x.kind == "mla":
                    pass
                dst = scores(x)[:, j * x.keys:(j + 1) * x.keys]
                if x.kind == "fox":
                    mm = pe.matmul(dst, qkn[rows, 6 + j, q0:q0 + P], qkn[rows, 8 + j, :], start=True, stop=False)
                    for st in range(TT):
                        mm = pe.matmul(dst, fa[:, st, 2 * j + x.hh, q0:q0 + P], gtk[:, st, :],
                                       start=False, stop=(st == TT - 1))
                else:
                    key = kcb[rows, x.g * N_CMP:(x.g + 1) * N_CMP] if x.kind == "cmp" else \
                        kd[rows, x.g, 0 if x.kind == "slc" else 1, :]
                    mm = pe.matmul(dst, qr[rows, x.tile0 + j, q0:q0 + P], key, start=True, stop=True)
            mm.then_inc(s.att_s, 1)

        def unit_turn(pe, x):
            pe.wait_ge(s.att_p, x.u + 1)
            if x.u >= 1:
                pe.wait_ge(s.att_c, x.u)
            kt = 1 if x.kind == "cmp" else TT
            kw = min(x.keys, P)
            for j in range(2):
                for k in range(kt):
                    mm = pe.transpose(bank[6][0:kw, (j * kt + k) * P:(j * kt + k + 1) * P],
                                      pr[:, x.u % 2, j * x.keys + k * P:j * x.keys + k * P + kw], ident)
            mm.then_inc(s.att_t, 1)

        VCOL = {"slc": 384, "win": 512, "fox": 640}

        def unit_values(pe, x):
            pe.wait_ge(s.att_c, x.u + 1)
            if x.first and x.o >= 2:
                pe.wait_ge(s.att_o, x.o - 1)
            kt = 1 if x.kind == "cmp" else TT
            for j in range(2):
                dst = bank[7][head_cols(x), j * P:(j + 1) * P]
                for k in range(kt):
                    if x.kind == "cmp":
                        v, p_t = vc[0:N_CMP, x.g, :], pt[0:N_CMP, x.u % 2, j * P:(j + 1) * P]
                    else:
                        head = 2 * j + x.hh if x.kind == "fox" else x.g
                        c0 = VCOL[x.kind] + head * DH
                        v, p_t = vtok[:, k, c0:c0 + DH], pt[:, x.u % 2, (j * kt + k) * P:(j * kt + k + 1) * P]
                    mm = pe.matmul(dst, v, p_t, start=(x.first and j == 0 and k == 0),
                                   stop=(x.last and k == kt - 1), skip_group_check=True)
            mm.then_inc(s.att_v, 1)

        def attention_pe(pe, l, units):
            for n in range(len(units) + 2):
                ada_pe(pe, l, n)
                if n < len(units):
                    unit_scores(pe, units[n])
                if 1 <= n <= len(units):
                    unit_turn(pe, units[n - 1])
                if n >= 2:
                    unit_values(pe, units[n - 2])

        def unit_mask(dve, x):
            dve.wait_ge(s.att_s, x.u + 1)
            if x.u >= 2:
                dve.wait_ge(s.att_e, x.u - 1)
            n = 2 * x.keys
            src = scores(x)[:, 0:n].rearrange("p (j k) -> p j k", j=2)
            dst = sm[:, x.u % 2, 0:n].rearrange("p (j k) -> p j k", j=2)
            if x.kind == "cmp":
                add = cneg[:, x.tt, :].rearrange("p (j k) -> p j k", j=2)
            else:
                add = causal[:, x.tt, :].unsqueeze(1).broadcast_to([P, 2, T])
            dve.scalar_tensor_tensor(out=dst, in0=src, scalar=1.0 if x.kind == "fox" else DH ** -0.5, in1=add,
                                     op0=ALU.mult, op1=ALU.add)
            dve.drain()
            dve.tensor_reduce(mx[:, 2 * (x.u % 2):2 * (x.u % 2) + 2], dst, AX_X, ALU.max)
            dve.drain()
            dve.tensor_scalar(negmx[:, 2 * (x.u % 2):2 * (x.u % 2) + 2], mx[:, 2 * (x.u % 2):2 * (x.u % 2) + 2],
                              -1.0, None, ALU.mult).then_inc(s.att_m, 1)

        def unit_norm(dve, x):
            dve.wait_ge(s.att_e, x.u + 1)
            if x.u == 0:
                pass
            at = 2 * (x.u % 2)
            n = 2 * x.keys
            p_u = pr[:, x.u % 2, 0:n].rearrange("p (j k) -> p j k", j=2)
            if x.kind == "cmp":
                dve.tensor_tensor(p_u, p_u, cmask[:, x.tt, :].rearrange("p (j k) -> p j k", j=2), ALU.mult)
                dve.drain()
                dve.tensor_reduce(smu[:, at:at + 2], p_u, AX_X, ALU.add)
                dve.drain()
            dve.tensor_scalar(smu[:, at:at + 2], smu[:, at:at + 2], TINY, None, ALU.max)
            dve.drain()
            dve.reciprocal(rcp[:, at:at + 2], smu[:, at:at + 2])
            dve.drain()
            if x.kind != "fox":
                br = ("cmp", "slc", "win").index(x.kind)
                c0 = br * 8 + 4 * x.g + x.hh
                dve.tensor_tensor(rcp[:, at:at + 2], rcp[:, at:at + 2], gate[:, x.tt, c0:c0 + 3:2], ALU.mult)
                dve.drain()
            for j in range(2):
                last = dve.tensor_scalar(pr[:, x.u % 2, j * x.keys:(j + 1) * x.keys],
                                         pr[:, x.u % 2, j * x.keys:(j + 1) * x.keys],
                                         rcp[:, at + j:at + j + 1], None, ALU.mult)
            last.then_inc(s.att_p, 1)

        def attention_dve(dve, l, units):
            for n in range(len(units) + 2):
                ada_dve(dve, l, n)
                if n < len(units):
                    unit_mask(dve, units[n])
                if 1 <= n <= len(units):
                    unit_norm(dve, units[n - 1])

        def unit_exp(act, x):
            act.wait_ge(s.att_m, x.u + 1)
            if x.u >= 2:
                act.wait_ge(s.att_t, x.u - 1)
            at = 2 * (x.u % 2)
            for j in range(2):
                last = act.activation(pr[:, x.u % 2, j * x.keys:(j + 1) * x.keys],
                                      sm[:, x.u % 2, j * x.keys:(j + 1) * x.keys], ACT.Exp,
                                      bias=negmx[:, at + j:at + j + 1], accum_out=smu[:, at + j:at + j + 1])
            last.then_inc(s.att_e, 1)

        def unit_copy(act, x):
            act.wait_ge(s.att_t, x.u + 1)
            if x.u >= 2:
                act.wait_ge(s.att_v, x.u - 1)
            kw = min(x.keys, P)
            n = 2 * P if x.kind == "cmp" else 4 * P
            act.activation(pt[0:kw, x.u % 2, 0:n], bank[6][0:kw, 0:n], ACT.Copy).then_inc(s.att_c, 1)

        def unit_out(act, x):
            if not x.last:
                return
            act.wait_ge(s.att_v, x.u + 1)
            t0 = x.tt * P
            m0 = 6 if x.kind == "fox" else 2 + x.tile0
            act.activation(mixt[head_cols(x), m0:m0 + 2, t0:t0 + P],
                           bank[7][head_cols(x), 0:2 * P].rearrange("p (j q) -> p j q", j=2),
                           ACT.Copy).then_inc(s.att_o, 1)

        def attention_act(act, l, units):
            for n in range(len(units) + 2):
                ada_act(act, l, n)
                if n < len(units):
                    unit_exp(act, units[n])
                if 1 <= n <= len(units):
                    unit_copy(act, units[n - 1])
                if n >= 2:
                    unit_out(act, units[n - 2])

        NL = len(HG_LEVELS)
        HG_STEPS = NL + 3

        MIX_STEPS = len(units_block1(0)) + 2

        def hg_banks(l, n):
            u = l * HG_STEPS + n
            return u, bank[4 + 2 * (u % 2)], bank[5 + 2 * (u % 2)]

        def hg_decayed(l, n):
            return l * (HG_STEPS - 1) + (n if n < NL + 1 else n - 1)

        def hg_pe(pe, l):
            for n in range(HG_STEPS):
                u, b0, b1 = hg_banks(l, n)
                if n != NL + 1:
                    pe.wait_ge(s.hg_qk, hg_decayed(l, n) + 1)
                if n >= 2:
                    pe.wait_ge(s.hg_sc, u - 1)
                far, diag = n == NL + 2, n == NL + 1
                for hh, b in enumerate((b0, b1)):
                    rows = slice(hh * DH, hh * DH + DH)
                    for kt in range(2):
                        for tt in range(1 if far else TT):
                            k0 = kt * T + tt * P
                            keys = (kc if diag else qk)[rows, k0:k0 + P]
                            q0 = k0 + P if far else k0
                            queries = (q8 if diag else qk)[rows, q0:q0 + P]
                            c0 = kt * P if far else (kt * 2 + tt) * P
                            mm = pe.matmul(b[:, c0:c0 + P], keys, queries, start=True, stop=True)
                mm.then_inc(s.hg_x, 1)
                ada_pe(pe, l, MIX_STEPS + n)
            pe.wait_ge(s.hg_sc, (l + 1) * HG_STEPS)
            u, b0, b1 = hg_banks(l, 0)
            for kt in range(2):
                for hh in range(2):
                    rows, c0 = slice(hh * DH, hh * DH + DH), 128 + (2 * kt + hh) * DH
                    for tt in range(TT):
                        dst = bank[4][rows, kt * T + tt * P:kt * T + (tt + 1) * P]
                        pe.matmul(dst, vtok[:, tt, c0:c0 + DH], scores_hg[:, hh, kt * 2 + tt, :],
                                  start=True, stop=(tt == 0), skip_group_check=True)
                        if tt == 1:
                            mm = pe.matmul(dst, vtok[:, 0, c0:c0 + DH], scores_far[:, hh, kt, :],
                                           start=False, stop=True, skip_group_check=True)
            mm.then_inc(s.hg_o, 1)
            pe.wait_ge(s.hg_osq, l + 1)
            pe.matmul(bank[5][:, :], blk64, ee, start=True, stop=True).then_inc(s.hg_oms, 1)

        def halves(ap, L):
            v = ap.rearrange("p (b h t) -> p b h t", h=2, t=L)
            return v[:, :, 0, :], v[:, :, 1, :]

        def hg_dve(dve, l):
            z_ = proj_b[:, 0:2 * T]
            q_ = proj_b[:, 2 * T:4 * T]
            dve.wait_ge(s.sig, l + 1)
            for kt in range(2):
                c = slice(kt * T, (kt + 1) * T)
                dve.tensor_scalar(sg[:, c], sg[:, c], lb_u[:, 2 * l + kt:2 * l + kt + 1],
                                  lb_t[:, 2 * l + kt:2 * l + kt + 1], ALU.mult, ALU.add)
                dve.tensor_scalar(kc[:, c], kc[:, c], lb_u[:, 2 * l + kt:2 * l + kt + 1], None, ALU.mult)
            dve.tensor_scalar(q8, q_, DH ** -0.5, None, ALU.mult)
            dve.drain()
            dve.tensor_scalar(ee, sg, 1.0 / LN_SPLIT, None, ALU.max)
            dve.tensor_scalar(gg, sg, TINY, LN_SPLIT, ALU.max, ALU.mult)
            dve.drain()
            dve.tensor_scalar(gg, gg, 1.0, None, ALU.min).then_inc(s.hg_f, 1)
            dve.wait_ge(s.hg_ln, l + 1)
            dve.tensor_tensor(sg, ee, gg, ALU.add)
            dve.drain()
            dve.tensor_tensor_scan(gg, const(1, "reset"), sg, 0.0, ALU.mult, ALU.add)
            dve.drain()
            steps = list(HG_LEVELS) + [HG_CHUNK, None, "far"]

            def take(n):
                u, b0, b1 = hg_banks(l, n)
                dve.wait_ge(s.hg_x, u + 1)
                if n == 0:
                    dve.wait_ge(s.zeroed, l + 1)
                for hh, b in enumerate((b0, b1)):
                    if steps[n] == "far":
                        last = dve.tensor_copy(scores_far[:, hh, :, :], b[:, 0:2 * P].rearrange("p (b t) -> p b t", b=2))
                    else:
                        m = lvl_u[:, NL + 1 if steps[n] is None else n, :].unsqueeze(1).broadcast_to([P, 4, P])
                        last = dve.copy_predicated(scores_hg[:, hh, :, :], m,
                                                   b[:, :].rearrange("p (b t) -> p b t", b=4))
                last.then_inc(s.hg_sc, 1)

            for n, L in enumerate(steps):
                ada_dve(dve, l, MIX_STEPS + n)
                dve.drain()
                if L is None:
                    take(n - 1)
                    continue
                if L == "far":
                    v = gg.rearrange("p (k c t) -> p k c t", k=2, t=HG_CHUNK)
                    e = ee.rearrange("p (k c t) -> p k c t", k=2, t=HG_CHUNK)
                    end = lambda c: v[:, :, c, HG_CHUNK - 1:HG_CHUNK].broadcast_to([P, 2, HG_CHUNK])
                    dve.tensor_tensor(e[:, :, 0, :], end(0), v[:, :, 0, :], ALU.subtract)
                    dve.tensor_tensor(e[:, :, 1, :], end(1), v[:, :, 1, :], ALU.subtract)
                    dve.tensor_copy(e[:, :, 2, :], v[:, :, 2, :])
                    dve.tensor_tensor(e[:, :, 3, :], end(2), v[:, :, 3, :], ALU.add)
                    dve.drain()
                    dve.tensor_tensor(e[:, :, 0, :], e[:, :, 0, :], end(1), ALU.add).then_inc(s.hg_g, 1)
                else:
                    gl, gr = halves(gg, L)
                    el, er = halves(ee, L)
                    mid = gl[:, :, L - 1:L].broadcast_to(list(gl.shape))
                    dve.tensor_tensor(el, mid, gl, ALU.subtract)
                    if L == HG_CHUNK:
                        dve.tensor_copy(er, gr).then_inc(s.hg_g, 1)
                    else:
                        dve.tensor_tensor(er, gr, mid, ALU.subtract).then_inc(s.hg_g, 1)
                if n >= 1 and steps[n - 1] is not None or L == "far":
                    take(n - 1)
                dve.wait_ge(s.hg_e, hg_decayed(l, n) + 1)
                if L == "far":
                    kl, ql = [t.rearrange("p (k h t) -> p k h t", k=2, h=2)[:, :, i, :] for t, i in ((kc, 0), (q8, 1))]
                    eh = ee.rearrange("p (k h t) -> p k h t", k=2, h=2)
                    dst = qk.rearrange("p (k h t) -> p k h t", k=2, h=2)
                    el, er, dl, dr = eh[:, :, 0, :], eh[:, :, 1, :], dst[:, :, 0, :], dst[:, :, 1, :]
                else:
                    kl, ql = halves(kc, L)[0], halves(q8, L)[1]
                    dl, dr = halves(qk, L)
                dve.tensor_tensor(dl, el, kl, ALU.mult)
                dve.tensor_tensor(dr, er, ql, ALU.mult).then_inc(s.hg_qk, 1)
            take(HG_STEPS - 1)
            dve.wait_ge(s.hg_ors, l + 1)
            dve.scalar_tensor_tensor(out=gg, in0=bank[4][:, :], scalar=param(f"onorm@{l}"), in1=ee,
                                     op0=ALU.mult, op1=ALU.mult)
            dve.tensor_tensor(sg, proj_b[:, 16 * T:18 * T], sga, ALU.mult)
            dve.drain()
            dve.tensor_tensor(mix_b[:, 0:2 * T], gg, sg, ALU.mult).then_inc(s.mixa, 1)

        def hg_act(act, l):
            act.wait_ge(s.hg_f, l + 1)
            act.activation(ee, ee, ACT.Ln)
            act.activation(gg, gg, ACT.Ln).then_inc(s.hg_ln, 1)
            for n in range(HG_STEPS - 1):
                ada_act(act, l, MIX_STEPS + n)
                u = l * (HG_STEPS - 1) + n
                act.wait_ge(s.hg_g, u + 1)
                act.activation(ee, ee, ACT.Exp).then_inc(s.hg_e, 1)
            act.wait_ge(s.hg_o, l + 1)
            act.activation(ee, bank[4][:, :], ACT.Square).then_inc(s.hg_osq, 1)
            act.wait_ge(s.hg_oms, l + 1)
            act.activation(qk, bank[5][:, :], ACT.Ln, bias=eps_col)
            act.drain()
            act.activation(ee, qk, ACT.Exp, scale=-0.5).then_inc(s.hg_ors, 1)

        def dense_t(pe, lin, norm):
            w = norm_width(norm)
            for g in turns(pe, lin):
                wait_banks(pe, lin, g)
                wait_weights(pe, lin, g, 0)
                for k in range(KT):
                    if g.at == 0:
                        wait_normed(pe, norm, k)
                    mm = pe.matmul(bank[2 * parity(lin, g)][:, 0:w], ring[:, slot_of(lin, g, 0), k * P:(k + 1) * P],
                                   hn[:, k, 0:w], start=(k == 0), stop=(k == KT - 1))
                mm.then_inc(used[slot_of(lin, g, 0)], 1)

        def block1_pe(pe, l):
            norm_pe(pe, 2 * l)
            dense_t(pe, PLAN["in_t", l], 2 * l)
            lin = PLAN["in_a", l]
            for g in turns(pe, lin):
                wait_banks(pe, lin, g)
                wait_weights(pe, lin, g, 0)
                for tt in range(TT):
                    for k in range(KT):
                        mm = pe.matmul(bank[2 * parity(lin, g)][:, tt * P:(tt + 1) * P],
                                       hn[:, k, tt * P:(tt + 1) * P],
                                       ring[:, slot_of(lin, g, 0), k * P:(k + 1) * P],
                                       start=(k == 0), stop=(k == KT - 1))
                mm.then_inc(used[slot_of(lin, g, 0)], 1)
            pe.wait_ge(s.hn_sq, l + 1)
            for u in range(5):
                if u >= 2:
                    pe.wait_ge(s.hn_ln, 5 * l + u - 1)
                pe.matmul(bank[4 + u % 2][:, :], blk64, sq_b[:, u * 2 * T:(u + 1) * 2 * T],
                          start=True, stop=True).then_inc(s.hn_ms, 1)
            pe.wait_ge(s.qkn, l + 1)
            pe.matmul(bank[4][:, :], rot, qkn_b[:, 2 * T:4 * T], start=True, stop=True).then_inc(s.rotated, 1)
            pe.matmul(bank[5][:, :], rot, qkn_b[:, 4 * T:6 * T], start=True, stop=True).then_inc(s.rotated, 1)
            for g in range(2):
                if g == 1:
                    pe.wait_ge(s.rope, 4 * l + 3)
                pe.matmul(bank[6][:, :], dup[:, g, :], qkn_b[:, 0:2 * T], start=True, stop=True)
                pe.matmul(bank[7][:, :], rotdup[:, g, :], qkn_b[:, 0:2 * T],
                          start=True, stop=True).then_inc(s.rotated, 1)
            lin = PLAN["cmp", l]
            for g in turns(pe, lin):
                wait_banks(pe, lin, g)
                pe.wait_ge(s.blocks, 2 * l + g.m + 1)
                for c in range(4):
                    wait_weights(pe, lin, g, c)
                    for i in range(8):
                        mm = pe.matmul(bank[2 * parity(lin, g)][:, 0:2 * N_CMP],
                                       ring[:, slot_of(lin, g, c), i * P:(i + 1) * P],
                                       bc_b[:, (g.m * CMP_L + 8 * c + i) * 2 * N_CMP:(g.m * CMP_L + 8 * c + i + 1) * 2 * N_CMP],
                                       start=(c == 0 and i == 0), stop=(c == 3 and i == 7))
                    mm.then_inc(used[slot_of(lin, g, c)], 1)
            pe.wait_ge(s.rope, 4 * l + 4)
            wait_drained(pe, lin, 0)
            pe.matmul(bank[4][:, 0:2 * N_CMP], param(f"w2k@{l}"), hk, start=True, stop=True).then_inc(s.cmp_raw, 1)
            wait_drained(pe, lin, 1)
            for g in range(2):
                mm = pe.matmul(bank[5][0:N_CMP, g * DH:(g + 1) * DH], hv[:, g * N_CMP:(g + 1) * N_CMP],
                               param(f"w2v@{l}"), start=True, stop=True)
            mm.then_inc(s.cmp_raw, 1)
            pe.wait_ge(s.kc_sq, l + 1)
            pe.matmul(bank[6][:, 0:2 * N_CMP], blk64, krot, start=True, stop=True).then_inc(s.kc_ms, 1)
            pe.wait_ge(s.kc_n, l + 1)
            pe.matmul(bank[7][:, 0:2 * N_CMP], rot, kcn, start=True, stop=True).then_inc(s.kc_rot, 1)
            pe.wait_ge(s.kc_done, l + 1)
            pe.wait_ge(s.vc_done, l + 1)
            pe.wait_ge(s.fa, l + 1)
            attention_pe(pe, l, units_block1(l))
            pe.wait_ge(s.att_o, N_OUTS1 // DEPTH * (l + 1))
            hg_pe(pe, l)
            lin = PLAN["wo", l]
            pe.wait_ge(s.mixa, l + 1)
            for g in turns(pe, lin):
                wait_banks(pe, lin, g)
                wait_weights(pe, lin, g, 0)
                for k in range(KT):
                    mm = pe.matmul(bank[2 * parity(lin, g)][:, 0:T], ring[:, slot_of(lin, g, 0), k * P:(k + 1) * P],
                                   mixt[:, k, :], start=(k == 0), stop=(k == KT - 1))
                mm.then_inc(used[slot_of(lin, g, 0)], 1)
            norm_pe(pe, 2 * l + 1)
            dense_t(pe, PLAN["up", l], 2 * l + 1)
            lin = PLAN["down", l]
            wait_all_drained(pe, PLAN["up", l])
            for g in turns(pe, lin):
                wait_banks(pe, lin, g)
                for c in range(lin.cpg):
                    wait_weights(pe, lin, g, c)
                    for k in range(8):
                        mm = pe.matmul(bank[2 * parity(lin, g)][:, 0:T],
                                       ring[:, slot_of(lin, g, c), k * P:(k + 1) * P], hid1[:, 8 * c + k, :],
                                       start=(c == 0 and k == 0), stop=(c == lin.cpg - 1 and k == 7))
                    mm.then_inc(used[slot_of(lin, g, c)], 1)

        def block1_act(act, l):
            norm_act(act, 2 * l)
            lin = PLAN["in_t", l]
            for g in turns(act, lin):
                wait_products(act, lin, g)
                act.activation(proj[:, g.m, :], bank[2 * parity(lin, g)][:, 0:T],
                               ACT.Copy).then_inc(drained[parity(lin, g)], 1)
            lin = PLAN["in_a", l]
            for g in turns(act, lin):
                wait_products(act, lin, g)
                act.activation(vtok[:, :, g.m * P:(g.m + 1) * P],
                               bank[2 * parity(lin, g)][:, 0:T].rearrange("p (t c) -> p t c", t=TT),
                               ACT.Copy).then_inc(drained[parity(lin, g)], 1)
            act.drain()
            act.activation(sq_b, proj_b[:, 4 * T:14 * T], ACT.Square).then_inc(s.hn_sq, 1)
            for u in range(5):
                act.wait_ge(s.hn_ms, 5 * l + u + 1)
                act.activation(sq_b[:, u * 2 * T:(u + 1) * 2 * T], bank[4 + u % 2][:, :], ACT.Ln,
                               bias=eps_col).then_inc(s.hn_ln, 1)
            act.drain()
            act.activation(sq_b, sq_b, ACT.Exp, scale=-0.5).then_inc(s.hn_rs, 1)
            act.wait_ge(s.fox_in, l + 1)
            act.activation(lx, lx, ACT.Exp, scale=-1.0)
            act.drain()
            act.activation(ly, lx, ACT.Ln, bias=one_col).then_inc(s.fox_e, 1)
            act.activation(sg, proj_b[:, 0:2 * T], ACT.Sigmoid)
            act.activation(kc, proj_b[:, 0:2 * T], ACT.Sigmoid, scale=-1.0)
            act.activation(sga, proj_b[:, 16 * T:18 * T], ACT.Sigmoid)
            act.activation(gate, vtok[:, :, 0:24], ACT.Sigmoid).then_inc(s.sig, 1)
            lin = PLAN["cmp", l]
            for g, dst in zip(turns(act, lin), (hk, hv)):
                wait_products(act, lin, g)
                act.activation(dst, bank[2 * parity(lin, g)][:, 0:2 * N_CMP],
                               ACT.Gelu_apprx_tanh).then_inc(drained[parity(lin, g)], 1)
            act.wait_ge(s.cmp_raw, 2 * l + 1)
            act.activation(krot, bank[4][:, 0:2 * N_CMP], ACT.Square).then_inc(s.kc_sq, 1)
            act.wait_ge(s.kc_ms, l + 1)
            act.activation(kcb, bank[6][:, 0:2 * N_CMP], ACT.Ln, bias=eps_col)
            act.drain()
            act.activation(kcb, kcb, ACT.Exp, scale=-0.5).then_inc(s.kc_rs, 1)
            attention_act(act, l, units_block1(l))
            hg_act(act, l)
            norm_act(act, 2 * l + 1)
            lin = PLAN["up", l]
            for g in turns(act, lin):
                wait_products(act, lin, g)
                act.activation(hid1[:, g.m, :], bank[2 * parity(lin, g)][:, 0:T], ACT.Relu)
                act.drain()
                act.activation(hid1[:, g.m, :], hid1[:, g.m, :], ACT.Square).then_inc(drained[parity(lin, g)], 1)

        def norm1_dve(dve, n, gain):
            dve.wait_ge(s.rstd, n + 1)
            for k in range(KT):
                dve.scalar_tensor_tensor(out=hn[:, k, 0:T], in0=res[:, k, 0:T], scalar=gain[:, k:k + 1],
                                         in1=rstd[:, 0:T], op0=ALU.mult, op1=ALU.mult).then_inc(s.normed, 1)

        def add_to_residual(dve, lin):
            for g in turns(dve, lin):
                wait_products(dve, lin, g)
                dve.tensor_tensor(res[:, g.m, 0:T], bank[2 * parity(lin, g)][:, 0:T], res[:, g.m, 0:T],
                                  ALU.add).then_inc(drained[parity(lin, g)], 1)

        def block1_dve(dve, l):
            norm1_dve(dve, 2 * l, param(f"norm1@{l}"))
            wait_drained(dve, PLAN["in_a", l], 0)
            for tt in range(TT):
                dve.tensor_tensor(lx[:, 4 * tt:4 * tt + 4], vtok[:, tt, 24:28], param(f"fb@{l}"), ALU.add)
            dve.drain()
            dve.tensor_scalar(lz, lx, 0.0, None, ALU.min)
            dve.tensor_scalar(ly, lx, -1.0, None, ALU.mult)
            dve.drain()
            dve.tensor_tensor(lx, lx, ly, ALU.max).then_inc(s.fox_in, 1)
            dve.tensor_copy(qkg, param(f"qkg@{l}"))
            dve.drain()
            dve.tensor_scalar(qkg[:, 6:8], qkg[:, 6:8], DH ** -0.5, None, ALU.mult)
            dve.drain()
            dve.wait_ge(s.hn_rs, l + 1)
            for j in range(10):
                last = dve.scalar_tensor_tensor(out=qkn[:, j, :], in0=proj[:, 4 + j, :], scalar=qkg[:, j:j + 1],
                                                in1=sqh[:, j, :], op0=ALU.mult, op1=ALU.mult)
            last.then_inc(s.qkn, 1)
            dve.drain()
            cos2 = cos.unsqueeze(1).broadcast_to([P, 2, T])
            sin2 = sin.unsqueeze(1).broadcast_to([P, 2, T])
            tmp = ee.rearrange("p (m t) -> p m t", m=2)
            for u in range(2):
                dve.wait_ge(s.rotated, 4 * l + u + 1)
                dve.tensor_tensor(qr[:, 2 * u:2 * u + 2, :], qkn[:, 2 + 2 * u:4 + 2 * u, :], cos2, ALU.mult)
                dve.tensor_tensor(tmp, bank[4 + u][:, :].rearrange("p (m t) -> p m t", m=2), sin2, ALU.mult)
                dve.drain()
                dve.tensor_tensor(qr[:, 2 * u:2 * u + 2, :], qr[:, 2 * u:2 * u + 2, :], tmp,
                                  ALU.add).then_inc(s.rope, 1)
                dve.drain()
            for g in range(2):
                dve.wait_ge(s.rotated, 4 * l + 3 + g)
                dve.tensor_tensor(kd[:, g, :, :], bank[6][:, :].rearrange("p (m t) -> p m t", m=2), cos2, ALU.mult)
                dve.tensor_tensor(tmp, bank[7][:, :].rearrange("p (m t) -> p m t", m=2), sin2, ALU.mult)
                dve.drain()
                dve.tensor_tensor(kd[:, g, :, :], kd[:, g, :, :], tmp, ALU.add).then_inc(s.rope, 1)
                dve.drain()
            dve.wait_ge(s.fox_e, l + 1)
            dve.tensor_tensor(lf, lz, ly, ALU.subtract)
            dve.drain()
            for st in range(TT):
                for h in range(4):
                    last = dve.tensor_scalar(fa[:, st, h, :], tri[:, st, :], lf[:, 4 * st + h:4 * st + h + 1], None,
                                             ALU.mult)
            last.then_inc(s.fa, 1)
            dve.wait_ge(s.kc_rs, l + 1)
            dve.scalar_tensor_tensor(out=kcn, in0=bank[4][:, 0:2 * N_CMP], scalar=param(f"kng@{l}"), in1=kcb,
                                     op0=ALU.mult, op1=ALU.mult).then_inc(s.kc_n, 1)
            dve.drain()
            dve.wait_ge(s.cmp_raw, 2 * l + 2)
            dve.tensor_copy(vc_b[0:N_CMP, :], bank[5][0:N_CMP, 0:2 * DH]).then_inc(s.vc_done, 1)
            dve.wait_ge(s.kc_rot, l + 1)
            dve.tensor_tensor(kcb, kcn, const(1, "ccos"), ALU.mult)
            dve.tensor_tensor(krot, bank[7][:, 0:2 * N_CMP], const(1, "csin"), ALU.mult)
            dve.drain()
            dve.tensor_tensor(kcb, kcb, krot, ALU.add).then_inc(s.kc_done, 1)
            dve.wait_ge(s.sig, l + 1)
            attention_dve(dve, l, units_block1(l))
            hg_dve(dve, l)
            add_to_residual(dve, PLAN["wo", l])
            norm1_dve(dve, 2 * l + 1, param(f"norm2@{l}"))
            add_to_residual(dve, PLAN["down", l])

        def block1_pool(pool, l):
            if l >= 1:
                pool.wait_ge(s.mixa, l)
            wait_all_drained(pool, PLAN["in_t", l])
            if l >= 1:
                wait_all_drained(pool, PLAN["down", l - 1])
                pool.wait_ge(s.blocks, 2 * l)
            pool.memset(sc_b, 0.0).then_inc(s.zeroed, 1)
            pool.wait_ge(s.zeroed, l + 1)
            pos = param(f"pos@{l}").rearrange("p (w l) -> p w l", w=2)
            for w in range(2):
                for g in range(2):
                    rows = slice(g * DH, g * DH + DH)
                    for h in range(2):
                        src = proj[rows, 14 + w, 16 * h:16 * h + 16 * N_CMP].rearrange("p (n l) -> p l n", l=16)
                        add = pos[rows, w, 16 * h:16 * h + 16].unsqueeze(2).broadcast_to([DH, 16, N_CMP])
                        last = pool.tensor_tensor(bc[rows, w, 16 * h:16 * h + 16, g, :], src, add, ALU.add)
                last.then_inc(s.blocks, 1)


        gs = gate_b.rearrange("p (n k c) -> p n k c", n=3, c=2)
        tmp2 = sm2_b.rearrange("p (u t) -> p u t", u=2)
        tmp3 = pr2_b.rearrange("p (u t) -> p u t", u=2)
        tmp4 = (rstd2, lnb2)
        SHIFT, SCALE, GATE = (0, 3, 6), (1, 4, 7), (2, 5, 8)

        def seqs(l):
            return 2 if l < DEPTH - 1 else 1

        def both(ap, w):
            return ap[:, 0:w].rearrange("p (s t) -> p s t", t=T)

        def units_block2(l):
            out = [Unit("lat", tt, h=h) for tt in range(TT) for h in range(QH)]
            if seqs(l) == 2:
                out += [Unit("ctx", TT + tt, h=2 * x) for tt in range(TT) for x in range(QH // 2)]
            u0 = N_UNITS1 + sum(len(units_block2(i)) for i in range(l))
            o0 = N_OUTS1 + sum(len(units_block2(i)) for i in range(l))
            for n, x in enumerate(out):
                x.u, x.o = u0 + n, o0 + n
                x.heads = 1 if x.kind == "lat" else 2
                x.keys = 4 * P // x.heads
                x.key0 = 0 if x.kind == "lat" else T
            return out

        def latent_scores(pe, x):
            pe.wait_ge(s.att_e, x.u - 1)
            for j in range(x.heads):
                mm = pe.matmul(scores(x)[:, j * x.keys:(j + 1) * x.keys],
                               q2[0:QK, x.h + j, x.tt * P:(x.tt + 1) * P],
                               k2[0:QK, x.h + j, x.key0:x.key0 + x.keys], start=True, stop=True)
            mm.then_inc(s.att_s, 1)

        def latent_turn(pe, x):
            pe.wait_ge(s.att_p, x.u + 1)
            pe.wait_ge(s.att_c, x.u)
            for k in range(4):
                mm = pe.transpose(bank[6][:, k * P:(k + 1) * P], pr[:, x.u % 2, k * P:(k + 1) * P], ident)
            mm.then_inc(s.att_t, 1)

        def latent_values(pe, x):
            pe.wait_ge(s.att_c, x.u + 1)
            pe.wait_ge(s.att_o, x.o - 1 if x.heads == 1 else x.o)
            kt = 4 // x.heads
            for j in range(x.heads):
                h = x.h + j
                rows = slice((h % 2) * DH, (h % 2) * DH + DH)
                for k in range(kt):
                    mm = pe.matmul(bank[7][rows, 0:P], v2[:, x.key0 // P + k, h * DH:(h + 1) * DH],
                                   pt[:, x.u % 2, (j * kt + k) * P:(j * kt + k + 1) * P],
                                   start=(k == 0), stop=(k == kt - 1), skip_group_check=True)
            mm.then_inc(s.att_v, 1)

        def latent_max(dve, x):
            dve.wait_ge(s.att_s, x.u + 1)
            dve.wait_ge(s.att_e, x.u - 1)
            at = 2 * (x.u % 2)
            dve.tensor_reduce(mx[:, at:at + x.heads], scores(x)[:, :].rearrange("p (j k) -> p j k", j=x.heads),
                              AX_X, ALU.max)
            dve.drain()
            dve.tensor_scalar(negmx[:, at:at + x.heads], mx[:, at:at + x.heads], -ATTN_SCALE, None,
                              ALU.mult).then_inc(s.att_m, 1)

        def latent_norm(dve, x):
            dve.wait_ge(s.att_e, x.u + 1)
            at = 2 * (x.u % 2)
            dve.reciprocal(rcp[:, at:at + x.heads], smu[:, at:at + x.heads])
            dve.drain()
            for j in range(x.heads):
                c = slice(j * x.keys, (j + 1) * x.keys)
                last = dve.tensor_scalar(pr[:, x.u % 2, c], pr[:, x.u % 2, c], rcp[:, at + j:at + j + 1], None,
                                         ALU.mult)
            last.then_inc(s.att_p, 1)

        def latent_exp(act, x):
            act.wait_ge(s.att_m, x.u + 1)
            act.wait_ge(s.att_t, x.u - 1)
            at = 2 * (x.u % 2)
            for j in range(x.heads):
                c = slice(j * x.keys, (j + 1) * x.keys)
                last = act.activation(pr[:, x.u % 2, c], scores(x)[:, c], ACT.Exp, scale=ATTN_SCALE,
                                      bias=negmx[:, at + j:at + j + 1], accum_out=smu[:, at + j:at + j + 1])
            last.then_inc(s.att_e, 1)

        def latent_copy(act, x):
            act.wait_ge(s.att_t, x.u + 1)
            act.wait_ge(s.att_v, x.u - 1)
            act.activation(pt[:, x.u % 2, :], bank[6][:, :], ACT.Copy).then_inc(s.att_c, 1)

        def latent_out(act, x):
            act.wait_ge(s.att_v, x.u + 1)
            rows = slice((x.h % 2) * DH, (x.h % 2) * DH + DH) if x.heads == 1 else slice(0, P)
            act.activation(att[rows, x.h // 2, x.tt * P:(x.tt + 1) * P], bank[7][rows, 0:P],
                           ACT.Copy).then_inc(s.att_o, 1)

        def gated_norm_dve(dve, l, which):
            n = 2 * DEPTH + 3 * l + which
            w = norm_width(n)
            mod = modulation(l)
            dve.wait_ge(s.rstd, n + 1)
            for k0 in range(0, KT, 2):
                for k in (k0, k0 + 1):
                    dve.tensor_tensor(hn[:, k, 0:w], res[:, k, 0:w], rstd[:, 0:w], ALU.mult)
                dve.drain()
                for k in (k0, k0 + 1):
                    for c in range(w // T):
                        last = dve.tensor_scalar(hn[:, k, c * T:(c + 1) * T], hn[:, k, c * T:(c + 1) * T],
                                                 gs[:, which, k, c:c + 1], mod[:, SHIFT[which], k, c:c + 1],
                                                 ALU.mult, ALU.add)
                    last.then_inc(s.normed, 1)

        def gated_add(dve, l, lin, which, w):
            mod = modulation(l)
            for g in turns(dve, lin):
                wait_products(dve, lin, g)
                for c in range(w // T):
                    t = slice(c * T, (c + 1) * T)
                    last = dve.scalar_tensor_tensor(out=res[:, g.m, t], in0=bank[2 * parity(lin, g)][:, t],
                                                    scalar=mod[:, GATE[which], g.m, c:c + 1], in1=res[:, g.m, t],
                                                    op0=ALU.mult, op1=ALU.add)
                last.then_inc(drained[parity(lin, g)], 1)

        def ffn_pe(pe, l, which):
            n = 2 * DEPTH + 3 * l + which
            w = norm_width(n)
            lin = PLAN["ffn1" if which == 0 else "ffn2", l]
            norm_pe(pe, n)
            for g in turns(pe, lin):
                wait_banks(pe, lin, g)
                for c in range(2):
                    wait_weights(pe, lin, g, c)
                    for k in range(KT):
                        if g.at == 0 and c == 0:
                            wait_normed(pe, n, k)
                        mm = pe.matmul(bank[2 * parity(lin, g) + c][:, 0:w],
                                       ring[:, slot_of(lin, g, c), k * P:(k + 1) * P], hn[:, k, 0:w],
                                       start=(k == 0), stop=(k == KT - 1))
                    mm.then_inc(used[slot_of(lin, g, c)], 1)
            wait_all_drained(pe, lin)
            lin = PLAN["ffn1_out" if which == 0 else "ffn2_out", l]
            for g in turns(pe, lin):
                wait_banks(pe, lin, g)
                for c in range(2):
                    wait_weights(pe, lin, g, c)
                    for k in range(11):
                        mm = pe.matmul(bank[2 * parity(lin, g)][:, 0:w],
                                       ring[:, slot_of(lin, g, c), k * P:(k + 1) * P], hid2[:, 11 * c + k, 0:w],
                                       start=(c == 0 and k == 0), stop=(c == 1 and k == 10))
                    mm.then_inc(used[slot_of(lin, g, c)], 1)

        def ffn_act(act, l, which):
            n = 2 * DEPTH + 3 * l + which
            norm_act(act, n)
            lin = PLAN["ffn1" if which == 0 else "ffn2", l]
            for g in turns(act, lin):
                act.wait_ge(used[slot_of(lin, g, 0)], turn_of(lin, g, 0) + 1)
                act.activation(tmp2[:, parity(lin, g), 0:norm_width(n)],
                               bank[2 * parity(lin, g)][:, 0:norm_width(n)], ACT.Silu).then_inc(s.silu, 1)

        def ffn_dve(dve, l, which):
            w = norm_width(2 * DEPTH + 3 * l + which)
            gated_norm_dve(dve, l, which)
            lin = PLAN["ffn1" if which == 0 else "ffn2", l]
            before = FF2 * (2 * l + which // 2)
            for g in turns(dve, lin):
                wait_products(dve, lin, g)
                dve.wait_ge(s.silu, g.m + (before + 1))
                dve.tensor_tensor(hid2[:, g.m, 0:w], bank[2 * parity(lin, g) + 1][:, 0:w],
                                  tmp2[:, parity(lin, g), 0:w], ALU.mult).then_inc(drained[parity(lin, g)], 1)
            gated_add(dve, l, PLAN["ffn1_out" if which == 0 else "ffn2_out", l], which, w)

        def fourier_steps(l):
            first = [(1, c, tt, gp) for c in range(seqs(l)) for tt in range(TT) for gp in range(2)]
            steps = first + [(2, g, 0, 0) for g in range(G4)]
            u0 = sum(len(fourier_steps(i)) for i in range(l))
            return [(u0 + n,) + x for n, x in enumerate(steps)]

        def fourier_pe(pe, l):
            wait_all_drained(pe, PLAN["lat_in", l])
            for u, stage, a, tt, gp in fourier_steps(l):
                b = bank[4 + u % 2]
                if u >= 2:
                    pe.wait_ge(s.f_sb, u - 1)
                if stage == 1:
                    for j in range(2):
                        mm = pe.matmul(b[:, j * T:(j + 1) * T],
                                       z[:, 6 + 2 * gp + j, a * T + tt * P:a * T + (tt + 1) * P], dft_c,
                                       start=True, stop=True)
                else:
                    if a == 0:
                        pe.wait_ge(s.f_sb, u)
                    for c in range(seqs(l)):
                        for i in range(4):
                            mm = pe.matmul(b[:, c * T:(c + 1) * T],
                                           f1[:, c, i // 2, a, (i % 2) * P:(i % 2 + 1) * P],
                                           dft_t[:, i // 2, i % 2, :], start=(i == 0), stop=(i == 3))
                mm.then_inc(s.f_mm, 1)

        def fourier_act(act, l):
            for u, stage, a, tt, gp in fourier_steps(l):
                act.wait_ge(s.f_mm, u + 1)
                b = bank[4 + u % 2]
                if stage == 1:
                    act.activation(f1[:, a, tt, 2 * gp:2 * gp + 2, :], b[:, :].rearrange("p (g c) -> p g c", g=2),
                                   ACT.Copy).then_inc(s.f_sb, 1)
                else:
                    act.activation(four[:, a, 0:seqs(l) * T], b[:, 0:seqs(l) * T], ACT.Copy).then_inc(s.f_sb, 1)

        BRANCHES = (("mrg_conv", 3, 0), ("mrg_four", 4, 16), ("mrg_mla", 4, 8))

        def branch_pe(pe, l, b, g):
            name, kt, _ = BRANCHES[b]
            w = seqs(l) * T
            lin = PLAN[name, l]
            src = (cvo, four, att)[b]
            wait_banks(pe, lin, g)
            for k in range(kt):
                if k == 0:
                    wait_weights(pe, lin, g, 0)
                mm = pe.matmul(bank[2 * parity(lin, g)][:, 0:w], ring[:, slot_of(lin, g, 0), k * P:(k + 1) * P],
                               src[:, k, 0:w], start=(k == 0), stop=(k == kt - 1))
            last = lin.cpg - 1
            if last:
                mm.then_inc(used[slot_of(lin, g, 0)], 1)
                wait_weights(pe, lin, g, 1)
            k0 = 0 if last else kt
            for k in range(KT):
                mm = pe.matmul(bank[2 * parity(lin, g) + 1][:, 0:w],
                               ring[:, slot_of(lin, g, last), (k0 + k) * P:(k0 + k + 1) * P],
                               hn[:, k, 0:w], start=(k == 0), stop=(k == KT - 1))
            mm.then_inc(used[slot_of(lin, g, last)], 1)

        def branch_act(act, l, b, g):
            name, _, tile0 = BRANCHES[b]
            w = seqs(l) * T
            lin = PLAN[name, l]
            bias = param(f"bbg@@{l}").rearrange("p (m c) -> p m c", c=1)
            wait_products(act, lin, g)
            act.activation(tmp2[:, parity(lin, g), 0:w], bank[2 * parity(lin, g) + 1][:, 0:w], ACT.Sigmoid,
                           bias=bias[:, g.m + tile0, :]).then_inc(s.sig_g, 1)

        def branch_dve(dve, l, b, g):
            w = seqs(l) * T
            q = parity(PLAN[BRANCHES[b][0], l], g)
            dve.wait_ge(s.sig_g, g.m + (KT * (3 * l + b) + 1))
            if b < 2:
                bias = param((f"bpw@@{l}", f"bfour@@{l}")[b]).rearrange("p (m c) -> p m c", c=1)[:, g.m, :]
            else:
                bias = 0.0
            dst = mrg[:, g.m, 0:w] if b == 0 else tmp4[q][:, 0:w]
            one = dve.scalar_tensor_tensor(out=dst, in0=bank[2 * q][:, 0:w], scalar=bias, in1=tmp2[:, q, 0:w],
                                           op0=ALU.add, op1=ALU.mult)
            if b == 0:
                one.then_inc(drained[q], 1)
            else:
                dve.drain()
                dve.tensor_tensor(mrg[:, g.m, 0:w], mrg[:, g.m, 0:w], tmp4[q][:, 0:w],
                                  ALU.add).then_inc(drained[q], 1)

        def between_units(branch, eng, l, n):
            if 0 <= n < 2 * KT:
                branch(eng, l, n // KT, Group(n % KT, n % KT, 0, KT))

        def block2_pe(pe, l):
            n = 2 * DEPTH + 3 * l
            if l == 0:
                pe.wait_ge(s.consts2, 32)
            ffn_pe(pe, l, 0)
            norm_pe(pe, n + 1)
            w = seqs(l) * T
            lin = PLAN["conv_in", l]
            for g in turns(pe, lin):
                wait_banks(pe, lin, g)
                for c in range(2):
                    wait_weights(pe, lin, g, c)
                    for k in range(KT):
                        if g.at == 0 and c == 0:
                            wait_normed(pe, n + 1, k)
                        mm = pe.matmul(bank[2 * parity(lin, g) + c][:, 0:w],
                                       ring[:, slot_of(lin, g, c), k * P:(k + 1) * P], hn[:, k, 0:w],
                                       start=(k == 0), stop=(k == KT - 1))
                    mm.then_inc(used[slot_of(lin, g, c)], 1)
            lin = PLAN["lat_in", l]
            for g in turns(pe, lin):
                wait_banks(pe, lin, g)
                wait_weights(pe, lin, g, 0)
                wg = 2 * T if g.m < 3 else w
                for k in range(KT):
                    mm = pe.matmul(bank[2 * parity(lin, g)][:, 0:wg], ring[:, slot_of(lin, g, 0), k * P:(k + 1) * P],
                                   hn[:, k, 0:wg], start=(k == 0), stop=(k == KT - 1))
                mm.then_inc(used[slot_of(lin, g, 0)], 1)
            pe.wait_ge(s.c_sq, l + 1)
            for k in range(3):
                mm = pe.matmul(bank[6][:, 0:w], const(2, "ones_ct"), q2[:, 3 + k, 0:w], start=(k == 0), stop=(k == 2))
            mm.then_inc(s.c_ms, 1)
            for k in range(2):
                mm = pe.matmul(bank[7][:, :], const(2, "ones_kv"), q2[:, 6 + k, :], start=(k == 0), stop=(k == 1))
            mm.then_inc(s.c_ms, 1)
            fourier_pe(pe, l)
            pe.wait_ge(s.cv_done, l + 1)
            pe.wait_ge(s.f_sb, fourier_steps(l)[-1][0] + 1)
            for k in range(CT):
                mm = pe.matmul(bank[4][:, 0:w], const(2, "ones_ct"), cvo[:, k, 0:w], start=(k == 0), stop=(k == CT - 1))
            mm.then_inc(s.ln_ms, 1)
            pe.wait_ge(s.ln_sq, l + 1)
            for k in range(CT):
                mm = pe.matmul(bank[5][:, 0:w], const(2, "ones_ct"), q2[:, k, 0:w], start=(k == 0), stop=(k == CT - 1))
            mm.then_inc(s.ln_ms, 1)
            pe.wait_ge(s.c_n, l + 1)
            pe.matmul(bank[6][:, 0:T], const(2, "rot96"), z[:, 2, 0:T], start=True, stop=True).then_inc(s.kr_rot, 1)
            lin = PLAN["uq", l]
            for g in turns(pe, lin):
                wait_banks(pe, lin, g)
                wait_weights(pe, lin, g, 0)
                for k in range(3):
                    mm = pe.matmul(bank[2 * parity(lin, g)][:, 0:w], ring[:, slot_of(lin, g, 0), k * P:(k + 1) * P],
                                   z[:, 3 + k, 0:w], start=(k == 0), stop=(k == 2))
                mm.then_inc(used[slot_of(lin, g, 0)], 1)
            lin = PLAN["uk", l]
            for g in turns(pe, lin):
                wait_banks(pe, lin, g)
                wait_weights(pe, lin, g, 0)
                for k in range(2):
                    mm = pe.matmul(bank[2 * parity(lin, g)][:, :], ring[:, slot_of(lin, g, 0), k * P:(k + 1) * P],
                                   z[:, k, :], start=(k == 0), stop=(k == 1))
                mm.then_inc(used[slot_of(lin, g, 0)], 1)
            pe.wait_ge(s.kr_done, l + 1)
            pe.wait_ge(s.ln_n, l + 1)
            lin = PLAN["uv", l]
            for g in turns(pe, lin):
                wait_weights(pe, lin, g, 0)
                for tt in range(4):
                    for k in range(2):
                        mm = pe.matmul(bank[4 + tt][:, :], z[:, k, tt * P:(tt + 1) * P],
                                       ring[:, slot_of(lin, g, 0), k * 4 * P:(k + 1) * 4 * P],
                                       start=(k == 0), stop=(k == 1))
                mm.then_inc(used[slot_of(lin, g, 0)], 1)
            wait_all_drained(pe, PLAN["uq", l])
            pe.wait_ge(s.v_done, 4 * (l + 1))
            for u in range(4):
                if u >= 2:
                    pe.wait_ge(s.q_done, 4 * l + u - 1)
                pe.matmul(bank[4 + u % 2][:, :], const(2, "rot96"), q2[:, 2 * u:2 * u + 2, 0:T],
                          start=True, stop=True).then_inc(s.q_rot, 1)
            wait_all_drained(pe, PLAN["uk", l])
            pe.wait_ge(s.q_done, 4 * (l + 1))
            units = units_block2(l)
            pe.wait_ge(s.ln_out, l + 1)
            for i in range(len(units) + 2):
                between_units(branch_pe, pe, l, i)
                if i < len(units):
                    latent_scores(pe, units[i])
                if 1 <= i <= len(units):
                    latent_turn(pe, units[i - 1])
                if i >= 2:
                    latent_values(pe, units[i - 2])
            pe.wait_ge(s.att_o, units[-1].o + 1)
            for g in turns(pe, PLAN["mrg_mla", l]):
                branch_pe(pe, l, 2, g)
            wait_all_drained(pe, PLAN["mrg_mla", l])
            lin = PLAN["mix_out", l]
            for g in turns(pe, lin):
                wait_banks(pe, lin, g)
                wait_weights(pe, lin, g, 0)
                for k in range(KT):
                    mm = pe.matmul(bank[2 * parity(lin, g)][:, 0:w], ring[:, slot_of(lin, g, 0), k * P:(k + 1) * P],
                                   mrg[:, k, 0:w], start=(k == 0), stop=(k == KT - 1))
                mm.then_inc(used[slot_of(lin, g, 0)], 1)
            ffn_pe(pe, l, 2)

        def block2_act(act, l):
            n = 2 * DEPTH + 3 * l
            w = seqs(l) * T
            ffn_act(act, l, 0)
            norm_act(act, n + 1)
            lin = PLAN["conv_in", l]
            for g in turns(act, lin):
                wait_products(act, lin, g)
                act.activation(tmp2[:, parity(lin, g), 0:w], bank[2 * parity(lin, g) + 1][:, 0:w],
                               ACT.Sigmoid).then_inc(s.cv_in, 1)
            lin = PLAN["lat_in", l]
            for g in turns(act, lin):
                wait_products(act, lin, g)
                wg = 2 * T if g.m < 3 else w
                act.activation(z[:, g.m, 0:wg], bank[2 * parity(lin, g)][:, 0:wg],
                               ACT.Copy).then_inc(drained[parity(lin, g)], 1)
                if g.m == 5:
                    act.drain()
                    act.activation(q2[:, 3:6, 0:w], z[:, 3:6, 0:w], ACT.Square)
                    act.activation(q2[:, 6:8, :], z[:, 0:2, :], ACT.Square).then_inc(s.c_sq, 1)
            for i, (b, wi) in enumerate(((6, w), (7, 2 * T))):
                act.wait_ge(s.c_ms, 2 * l + i + 1)
                act.activation(tmp3[:, i, 0:wi], bank[b][:, 0:wi], ACT.Ln, bias=eps_col)
                act.drain()
                last = act.activation(tmp3[:, i, 0:wi], tmp3[:, i, 0:wi], ACT.Exp, scale=-0.5)
            last.then_inc(s.c_rs, 1)
            fourier_act(act, l)
            act.wait_ge(s.ln_cen, l + 1)
            act.activation(q2[:, 0:3, 0:w], cvo[:, 0:3, 0:w], ACT.Square).then_inc(s.ln_sq, 1)
            act.wait_ge(s.ln_ms, 2 * l + 2)
            act.activation(lnb2[:, 0:w], bank[5][:, 0:w], ACT.Ln, bias=eps_col)
            act.drain()
            act.activation(rstd2[:, 0:w], lnb2[:, 0:w], ACT.Exp, scale=-0.5).then_inc(s.ln_rs, 1)
            lin = PLAN["uq", l]
            for g in turns(act, lin):
                wait_products(act, lin, g)
                act.activation(q2[:, g.m, 0:w], bank[2 * parity(lin, g)][:, 0:w],
                               ACT.Copy).then_inc(drained[parity(lin, g)], 1)
            act.wait_ge(s.ln_n, l + 1)
            for k in range(CT):
                last = act.activation(cvo[:, k, 0:w], cvo[:, k, 0:w], ACT.Silu, bias=param(f"lnb@@{l}")[:, k:k + 1])
            last.then_inc(s.ln_out, 1)
            lin = PLAN["uv", l]
            for g in turns(act, lin):
                wait_products(act, lin, g)
                for tt in range(4):
                    act.activation(v2[:, tt, :], bank[4 + tt][:, :], ACT.Copy).then_inc(s.v_done, 1)
            units = units_block2(l)
            for i in range(len(units) + 2):
                between_units(branch_act, act, l, i - 1)
                if i < len(units):
                    latent_exp(act, units[i])
                if 1 <= i <= len(units):
                    latent_copy(act, units[i - 1])
                if i >= 2:
                    latent_out(act, units[i - 2])
            for g in turns(act, PLAN["mrg_mla", l]):
                branch_act(act, l, 2, g)
            ffn_act(act, l, 2)

        def block2_dve(dve, l):
            w = seqs(l) * T
            if l == 0:
                dve.wait_ge(s.consts2, 32)
            dve.drain()
            mod = modulation(l)
            for i, name in enumerate(("g1", "gm", "g2")):
                dve.scalar_tensor_tensor(out=gs[:, i, :, :], in0=mod[:, SCALE[i], :, :], scalar=1.0,
                                         in1=param(f"{name}@@{l}").unsqueeze(2).broadcast_to([P, KT, 2]),
                                         op0=ALU.add, op1=ALU.mult)
            for i in (0, 2):
                dve.tensor_scalar(mod[:, GATE[i], :, :], mod[:, GATE[i], :, :], 0.5, None, ALU.mult)
            dve.drain()
            ffn_dve(dve, l, 0)
            gated_norm_dve(dve, l, 1)
            lin = PLAN["conv_in", l]
            dve.wait_ge(s.padded, 1)
            for g in turns(dve, lin):
                wait_products(dve, lin, g)
                dve.wait_ge(s.cv_in, CT * l + g.m + 1)
                dve.tensor_tensor(cvp[:, g.m, 0:seqs(l), PAD:PAD + T], both(bank[2 * parity(lin, g)], w),
                                  both(tmp2[:, parity(lin, g), :], w), ALU.mult).then_inc(drained[parity(lin, g)], 1)
            taps = param(f"dw@@{l}").rearrange("p (m k) -> p m k", k=CONV_K)
            dve.drain()
            for k in range(CONV_K):
                for m in range(CT):
                    src = cvp[:, m, 0:seqs(l), k:k + T]
                    dst = both(cvo[:, m, :], w)
                    if k == 0:
                        last = dve.tensor_scalar(dst, src, taps[:, m, 0:1], param(f"bdw@@{l}")[:, m:m + 1],
                                                 ALU.mult, ALU.add)
                    else:
                        last = dve.scalar_tensor_tensor(out=dst, in0=src, scalar=taps[:, m, k:k + 1], in1=dst,
                                                        op0=ALU.mult, op1=ALU.add)
                if k < CONV_K - 1:
                    dve.drain()
            last.then_inc(s.cv_done, 1)
            dve.wait_ge(s.c_rs, l + 1)
            for k in range(3):
                dve.scalar_tensor_tensor(out=z[:, 3 + k, 0:w], in0=z[:, 3 + k, 0:w], scalar=param(f"gq@@{l}")[:, k:k + 1],
                                         in1=tmp3[:, 0, 0:w], op0=ALU.mult, op1=ALU.mult)
            for k in range(2):
                last = dve.scalar_tensor_tensor(out=z[:, k, :], in0=z[:, k, :], scalar=param(f"gkv@@{l}")[:, k:k + 1],
                                                in1=tmp3[:, 1, :], op0=ALU.mult, op1=ALU.mult)
            last.then_inc(s.c_n, 1)
            dve.wait_ge(s.ln_ms, 2 * l + 1)
            for k in range(CT):
                last = dve.tensor_tensor(cvo[:, k, 0:w], cvo[:, k, 0:w], bank[4][:, 0:w], ALU.subtract)
            last.then_inc(s.ln_cen, 1)
            dve.wait_ge(s.kr_rot, l + 1)
            mcos, msin = const(2, "mcos"), const(2, "msin")
            dve.tensor_tensor(tmp3[:, 0, 0:T], bank[6][:, 0:T], msin, ALU.mult)
            dve.tensor_tensor(z[:, 2, 0:T], z[:, 2, 0:T], mcos, ALU.mult)
            dve.drain()
            dve.tensor_tensor(z[:, 2, 0:T], z[:, 2, 0:T], tmp3[:, 0, 0:T], ALU.add).then_inc(s.kr_done, 1)
            dve.wait_ge(s.ln_rs, l + 1)
            for k in range(CT):
                last = dve.scalar_tensor_tensor(out=cvo[:, k, 0:w], in0=cvo[:, k, 0:w],
                                                scalar=param(f"lng@@{l}")[:, k:k + 1], in1=rstd2[:, 0:w],
                                                op0=ALU.mult, op1=ALU.mult)
            last.then_inc(s.ln_n, 1)
            dve.drain()
            lin = PLAN["uk", l]
            for g in turns(dve, lin):
                wait_products(dve, lin, g)
                dve.tensor_tensor(k2[:, g.m, :], bank[2 * parity(lin, g)][:, :], z[:, 2, :],
                                  ALU.add).then_inc(drained[parity(lin, g)], 1)
            for u in range(4):
                dve.wait_ge(s.q_rot, 4 * l + u + 1)
                dst = q2[:, 2 * u:2 * u + 2, 0:T]
                b = both(bank[4 + u % 2], 2 * T)
                t3 = both(tmp3[:, 0, :], 2 * T)
                dve.tensor_tensor(dst, dst, mcos.unsqueeze(1).broadcast_to([P, 2, T]), ALU.mult)
                dve.tensor_tensor(t3, b, msin.unsqueeze(1).broadcast_to([P, 2, T]), ALU.mult)
                dve.drain()
                dve.tensor_tensor(dst, dst, t3, ALU.add).then_inc(s.q_done, 1)
                dve.drain()
            units = units_block2(l)
            for i in range(len(units) + 2):
                between_units(branch_dve, dve, l, i - 1)
                if i < len(units):
                    latent_max(dve, units[i])
                if 1 <= i <= len(units):
                    latent_norm(dve, units[i - 1])
            for g in turns(dve, PLAN["mrg_mla", l]):
                branch_dve(dve, l, 2, g)
            gated_add(dve, l, PLAN["mix_out", l], 1, w)
            ffn_dve(dve, l, 2)

        def pad_pool(pool):
            wait_all_drained(pool, PLAN["down", DEPTH - 1])
            pool.memset(cvp_b, 0.0).then_inc(s.padded, 1)

        block = stack.enter_context(nc.Block())

        @block.sync
        def _(sp):
            for seg in SEGMENTS:
                if seg.chunk >= limit:
                    break
                n_pat = len(seg.pattern)
                per = SLOTS // n_pat
                times = min(seg.times, (limit - seg.chunk) // n_pat)

                def load(k, at, i):
                    for c, w in enumerate(seg.pattern):
                        chunk = seg.chunk + at * n_pat + c
                        slot, turn = chunk % SLOTS, chunk // SLOTS + i
                        if not (isinstance(turn, int) and turn == 0):
                            sp.wait_ge(used[slot], turn)
                        sp.dma_start(ring[:, slot, 0:w * P], streams[w][seg.at.get(w, 0) + k]).then_inc(landed[slot], 16)

                first = per if seg.chunk < SLOTS else 0
                for k in range(min(first, times)):
                    load(k, k, 0)
                end = times // per
                if end - first // per >= 2:
                    with sp.Fori(first // per, end) as i:
                        for j in range(per):
                            load(i * per + j, j, i)
                    rest = end * per
                else:
                    rest = first
                for k in range(rest, times):
                    load(k, k, 0)
            sp.wait_ge(s.final, KT)
            sp.dma_start(out_cm, hn[:, :, 0:T]).then_inc(s.stored, 16)
            sp.wait_ge(s.stored, 16)

        @block.tensor
        def _(pe):
            pe.wait_ge(s.consts, 64)
            pe.wait_ge(s.csilu, 1)
            for l in range(DEPTH):
                block1_pe(pe, l)
            if 2 in blocks:
                for l in range(DEPTH):
                    block2_pe(pe, l)
                norm_pe(pe, LAST_NORM)

        @block.scalar
        def _(act):
            act.dma_start(res[:, :, 0:T], x_cm).then_inc(s.x_in, 16)
            act.dma_start(con0[:, :], consts[0]).then_inc(s.consts, 16)
            act.dma_start(con12[:, 0:CONST_SETS[1][1]], consts[1]).then_inc(s.consts, 16)
            act.dma_start(par0[:, :], params[0]).then_inc(s.consts, 16)
            act.dma_start(par12[:, 0:PARAM_SETS[1][1]], params[1]).then_inc(s.consts, 16)
            act.dma_start(res[:, :, T:2 * T], ctx_cm).then_inc(s.ctx_in, 16)
            act.wait_ge(s.consts, 64)
            act.activation(conds[:, :], param("cvec"), ACT.Silu).then_inc(s.csilu, 1)
            act.wait_ge(s.lb, 1)
            act.activation(lb, lb, ACT.Exp).then_inc(s.lb, 1)
            for l in range(DEPTH):
                block1_act(act, l)
            if 2 in blocks:
                act.wait_ge(s.squares, 2 * DEPTH * KT)
                act.wait_ge(s.mixa, DEPTH)
                act.dma_start(con12[:, 0:CONST_SETS[2][1]], consts[2]).then_inc(s.consts2, 16)
                act.dma_start(par12[:, 0:PARAM_SETS[2][1]], params[2]).then_inc(s.consts2, 16)
                for l in range(DEPTH):
                    block2_act(act, l)
                norm_act(act, LAST_NORM)
            else:
                act.wait_ge(s.ctx_in, 16)

        @block.vector
        def _(dve):
            dve.memset(eps_col, EPS)
            dve.memset(one_col, 1.0)
            dve.wait_ge(s.consts, 64)
            a, b = param("lb")[:, 0:2], param("lb")[:, 2:4]
            dve.tensor_tensor(lb_u[:, 0:2], a, b, ALU.max)
            dve.drain()
            dve.tensor_tensor(lb[:, 0:2], a, lb_u[:, 0:2], ALU.subtract)
            dve.tensor_tensor(lb[:, 2:4], b, lb_u[:, 0:2], ALU.subtract).then_inc(s.lb, 1)
            dve.wait_ge(s.lb, 2)
            dve.tensor_tensor(lb_u[:, 0:2], lb[:, 0:2], lb[:, 2:4], ALU.add)
            dve.drain()
            dve.reciprocal(lb_u[:, 2:4], lb_u[:, 0:2])
            dve.drain()
            dve.tensor_tensor(lb[:, 0:2], lb[:, 0:2], lb_u[:, 2:4], ALU.mult)
            dve.tensor_tensor(lb[:, 2:4], lb[:, 2:4], lb_u[:, 2:4], ALU.mult)
            dve.drain()
            dve.tensor_tensor(lb_t[:, 0:2], lb[:, 0:2], lb[:, 0:2], ALU.subtract)
            dve.tensor_tensor(lb_t[:, 2:4], lb[:, 0:2], lb[:, 2:4], ALU.add)
            dve.drain()
            dve.tensor_tensor(lb_t[:, 2:4], lb_t[:, 2:4], lb[:, 0:2], ALU.subtract)
            dve.drain()
            dve.tensor_scalar(lb_u[:, 0:4], lb_t[:, 0:4], -1.0, 1.0, ALU.mult, ALU.add)
            dve.drain()
            for l in range(DEPTH):
                block1_dve(dve, l)
            if 2 in blocks:
                for l in range(DEPTH):
                    block2_dve(dve, l)
                dve.wait_ge(s.rstd, LAST_NORM + 1)
                for k in range(KT):
                    dve.scalar_tensor_tensor(out=hn[:, k, 0:T], in0=res[:, k, 0:T], scalar=param("gfin")[:, k:k + 1],
                                             in1=rstd[:, 0:T], op0=ALU.mult, op1=ALU.mult).then_inc(s.final, 1)
            else:
                dve.drain()
                for k in range(KT):
                    dve.tensor_copy(hn[:, k, 0:T], res[:, k, 0:T]).then_inc(s.final, 1)

        @block.gpsimd
        def _(pool):
            pool.memset(bc_b, 0.0).then_inc(s.cleared, 1)
            pool.wait_ge(s.cleared, 1)
            pool.wait_ge(s.consts, 64)
            for l in range(DEPTH):
                block1_pool(pool, l)
            if 2 in blocks:
                pad_pool(pool)


def kernel(**inputs):
    import numpy as _np
    import concourse.bacc as _bacc
    from concourse import mybir as _mybir
    from concourse.bass_utils import run_bass_kernel_spmd as _run

    a = {name: _np.asarray(v) for name, v in inputs.items()}
    nc = _bacc.Bacc("TRN2", target_bir_lowering=False, num_devices=1)
    arrays = {}

    def given(name, v):
        arrays[name] = _np.ascontiguousarray(v)
        return nc.dram_tensor(name, v.shape, _mybir.dt.from_np(v.dtype), kind="ExternalInput").ap()

    streams = {w: given(f"weights_{w}", v) for w, v in pack_stream(a).items()}
    consts = [given(f"consts_{k}", v) for k, v in enumerate(shape_constants())]
    params = [given(f"params_{k}", v) for k, v in enumerate(pack_params(a))]
    x_cm = given("x_cm", channel_major(a["x"][0]))
    ctx_cm = given("ctx_cm", channel_major(a["ctx_2"][0]))
    out_cm = nc.dram_tensor("out_cm", (P, KT, T), F32, kind="ExternalOutput").ap()
    kernel_program(nc, streams, consts, params, x_cm, ctx_cm, out_cm)
    out = _run(nc, [arrays], core_ids=[0]).results[0]["out_cm"]
    return out.transpose(1, 0, 2).reshape(D, T).T.reshape(1, T, D)
```

```python
from contextlib import ExitStack

import numpy as np

import concourse.bass as bass
from concourse import mybir

F32 = mybir.dt.float32
U32 = mybir.dt.uint32
F32R = mybir.dt.float32r
ALU = mybir.AluOpType
ACT = mybir.ActivationFunctionType
AX_X = mybir.AxisListType.X

P = 128
D = 1024
KT = D // P
T = 256
TT = T // P
DEPTH = 2
EPS = 1e-6
NEG_BIG = -1e30
TINY = 1e-30
DH = 64
LN_SPLIT = 2.0 ** 60

N_CMP = 15
CMP_L = 32
HG_CHUNK = 64
HG_LEVELS = (32, 16, 8, 4, 2, 1)

FF1 = 4 * D // P
FF2 = 22
CONV_K = 31
PAD = CONV_K // 2
TP = T + 2 * PAD
CT = 3
QH = 8
NOPE = 64
ROPE = 32
QK = NOPE + ROPE
ATTN_SCALE = float(QK) ** -0.5
G4 = 4


class Product:

    def __init__(self, chunk, group, n, tiles, split, split0):
        self.chunk, self.group, self.n, self.tiles, self.cpg = chunk, group, n, tiles, len(tiles)
        self.split, self.split0 = split, split0


class Segment:

    def __init__(self, pattern, chunk, times, at):
        self.pattern, self.chunk, self.times, self.at = pattern, chunk, times, at


class Group:

    def __init__(self, m, at, i, per):
        self.m, self.at, self.i, self.per = m, at, i, per


class Unit:

    def __init__(self, kind, tt, h=0, g=0, hh=0, tile0=0, first=True, last=True):
        self.kind, self.tt, self.h, self.g, self.hh, self.tile0 = kind, tt, h, g, hh, tile0
        self.first, self.last, self.lo = first, last, hh * DH


SLOTS = 4
SLOT_TILES = 8


def stream_plan():
    plan, chunk, group, split0 = {}, 0, 0, 0
    order = []
    for l in range(DEPTH):
        order += [("in_t", l, 18, (8,), ()), ("in_a", l, 7, (8,), ()), ("cmp", l, 2, (8,) * 4, ()),
                  ("ada", l, 72, (8,), ()), ("wo", l, 8, (8,), ()),
                  ("up", l, FF1, (8,), ()), ("down", l, 8, (8,) * 4, ())]
    for l in range(DEPTH):
        order += [("ffn1", l, FF2, (8, 8), (0, 1)), ("ffn1_out", l, 8, (8, 8, 6), (1,)),
                  ("conv_in", l, CT, (8, 8), (0, 1)), ("lat_in", l, 10, (8,), (0,)),
                  ("uq", l, QH, (3,), ()), ("uk", l, QH, (2,), ()), ("uv", l, 1, (8,), ()),
                  ("mrg_conv", l, 8, (3, 8), (1,)), ("mrg_four", l, 8, (4, 8), (1,)), ("mrg_mla", l, 8, (4, 8), (1,)),
                  ("mix_out", l, 8, (8,), ()), ("ffn2", l, FF2, (8, 8), (0, 1) if l < DEPTH - 1 else ()),
                  ("ffn2_out", l, 8, (8, 8, 6), (1,) if l < DEPTH - 1 else ())]
    for name, l, n, tiles, split in order:
        plan[name, l] = Product(chunk, group, n, tiles, split, split0)
        chunk += n * len(tiles)
        split0 += n * len(split)
        if name not in ("ada", "uv"):
            group += n
    return plan


PLAN = stream_plan()


def period(chunks):
    return next(n for n in range(2, 2 * SLOTS + 1, 2) if n * chunks % SLOTS == 0)


def segments():
    out, seen, pos = [], {}, 0
    for lin in PLAN.values():
        pattern = lin.tiles if len(set(lin.tiles)) > 1 else lin.tiles[:1]
        times = lin.n * lin.cpg // len(pattern)
        if out and out[-1].pattern == pattern:
            out[-1].times += times
        else:
            out.append(Segment(pattern, pos, times, dict(seen)))
        for w in pattern:
            seen[w] = seen.get(w, 0) + times
        pos += times * len(pattern)
    return out, seen


SEGMENTS, WIDTHS = segments()

CONST_ALL = [("ident", P), ("ones_d", P)]
CONST_1 = [("blk64", P), ("rot", P), ("dup", 2 * P), ("rotdup", 2 * P), ("cos", T), ("sin", T),
           ("ccos", 2 * N_CMP), ("csin", 2 * N_CMP), ("causal", TT * T), ("cmask", TT * 2 * N_CMP),
           ("cneg", TT * 2 * N_CMP), ("tri", TT * T), ("gtk", TT * T), ("reset", 2 * T), ("lvl", 8 * P)]
CONST_2 = [("ones_ct", P), ("ones_kv", P), ("rot96", P), ("dft_c", 2 * P), ("dft_t", TT * 2 * T), ("mcos", T),
           ("msin", T)]


def columns(items):
    at, out = 0, {}
    for name, n in items:
        out[name] = (at, n)
        at += n
    return out, at


CONST_SETS = [columns(c) for c in (CONST_ALL, CONST_1, CONST_2)]
PARAM_L1 = [("norm1", 8), ("norm2", 8), ("onorm", 1), ("qkg", 10), ("pos", 2 * CMP_L), ("w2k", P), ("w2v", DH),
            ("kng", 1), ("fb", 4)]
PARAM_L2 = [("g1", 8), ("gm", 8), ("g2", 8), ("dw", CT * CONV_K), ("bdw", CT), ("lng", CT), ("lnb", CT),
            ("bpw", 8), ("gq", 3), ("gkv", 2), ("bfour", 8), ("bbg", 24)]
PARAM_ALL = [("lb", 4), ("cvec", 16), ("gfin", 8), ("bada", 72 * DEPTH)]
PARAM_SETS = [columns(PARAM_ALL), columns([(f"{n}@{l}", c) for l in range(DEPTH) for n, c in PARAM_L1]),
              columns([(f"{n}@@{l}", c) for l in range(DEPTH) for n, c in PARAM_L2])]


def shape_constants():
    c = {}
    i = np.arange(P)
    eye = np.eye(P)
    c["ident"] = eye
    c["ones_d"] = np.full((P, P), 1.0 / D)
    c["ones_ct"] = np.full((P, P), 1.0 / (CT * P))
    c["ones_kv"] = np.full((P, P), 1.0 / 256)
    c["blk64"] = (i[:, None] // DH == i[None, :] // DH) / float(DH)
    rot = np.zeros((P, P))
    for b in (0, DH):
        for d in range(8):
            rot[b + 8 + d, b + d] = -1.0
            rot[b + d, b + 8 + d] = 1.0
    c["rot"] = rot
    dup = np.zeros((P, 2, P))
    for g in range(2):
        for h in range(2):
            dup[g * DH + np.arange(DH), g, h * DH + np.arange(DH)] = 1.0
    c["dup"] = dup
    c["rotdup"] = np.stack([rot @ dup[:, g] for g in range(2)], 1)
    inv = np.float32(500000.0) ** (-np.arange(0, 16, 2, dtype=np.float32) / np.float32(16))

    def rope(pos):
        ang = (pos.astype(np.float32)[None, :] * inv[:, None]).astype(np.float32)
        cs, sn = np.ones((P, len(pos))), np.zeros((P, len(pos)))
        for b in (0, 8, DH, DH + 8):
            cs[b:b + 8], sn[b:b + 8] = np.cos(ang), np.sin(ang)
        return cs, sn

    c["cos"], c["sin"] = rope(np.arange(T))
    cc, cs = rope(np.arange(N_CMP) * 16 + 31)
    c["ccos"], c["csin"] = np.tile(cc, (1, 2)), np.tile(cs, (1, 2))
    q = np.arange(T).reshape(TT, P)
    k = np.arange(T)
    c["causal"] = np.where(k[None, None] <= q.T[:, :, None], 0.0, NEG_BIG)
    end = np.arange(N_CMP) * 16 + 31
    seen = (end[None, None] <= q.T[:, :, None])
    c["cmask"] = np.tile(seen[:, :, None, :], (1, 1, 2, 1)).astype(float)
    c["cneg"] = np.where(np.tile(seen[:, :, None, :], (1, 1, 2, 1)), 0.0, NEG_BIG)
    c["tri"] = (q.T[:, :, None] <= k[None, None]).astype(float)
    c["gtk"] = (q.T[:, :, None] > k[None, None]).astype(float)
    c["reset"] = np.tile((np.arange(2 * T) % HG_CHUNK != 0).astype(float), (P, 1))
    lv = np.zeros((P, 8, P))
    for n, L in enumerate(HG_LEVELS + (64,)):
        s, t = i[:, None], i[None, :]
        lv[:, n] = (s // (2 * L) == t // (2 * L)) & (s // L % 2 == 0) & (t // L % 2 == 1)
    lv[:, 7] = eye
    c["lvl"] = lv
    a = 2 * np.pi * np.outer(i, i) / P
    c["dft_c"] = np.concatenate([np.cos(a), np.sin(a)], 1)
    a = 2 * np.pi * np.outer(k, k) % (2 * np.pi * T) / T
    n = 1.0 / np.sqrt(float(T * P))
    a = np.stack([np.cos(a) * n, -np.sin(a) * n], 1).reshape(TT, P, 2, T)
    c["dft_t"] = a.transpose(1, 0, 2, 3)
    r96 = np.zeros((P, P))
    for ax in (NOPE, NOPE + 16):
        for d in range(8):
            r96[ax + 8 + d, ax + d] = -1.0
            r96[ax + d, ax + 8 + d] = 1.0
    c["rot96"] = r96
    inv = 1.0 / (np.float32(10000.0) ** (np.arange(8, dtype=np.float32) * 2.0 / 16))
    row, col = np.repeat(np.arange(T // 64), 64), np.tile(np.arange(64), T // 64)
    ang = np.concatenate([row[None] * inv[:, None]] * 2 + [col[None] * inv[:, None]] * 2, 0).astype(np.float32)
    mc, ms = np.ones((P, T)), np.zeros((P, T))
    mc[NOPE:QK], ms[NOPE:QK] = np.cos(ang), np.sin(ang)
    c["mcos"], c["msin"] = mc, ms
    packed = []
    for at_of, width in CONST_SETS:
        out = np.zeros((P, width), np.float32)
        for name, (at, n) in at_of.items():
            out[:, at:at + n] = c[name].reshape(P, n)
        packed.append(out)
    return packed


def chan(v):
    return v.reshape(-1, P).T


def pack_params(a):
    rows = {}

    def rep(v):
        return np.tile(v.reshape(1, -1), (P, 1))

    lb = a["hgrn_lb_logits"]
    rows["lb"] = np.concatenate([chan(lb[0]), chan(lb[1])], 1)
    rows["cvec"] = np.stack([chan(a["c_2"][0]), chan(a["c_ctx_2"])], 2)
    rows["bada"] = np.concatenate([chan(a["b_ada_2"][l]) for l in range(DEPTH)], 1)
    rows["gfin"] = chan(a["g_final_2"])
    for l in range(DEPTH):
        twice = lambda v: np.tile(v.reshape(-1, 1), (2, 1))
        qn, kn = twice(a["nsa_qn_g"][l]), twice(a["nsa_kn_g"][l])
        fq, fk = twice(a["fox_qn_g"][l]), twice(a["fox_kn_g"][l])
        r = {"norm1": chan(a["norm1_g"][l]), "norm2": chan(a["norm2_g"][l]), "onorm": twice(a["hgrn_onorm_g"][l]),
             "qkg": np.concatenate([kn, kn, qn, qn, qn, qn, fq, fq, fk, fk], 1),
             "pos": np.tile(a["nsa_cmp_pos"][l].transpose(2, 0, 1).reshape(DH, -1), (2, 1)),
             "w2k": np.concatenate([a["nsa_cmp_w2"][l, 0]] * 2, 1), "w2v": a["nsa_cmp_w2"][l, 1],
             "kng": kn, "fb": rep(a["fox_fb"][l])}
        rows.update({f"{n}@{l}": v for n, v in r.items()})
        r = {"g1": chan(a["g_ffn1_2"][l]), "gm": chan(a["g_mix_2"][l]),
             "g2": chan(a["g_ffn2_2"][l]),
             "dw": a["w_dw_2"][l].T.reshape(CT, P, CONV_K).transpose(1, 0, 2),
             "bdw": chan(a["b_dw_2"][l]), "lng": chan(a["ln_g_conv_2"][l]), "lnb": chan(a["ln_b_conv_2"][l]),
             "bpw": chan(a["b_pw_conv_2"][l]), "gq": chan(a["g_qnorm_2"][l]), "gkv": chan(a["g_kvnorm_2"][l]),
             "bfour": chan(a["b_fourier_2"][l]), "bbg": chan(a["b_bgate_2"][l])}
        rows.update({f"{n}@@{l}": v for n, v in r.items()})
    packed = []
    for at_of, width in PARAM_SETS:
        out = np.zeros((P, width), np.float32)
        for name, (at, n) in at_of.items():
            out[:, at:at + n] = rows[name].reshape(P, n)
        packed.append(out)
    return packed


def tiles(w):
    k, n = w.shape
    m = -(-n // P)
    if n % P:
        w = np.concatenate([w, np.zeros((k, m * P - n), w.dtype)], 1)
    return w.reshape(k // P, P, m, P).transpose(2, 1, 0, 3)


def place(w, at):
    out = np.zeros((w.shape[0], P), w.dtype)
    out[:, at:at + w.shape[1]] = w
    return out


def pack_stream(a):
    out = {w: [] for w in WIDTHS}

    def put(t):
        t = np.ascontiguousarray(t)
        out[t.shape[1]].append(t.reshape(P, -1))

    def halves(t, w):
        for m in range(t.shape[0]):
            for c in range(0, t.shape[2], w):
                put(t[m][:, c:c + w])

    for l in range(DEPTH):
        w = a["w_in"][l]
        for lo, hi in ((256, 512), (0, 256), (1792, 1920), (2048, 2176), (1024, 1536), (2328, 2840),
                       (1536, 1792), (768, 1024)):
            halves(tiles(w[:, lo:hi]), 8)
        halves(tiles(np.concatenate([w[:, 2304:2328], w[:, 3096:3100]], 1)), 8)
        for lo, hi in ((512, 768), (1920, 2048), (2176, 2304), (2840, 3096)):
            halves(tiles(w[:, lo:hi]), 8)
        for which in range(2):
            t = a["nsa_cmp_w1"][l, which].reshape(CMP_L, DH, P).transpose(1, 0, 2)
            t = np.concatenate([t, t], 0)
            for c in range(4):
                put(t[:, 8 * c:8 * c + 8])
        halves(tiles(a["w_ada_2"][l]), 8)
        halves(tiles(a["w_o"][l]), 8)
        halves(tiles(a["w_up"][l]), 8)
        halves(tiles(a["w_down"][l]), 8)

    def pairs(x, y):
        for m in range(x.shape[0]):
            put(x[m])
            put(y[m])

    for l in range(DEPTH):
        pairs(tiles(a["w1_ffn1_2"][l]), tiles(a["w3_ffn1_2"][l]))
        halves(tiles(a["w2_ffn1_2"][l]), 8)
        w = a["w_in_2"][l]
        pairs(tiles(w[:, 0:384]), tiles(w[:, 384:768]))
        halves(tiles(w[:, 1152:1408]), 8)
        halves(tiles(place(w[:, 1408:1440], NOPE)), 8)
        halves(tiles(w[:, 768:1152]), 8)
        halves(tiles(w[:, 1440:1952]), 8)
        uq = a["w_uq_2"][l].reshape(384, QH, QK)
        ukv = a["w_ukv_2"][l].reshape(256, QH, NOPE + 64)
        for h in range(QH):
            halves(tiles(place(uq[:, h], 0)), 3)
        for h in range(QH):
            halves(tiles(place(ukv[:, h, :NOPE], 0)), 2)
        v = ukv[:, :, NOPE:].reshape(2, P, 4, P).transpose(1, 0, 2, 3)
        put(v.reshape(P, 8, P))
        gate = tiles(a["w_bgate_2"][l])
        pw, four, om = (tiles(a[n][l]) for n in ("w_pw_conv_2", "w_fourier_2", "w_o_mla_2"))
        pairs(pw, gate[0:8])
        pairs(four, gate[16:24])
        pairs(om, gate[8:16])
        halves(tiles(a["w_out_2"][l]), 8)
        pairs(tiles(a["w1_ffn2_2"][l]), tiles(a["w3_ffn2_2"][l]))
        halves(tiles(a["w2_ffn2_2"][l]), 8)
    return {w: np.stack(c) for w, c in out.items()}


def channel_major(x):
    return np.ascontiguousarray(x.T.reshape(-1, P, x.shape[0]).transpose(1, 0, 2))


class Semaphores:

    def __init__(self, sem):
        self.consts = sem("consts")
        self.consts2 = sem("consts2")
        self.x_in = sem("x_in")
        self.ctx_in = sem("ctx_in")
        self.squares = sem("squares")
        self.mean_sq = sem("mean_sq")
        self.rstd = sem("rstd")
        self.normed = sem("normed")
        self.hn_sq = sem("hn_sq")
        self.hn_ms = sem("hn_ms")
        self.hn_ln = sem("hn_ln")
        self.hn_rs = sem("hn_rs")
        self.qkn = sem("qkn")
        self.rotated = sem("rotated")
        self.rope = sem("rope")
        self.sig = sem("sig")
        self.lb = sem("lb")
        self.fa = sem("fa")
        self.fox_in = sem("fox_in")
        self.fox_e = sem("fox_e")
        self.hg_f = sem("hg_f")
        self.hg_ln = sem("hg_ln")
        self.hg_g = sem("hg_g")
        self.hg_e = sem("hg_e")
        self.hg_qk = sem("hg_qk")
        self.hg_x = sem("hg_x")
        self.hg_sc = sem("hg_sc")
        self.hg_o = sem("hg_o")
        self.hg_osq = sem("hg_osq")
        self.hg_oms = sem("hg_oms")
        self.hg_ors = sem("hg_ors")
        self.mixa = sem("mixa")
        self.zeroed = sem("zeroed")
        self.cleared = sem("cleared")
        self.blocks = sem("blocks")
        self.cmp_raw = sem("cmp_raw")
        self.kc_sq = sem("kc_sq")
        self.kc_ms = sem("kc_ms")
        self.kc_rs = sem("kc_rs")
        self.kc_n = sem("kc_n")
        self.kc_rot = sem("kc_rot")
        self.kc_done = sem("kc_done")
        self.vc_done = sem("vc_done")
        self.att_s = sem("att_s")
        self.att_m = sem("att_m")
        self.att_e = sem("att_e")
        self.att_p = sem("att_p")
        self.att_t = sem("att_t")
        self.att_c = sem("att_c")
        self.att_v = sem("att_v")
        self.att_o = sem("att_o")
        self.stored = sem("stored")
        self.csilu = sem("csilu")
        self.cv_in = sem("cv_in")
        self.cv_done = sem("cv_done")
        self.ln_ms = sem("ln_ms")
        self.ln_cen = sem("ln_cen")
        self.ln_sq = sem("ln_sq")
        self.ln_rs = sem("ln_rs")
        self.ln_n = sem("ln_n")
        self.ln_out = sem("ln_out")
        self.c_sq = sem("c_sq")
        self.c_ms = sem("c_ms")
        self.c_rs = sem("c_rs")
        self.c_n = sem("c_n")
        self.q_rot = sem("q_rot")
        self.q_done = sem("q_done")
        self.kr_rot = sem("kr_rot")
        self.kr_done = sem("kr_done")
        self.v_done = sem("v_done")
        self.f_mm = sem("f_mm")
        self.f_sb = sem("f_sb")
        self.sig_g = sem("sig_g")
        self.silu = sem("silu")
        self.padded = sem("padded")
        self.final = sem("final")
        self.ada_row = sem("ada_row")
        self.ada_t = sem("ada_t")
        self.ada_out = sem("ada_out")
        self.w_hi = sem("w_hi")
        self.w_lo = sem("w_lo")
        self.lo_used = sem("lo_used")
        self.norm_value = sem("norm_value")
        self.norm_hi = sem("norm_hi")
        self.hid_hi = sem("hid_hi")
        self.hid_lo = sem("hid_lo")
        self.split_normed = sem("split_normed")
        self.consts1 = sem("consts1")


def kernel_program(nc, streams, consts, params, x_cm, ctx_cm, out_cm, blocks=(1, 2)):
    with ExitStack() as stack:
        free = [-(-nc.sbuf_base // 32) * 32]

        def sb(name, shape, dt=F32):
            at = free[0]
            free[0] += -(-4 * int(np.prod(shape[1:])) // 32) * 32
            assert free[0] <= nc.sbuf_usable_end, name
            return nc.alloc_sbuf_tensor_at(name, shape, dt, offset=at)

        def sem(name):
            return stack.enter_context(nc.semaphore(name))

        ring = sb("ring", [P, SLOTS, SLOT_TILES * P])
        w_hi = sb("w_hi", [P, 2, SLOT_TILES * P], F32R)
        w_lo = sb("w_lo", [P, 2, SLOT_TILES * P], F32R)
        res = sb("res", [P, KT, 2 * T])
        hn_hi = sb("hn_hi", [P, KT, 2 * T], F32R)
        hn_lo = sb("hn_lo", [P, KT, 2 * T], F32R)
        hid = sb("hid", [P, FF2 * 2 * T])
        work = sb("work", [P, 14336])
        con0 = sb("con0", [P, CONST_SETS[0][1]])
        con12 = sb("con12", [P, max(CONST_SETS[1][1], CONST_SETS[2][1])])
        par0 = sb("par0", [P, PARAM_SETS[0][1]])
        par12 = sb("par12", [P, max(PARAM_SETS[1][1], PARAM_SETS[2][1])])
        mods = sb("mods", [P, DEPTH, 2 * 72])
        conds = sb("conds", [P, 16])
        small = sb("small", [P, 404])
        hid1 = hid[:, 0:FF1 * T].rearrange("p (m t) -> p m t", t=T)
        hid2 = hid[:, :].rearrange("p (m t) -> p m t", t=2 * T)
        sq = work[:, 4096:8192].rearrange("p (m t) -> p m t", t=2 * T)
        bank = [stack.enter_context(nc.psum_tensor(f"bank{b}", [P, 512], F32)) for b in range(8)]

        def carve(buffer, sizes):
            at, out = 0, []
            for n in sizes:
                out.append(buffer[:, at:at + n])
                at += n
            return out

        def const(k, name, **dims):
            at, n = CONST_SETS[k][0][name]
            v = (con0 if k == 0 else con12)[:, at:at + n]
            return v

        def param(name):
            k = 2 if "@@" in name else 1 if "@" in name else 0
            at, n = PARAM_SETS[k][0][name]
            return (par12 if k else par0)[:, at:at + n]

        limit = sum(x.n * x.cpg for x in PLAN.values()) if 2 in blocks else PLAN["ffn1", 0].chunk
        ident, ones_d = const(0, "ident"), const(0, "ones_d")
        blk64, rot = const(1, "blk64"), const(1, "rot")
        dup = const(1, "dup").rearrange("p (g m) -> p g m", g=2)
        rotdup = const(1, "rotdup").rearrange("p (g m) -> p g m", g=2)
        cos, sin = const(1, "cos"), const(1, "sin")
        causal = const(1, "causal").rearrange("p (t k) -> p t k", t=TT)
        cmask = const(1, "cmask").rearrange("p (t k) -> p t k", t=TT)
        cneg = const(1, "cneg").rearrange("p (t k) -> p t k", t=TT)
        tri = const(1, "tri").rearrange("p (t k) -> p t k", t=TT)
        gtk = const(1, "gtk").rearrange("p (t k) -> p t k", t=TT)
        lvl_u = const(1, "lvl").bitcast(U32).rearrange("p (n t) -> p n t", n=8)
        dft_c = const(2, "dft_c")
        dft_t = const(2, "dft_t").rearrange("p (t c k) -> p t c k", t=TT, c=2)

        HT = 2 * T
        proj_b, qkn_b, sq_b, sc_b, sc2_b = carve(hid, [18 * T, 10 * T, 10 * T, 4 * T, 2 * T])
        proj = proj_b.rearrange("p (m t) -> p m t", t=T)
        qkn = qkn_b.rearrange("p (m t) -> p m t", t=T)
        sqh = sq_b.rearrange("p (m t) -> p m t", t=T)
        scores_hg = sc_b.rearrange("p (h b t) -> p h b t", h=2, b=4)
        scores_far = sc2_b.rearrange("p (h b t) -> p h b t", h=2, b=2)
        qr = sqh[:, 0:4, :]
        kd = sq_b[:, 4 * T:8 * T].rearrange("p (g s t) -> p g s t", g=2, s=2)
        (sm_b, pr_b, pt_b, rstd, lnb, fa_b, gg, ee, qk, q8, vtok_b, sg, kc, sga, mix_b, ada_row) = carve(
            work, [1024, 1024, 1024, 512, 512, 2048, 512, 512, 512, 512, 1792, 512, 512, 512, 2048, 512])
        sm = sm_b.rearrange("p (u k) -> p u k", u=2)
        pr = pr_b.rearrange("p (u k) -> p u k", u=2)
        pt = pt_b.rearrange("p (u k) -> p u k", u=2)
        vtok = vtok_b.rearrange("p (t c) -> p t c", t=TT)
        bc_b = work[:, 0:2 * CMP_L * 2 * N_CMP]
        bc = bc_b.rearrange("p (w l g n) -> p w l g n", w=2, l=CMP_L, g=2)
        fa = fa_b.rearrange("p (s h q) -> p s h q", s=TT, h=4)
        mixt = mix_b.rearrange("p (m t) -> p m t", t=T)
        (mx, negmx, smu, rcp, lb, lb_t, lb_u, gate_b, lf, lx, ly, lz, qkg, hk, hv, kcn, kcb, krot, vc_b, eps_col,
         one_col) = carve(small, [4, 4, 4, 4, 4, 4, 4, 48, 8, 8, 8, 8, 10, 30, 30, 30, 30, 30, 128, 1, 1])
        gate = gate_b.rearrange("p (t c) -> p t c", t=TT)
        vc = vc_b.rearrange("p (g d) -> p g d", g=2)

        tmp2 = sm_b.rearrange("p (u t) -> p u t", u=2)
        tmp3 = pr_b.rearrange("p (u t) -> p u t", u=2)

        z = hid[:, 0:10 * HT].rearrange("p (m t) -> p m t", t=HT)
        q2 = hid[:, 10 * HT:18 * HT].rearrange("p (h t) -> p h t", t=HT)
        cvo = hid[:, 18 * HT:21 * HT].rearrange("p (m t) -> p m t", t=HT)
        att = z[:, 0:4, :]
        four = z[:, 6:10, :]
        (sm2_b, pr2_b, pt2_b, rstd2, lnb2, k2_b, v2_b, f1_b) = carve(
            work, [1024, 1024, 1024, 512, 512, 4096, 2048, 4096])
        k2 = k2_b.rearrange("p (h t) -> p h t", t=HT)
        cvq = k2_b[:, 0:CT * HT].rearrange("p (m t) -> p m t", t=HT)
        v2 = v2_b.rearrange("p (t c) -> p t c", t=4)
        f1 = f1_b.rearrange("p (s t g c) -> p s t g c", s=2, t=TT, g=G4)
        mrg = f1_b.rearrange("p (m t) -> p m t", t=HT)
        sumsq = rstd
        cvp_b = v2_b[:, 0:CT * 2 * TP]
        cvp = cvp_b.rearrange("p (m s t) -> p m s t", m=CT, s=2)

        landed = [sem(f"landed{s}") for s in range(SLOTS)]
        used = [sem(f"used{s}") for s in range(SLOTS)]
        drained = [sem(f"drained{p}") for p in range(2)]
        s = Semaphores(sem)

        def turns(eng, lin, tail=0):
            per = period(lin.cpg)
            first = per if lin.chunk < SLOTS else 0
            end = (lin.n - tail) // per
            if end - first // per < 2:
                for m in range(lin.n):
                    yield Group(m, m, 0, per)
                return
            for m in range(first):
                yield Group(m, m, 0, per)
            with eng.Fori(first // per, end) as i:
                for j in range(per):
                    yield Group(i * per + j, j, i, per)
            for m in range(end * per, lin.n):
                yield Group(m, m, 0, per)

        def slot_of(lin, g, c):
            return (lin.chunk + g.at * lin.cpg + c) % SLOTS

        def turn_of(lin, g, c):
            return (lin.chunk + g.at * lin.cpg + c) // SLOTS + g.i * (g.per * lin.cpg // SLOTS)

        def wait_weights(pe, lin, g, c):
            pe.wait_ge(landed[slot_of(lin, g, c)], (turn_of(lin, g, c) + 1) * 16)

        def split_number(lin, g, j):
            return lin.split0 + g.at * len(lin.split) + j + g.i * (g.per * len(lin.split))

        def split_high(act, lin, g, j):
            n_split = len(lin.split)
            at = Group(g.m, g.at + j // n_split, g.i, g.per)
            c = lin.split[j % n_split]
            slot, number = slot_of(lin, at, c), split_number(lin, g, j)
            even = (lin.split0 + g.at * n_split + j) % 2
            wait_weights(act, lin, at, c)
            if not (isinstance(number, int) and number < 2):
                act.wait_ge(s.lo_used, number)
            w = lin.tiles[c] * P
            act.activation(w_hi[:, even, 0:w], ring[:, slot, 0:w], ACT.Copy).then_inc(s.w_hi, 1)

        def split_low(eng, lin, g, j):
            n_split = len(lin.split)
            at = Group(g.m, g.at + j // n_split, g.i, g.per)
            c = lin.split[j % n_split]
            slot = slot_of(lin, at, c)
            even = (lin.split0 + g.at * n_split + j) % 2
            number = split_number(lin, g, j)
            eng.wait_ge(s.w_hi, number + 1)
            w = lin.tiles[c] * P
            eng.tensor_tensor(w_lo[:, even, 0:w], ring[:, slot, 0:w], w_hi[:, even, 0:w].bitcast(F32),
                              ALU.subtract).then_inc(s.w_lo, 1)

        def first_split(split, eng, lin):
            split(eng, lin, Group(0, 0, 0, period(lin.cpg)), 0)

        def splits_ahead(split, eng, lin, g, following=None):
            n_split = len(lin.split)
            for j in range(1, n_split + 1):
                if not isinstance(g.m, int) or g.m * n_split + j < lin.n * n_split:
                    split(eng, lin, g, j)
            if following is not None and isinstance(g.m, int) and g.m == lin.n - 1:
                first_split(split, eng, following)

        def wait_split(pe, lin, g, c):
            pe.wait_ge(s.w_lo, split_number(lin, g, lin.split.index(c)) + 1)

        def split_product(pe, lin, g, c, dst, wait_part, w, start=True, stop=True):
            wait_split(pe, lin, g, c)
            number = lin.split0 + g.at * len(lin.split) + lin.split.index(c)
            n = lin.tiles[c]
            for k in range(n):
                if g.at == 0:
                    wait_part(0, k)
                mm = pe.matmul(dst, w_lo[:, number % 2, k * P:(k + 1) * P], hn_hi[:, k, 0:w],
                               start=(start and k == 0), stop=False)
            mm.then_inc(s.lo_used, 1)
            for k in range(n):
                high = w_hi[:, number % 2, k * P:(k + 1) * P]
                pe.matmul(dst, high, hn_hi[:, k, 0:w], start=False, stop=False)
                if g.at == 0:
                    wait_part(1, k)
                mm = pe.matmul(dst, high, hn_lo[:, k, 0:w], start=False, stop=(stop and k == n - 1))
            mm.then_inc(used[slot_of(lin, g, c)], 1)

        def parity(lin, g):
            return (lin.group + g.at) % 2

        def wait_banks(pe, lin, g):
            before = (lin.group + g.at) // 2 + g.i * (g.per // 2)
            if not (isinstance(before, int) and before == 0):
                pe.wait_ge(drained[parity(lin, g)], before)

        def wait_products(eng, lin, g):
            c = lin.cpg - 1
            eng.wait_ge(used[slot_of(lin, g, c)], turn_of(lin, g, c) + 1)

        def wait_drained(eng, lin, m):
            n = lin.group + m
            eng.wait_ge(drained[n % 2], n // 2 + 1)

        def wait_all_drained(eng, lin):
            for m in range(max(lin.n - 2, 0), lin.n):
                wait_drained(eng, lin, m)

        cs = conds[:, :].rearrange("p (k c) -> p k c", c=2)
        ADA_QUADS = 72 // 4

        def modulation(l):
            return mods[:, l, :].rearrange("p (n k c) -> p n k c", n=9, k=8)

        def ada_bank(l, q):
            return bank[1 + 2 * ((ADA_QUADS * l + q) % 2)]

        def ada_pe(pe, l, step):
            lin = PLAN["ada", l]
            for m in range(2 * step, min(2 * step + 2, lin.n)):
                g, q = Group(m, m, 0, lin.n), m // 4
                if m % 4 == 0 and ADA_QUADS * l + q >= 2:
                    pe.wait_ge(s.ada_out, ADA_QUADS * l + q - 1)
                wait_weights(pe, lin, g, 0)
                for k in range(KT):
                    mm = pe.matmul(ada_bank(l, q)[0:2, (m % 4) * P:(m % 4 + 1) * P], cs[:, k, :],
                                   ring[:, slot_of(lin, g, 0), k * P:(k + 1) * P], start=(k == 0), stop=(k == KT - 1))
                mm.then_inc(used[slot_of(lin, g, 0)], 1)
            q = (step - 3) // 2
            if step % 2 == 1 and 0 <= q < ADA_QUADS:
                pe.wait_ge(s.ada_row, ADA_QUADS * l + q + 1)
                for j in range(4):
                    mm = pe.transpose(ada_bank(l, q)[:, 2 * j:2 * j + 2], ada_row[0:2, j * P:(j + 1) * P], ident[0:2, 0:2])
                mm.then_inc(s.ada_t, 1)

        def ada_act(act, l, step):
            q = (step - 2) // 2
            if step % 2 == 0 and 0 <= q < ADA_QUADS:
                lin = PLAN["ada", l]
                wait_products(act, lin, Group(4 * q + 3, 4 * q + 3, 0, lin.n))
                if ADA_QUADS * l + q >= 1:
                    act.wait_ge(s.ada_t, ADA_QUADS * l + q)
                act.activation(ada_row[0:2, :], ada_bank(l, q)[0:2, :], ACT.Copy).then_inc(s.ada_row, 1)

        def ada_dve(dve, l, step):
            q = (step - 4) // 2
            if step % 2 == 0 and 0 <= q < ADA_QUADS:
                dve.wait_ge(s.ada_t, ADA_QUADS * l + q + 1)
                c0 = 72 * l + 4 * q
                dve.tensor_tensor(mods[:, l, 8 * q:8 * q + 8].rearrange("p (m c) -> p m c", c=2),
                                  ada_bank(l, q)[:, 0:8].rearrange("p (m c) -> p m c", c=2),
                                  param("bada")[:, c0:c0 + 4].unsqueeze(2).broadcast_to([P, 4, 2]),
                                  ALU.add).then_inc(s.ada_out, 1)

        SHIFT, SCALE, GATE = (0, 3, 6), (1, 4, 7), (2, 5, 8)
        LAST_NORM = 5 * DEPTH
        OUT_LINS = [(a, l) for l in range(DEPTH) for a in ("wo", "down")] + [
            (a, l) for l in range(DEPTH) for a in ("ffn1_out", "mix_out", "ffn2_out")]

        def norm_width(n):
            return T if n < 2 * DEPTH or n >= LAST_NORM - 1 else 2 * T

        def is_split(n):
            return 2 * DEPTH <= n < LAST_NORM - 1

        def norm_act(act, n):
            w = norm_width(n)
            act.wait_ge(s.mean_sq, n + 1)
            act.activation(lnb[:, 0:w], bank[7][:, 0:w], ACT.Ln, bias=eps_col)
            act.drain()
            act.activation(rstd[:, 0:w], lnb[:, 0:w], ACT.Exp, scale=-0.5).then_inc(s.rstd, 1)
            if is_split(n):
                l, which = divmod(n - 2 * DEPTH, 3)
                for k in range(KT):
                    act.wait_ge(s.norm_value, KT * (n - 2 * DEPTH) + k + 1)
                    for c in range(w // T):
                        t = slice(c * T, (c + 1) * T)
                        last = act.activation(hn_hi[:, k, t], sq[:, k, t], ACT.Identity,
                                              bias=modulation(l)[:, SHIFT[which], k, c:c + 1])
                    last.then_inc(s.norm_hi, 1)

        def norm_pe(pe, n):
            w = norm_width(n)
            pe.wait_ge(s.squares, KT * (n + 1))
            pe.matmul(bank[7][:, 0:w], ones_d, sumsq[:, 0:w], start=True, stop=True).then_inc(s.mean_sq, 1)

        def norm_low(dve, n, k):
            w = norm_width(n)
            dve.wait_ge(s.norm_hi, KT * (n - 2 * DEPTH) + k + 1)
            l, which = divmod(n - 2 * DEPTH, 3)
            for c in range(w // T):
                t = slice(c * T, (c + 1) * T)
                last = dve.scalar_tensor_tensor(out=hn_lo[:, k, t], in0=sq[:, k, t],
                                                scalar=modulation(l)[:, SHIFT[which], k, c:c + 1],
                                                in1=hn_hi[:, k, t].bitcast(F32), op0=ALU.add, op1=ALU.subtract)
            last.then_inc(s.split_normed, 1)

        def wait_normed(pe, n, k):
            n = n if n < 2 * DEPTH else 2 * DEPTH
            pe.wait_ge(s.normed, KT * n + k + 1)

        def units_block1(l):
            out = []
            for tt in range(TT):
                for g in range(2):
                    for hh in range(2):
                        tile0 = 2 * g
                        for kind in ("cmp", "slc", "win"):
                            out.append(Unit(kind, tt, g=g, hh=hh, tile0=tile0,
                                                       first=kind == "cmp", last=kind == "win"))
                for hh in range(2):
                    out.append(Unit("fox", tt, hh=hh))
            base, obase = l * len(out), l * sum(x.last for x in out)
            o = 0
            for n, x in enumerate(out):
                x.u, x.o, x.l = base + n, obase + o, l
                x.keys = N_CMP if x.kind == "cmp" else T
                o += x.last
            return out

        N_UNITS1 = DEPTH * len(units_block1(0))
        N_OUTS1 = DEPTH * sum(x.last for x in units_block1(0))

        def scores(x):
            return bank[4 + x.u % 2]

        def head_cols(x):
            return slice(x.lo, x.lo + DH)

        def unit_scores(pe, x):
            if x.u >= 2:
                pe.wait_ge(s.att_m, x.u - 1)
            q0 = x.tt * P
            rows = slice(x.lo, x.lo + DH)
            for j in range(2):
                dst = scores(x)[:, j * x.keys:(j + 1) * x.keys]
                if x.kind == "fox":
                    mm = pe.matmul(dst, qkn[rows, 6 + j, q0:q0 + P], qkn[rows, 8 + j, :], start=True, stop=False)
                    for st in range(TT):
                        mm = pe.matmul(dst, fa[:, st, 2 * j + x.hh, q0:q0 + P], gtk[:, st, :],
                                       start=False, stop=(st == TT - 1))
                else:
                    key = kcb[rows, x.g * N_CMP:(x.g + 1) * N_CMP] if x.kind == "cmp" else \
                        kd[rows, x.g, 0 if x.kind == "slc" else 1, :]
                    mm = pe.matmul(dst, qr[rows, x.tile0 + j, q0:q0 + P], key, start=True, stop=True)
            mm.then_inc(s.att_s, 1)

        def unit_turn(pe, x):
            pe.wait_ge(s.att_p, x.u + 1)
            if x.u >= 1:
                pe.wait_ge(s.att_c, x.u)
            kt = 1 if x.kind == "cmp" else TT
            kw = min(x.keys, P)
            for j in range(2):
                for k in range(kt):
                    mm = pe.transpose(bank[6][0:kw, (j * kt + k) * P:(j * kt + k + 1) * P],
                                      pr[:, x.u % 2, j * x.keys + k * P:j * x.keys + k * P + kw], ident)
            mm.then_inc(s.att_t, 1)

        VCOL = {"slc": 384, "win": 512, "fox": 640}

        def unit_values(pe, x):
            pe.wait_ge(s.att_c, x.u + 1)
            if x.first and x.o >= 2:
                pe.wait_ge(s.att_o, x.o - 1)
            kt = 1 if x.kind == "cmp" else TT
            for j in range(2):
                dst = bank[7][head_cols(x), j * P:(j + 1) * P]
                for k in range(kt):
                    if x.kind == "cmp":
                        v, p_t = vc[0:N_CMP, x.g, :], pt[0:N_CMP, x.u % 2, j * P:(j + 1) * P]
                    else:
                        head = 2 * j + x.hh if x.kind == "fox" else x.g
                        c0 = VCOL[x.kind] + head * DH
                        v, p_t = vtok[:, k, c0:c0 + DH], pt[:, x.u % 2, (j * kt + k) * P:(j * kt + k + 1) * P]
                    mm = pe.matmul(dst, v, p_t, start=(x.first and j == 0 and k == 0),
                                   stop=(x.last and k == kt - 1), skip_group_check=True)
            mm.then_inc(s.att_v, 1)

        def attention_pe(pe, l, units):
            for n in range(len(units) + 2):
                ada_pe(pe, l, n)
                if n < len(units):
                    unit_scores(pe, units[n])
                if 1 <= n <= len(units):
                    unit_turn(pe, units[n - 1])
                if n >= 2:
                    unit_values(pe, units[n - 2])

        def unit_mask(dve, x):
            dve.wait_ge(s.att_s, x.u + 1)
            if x.u >= 2:
                dve.wait_ge(s.att_e, x.u - 1)
            n = 2 * x.keys
            src = scores(x)[:, 0:n].rearrange("p (j k) -> p j k", j=2)
            dst = sm[:, x.u % 2, 0:n].rearrange("p (j k) -> p j k", j=2)
            if x.kind == "cmp":
                add = cneg[:, x.tt, :].rearrange("p (j k) -> p j k", j=2)
            else:
                add = causal[:, x.tt, :].unsqueeze(1).broadcast_to([P, 2, T])
            dve.scalar_tensor_tensor(out=dst, in0=src, scalar=1.0 if x.kind == "fox" else DH ** -0.5, in1=add,
                                     op0=ALU.mult, op1=ALU.add)
            dve.drain()
            dve.tensor_reduce(mx[:, 2 * (x.u % 2):2 * (x.u % 2) + 2], dst, AX_X, ALU.max)
            dve.drain()
            dve.tensor_scalar(negmx[:, 2 * (x.u % 2):2 * (x.u % 2) + 2], mx[:, 2 * (x.u % 2):2 * (x.u % 2) + 2],
                              -1.0, None, ALU.mult).then_inc(s.att_m, 1)

        def unit_norm(dve, x):
            dve.wait_ge(s.att_e, x.u + 1)
            at = 2 * (x.u % 2)
            n = 2 * x.keys
            p_u = pr[:, x.u % 2, 0:n].rearrange("p (j k) -> p j k", j=2)
            if x.kind == "cmp":
                dve.tensor_tensor(p_u, p_u, cmask[:, x.tt, :].rearrange("p (j k) -> p j k", j=2), ALU.mult)
                dve.drain()
                dve.tensor_reduce(smu[:, at:at + 2], p_u, AX_X, ALU.add)
                dve.drain()
            dve.tensor_scalar(smu[:, at:at + 2], smu[:, at:at + 2], TINY, None, ALU.max)
            dve.drain()
            dve.reciprocal(rcp[:, at:at + 2], smu[:, at:at + 2])
            dve.drain()
            if x.kind != "fox":
                br = ("cmp", "slc", "win").index(x.kind)
                c0 = br * 8 + 4 * x.g + x.hh
                dve.tensor_tensor(rcp[:, at:at + 2], rcp[:, at:at + 2], gate[:, x.tt, c0:c0 + 3:2], ALU.mult)
                dve.drain()
            for j in range(2):
                last = dve.tensor_scalar(pr[:, x.u % 2, j * x.keys:(j + 1) * x.keys],
                                         pr[:, x.u % 2, j * x.keys:(j + 1) * x.keys],
                                         rcp[:, at + j:at + j + 1], None, ALU.mult)
            last.then_inc(s.att_p, 1)

        def attention_dve(dve, l, units):
            for n in range(len(units) + 2):
                ada_dve(dve, l, n)
                if 1 <= n <= len(units):
                    unit_norm(dve, units[n - 1])
                if n < len(units):
                    unit_mask(dve, units[n])

        def unit_exp(act, x):
            act.wait_ge(s.att_m, x.u + 1)
            if x.u >= 2:
                act.wait_ge(s.att_t, x.u - 1)
            at = 2 * (x.u % 2)
            for j in range(2):
                last = act.activation(pr[:, x.u % 2, j * x.keys:(j + 1) * x.keys],
                                      sm[:, x.u % 2, j * x.keys:(j + 1) * x.keys], ACT.Exp,
                                      bias=negmx[:, at + j:at + j + 1], accum_out=smu[:, at + j:at + j + 1])
            last.then_inc(s.att_e, 1)

        def unit_copy(act, x):
            act.wait_ge(s.att_t, x.u + 1)
            if x.u >= 2:
                act.wait_ge(s.att_v, x.u - 1)
            kw = min(x.keys, P)
            n = 2 * P if x.kind == "cmp" else 4 * P
            act.activation(pt[0:kw, x.u % 2, 0:n], bank[6][0:kw, 0:n], ACT.Copy).then_inc(s.att_c, 1)

        def unit_out(act, x):
            if not x.last:
                return
            act.wait_ge(s.att_v, x.u + 1)
            t0 = x.tt * P
            m0 = 6 if x.kind == "fox" else 2 + x.tile0
            act.activation(mixt[head_cols(x), m0:m0 + 2, t0:t0 + P],
                           bank[7][head_cols(x), 0:2 * P].rearrange("p (j q) -> p j q", j=2),
                           ACT.Copy).then_inc(s.att_o, 1)

        def attention_act(act, l, units):
            for n in range(len(units) + 2):
                ada_act(act, l, n)
                if n < len(units):
                    unit_exp(act, units[n])
                if 1 <= n <= len(units):
                    unit_copy(act, units[n - 1])
                if n >= 2:
                    unit_out(act, units[n - 2])

        NL = len(HG_LEVELS)
        HG_STEPS = NL + 3

        MIX_STEPS = len(units_block1(0)) + 2

        def hg_banks(l, n):
            u = l * HG_STEPS + n
            return u, bank[4 + 2 * (u % 2)], bank[5 + 2 * (u % 2)]

        def hg_decayed(l, n):
            return l * (HG_STEPS - 1) + (n if n < NL + 1 else n - 1)

        def hg_pe(pe, l):
            for n in range(HG_STEPS):
                u, b0, b1 = hg_banks(l, n)
                if n != NL + 1:
                    pe.wait_ge(s.hg_qk, hg_decayed(l, n) + 1)
                if n >= 2:
                    pe.wait_ge(s.hg_sc, u - 1)
                far, diag = n == NL + 2, n == NL + 1
                for hh, b in enumerate((b0, b1)):
                    rows = slice(hh * DH, hh * DH + DH)
                    for kt in range(2):
                        for tt in range(1 if far else TT):
                            k0 = kt * T + tt * P
                            keys = (kc if diag else qk)[rows, k0:k0 + P]
                            q0 = k0 + P if far else k0
                            queries = (q8 if diag else qk)[rows, q0:q0 + P]
                            c0 = kt * P if far else (kt * 2 + tt) * P
                            mm = pe.matmul(b[:, c0:c0 + P], keys, queries, start=True, stop=True)
                mm.then_inc(s.hg_x, 1)
                ada_pe(pe, l, MIX_STEPS + n)
            pe.wait_ge(s.hg_sc, (l + 1) * HG_STEPS)
            u, b0, b1 = hg_banks(l, 0)
            for kt in range(2):
                for hh in range(2):
                    rows, c0 = slice(hh * DH, hh * DH + DH), 128 + (2 * kt + hh) * DH
                    for tt in range(TT):
                        dst = bank[4][rows, kt * T + tt * P:kt * T + (tt + 1) * P]
                        pe.matmul(dst, vtok[:, tt, c0:c0 + DH], scores_hg[:, hh, kt * 2 + tt, :],
                                  start=True, stop=(tt == 0), skip_group_check=True)
                        if tt == 1:
                            mm = pe.matmul(dst, vtok[:, 0, c0:c0 + DH], scores_far[:, hh, kt, :],
                                           start=False, stop=True, skip_group_check=True)
            mm.then_inc(s.hg_o, 1)
            pe.wait_ge(s.hg_osq, l + 1)
            pe.matmul(bank[5][:, :], blk64, ee, start=True, stop=True).then_inc(s.hg_oms, 1)

        def halves(ap, L):
            v = ap.rearrange("p (b h t) -> p b h t", h=2, t=L)
            return v[:, :, 0, :], v[:, :, 1, :]

        def hg_dve(dve, l):
            z_ = proj_b[:, 0:2 * T]
            q_ = proj_b[:, 2 * T:4 * T]
            dve.wait_ge(s.sig, l + 1)
            for kt in range(2):
                c = slice(kt * T, (kt + 1) * T)
                dve.tensor_scalar(sg[:, c], sg[:, c], lb_u[:, 2 * l + kt:2 * l + kt + 1],
                                  lb_t[:, 2 * l + kt:2 * l + kt + 1], ALU.mult, ALU.add)
                dve.tensor_scalar(kc[:, c], kc[:, c], lb_u[:, 2 * l + kt:2 * l + kt + 1], None, ALU.mult)
            dve.tensor_scalar(q8, q_, DH ** -0.5, None, ALU.mult)
            dve.drain()
            dve.tensor_scalar(ee, sg, 1.0 / LN_SPLIT, None, ALU.max)
            dve.tensor_scalar(gg, sg, TINY, LN_SPLIT, ALU.max, ALU.mult)
            dve.drain()
            dve.tensor_scalar(gg, gg, 1.0, None, ALU.min).then_inc(s.hg_f, 1)
            dve.wait_ge(s.hg_ln, l + 1)
            dve.tensor_tensor(sg, ee, gg, ALU.add)
            dve.drain()
            dve.tensor_tensor_scan(gg, const(1, "reset"), sg, 0.0, ALU.mult, ALU.add)
            dve.drain()
            steps = list(HG_LEVELS) + [HG_CHUNK, None, "far"]

            def take(n):
                u, b0, b1 = hg_banks(l, n)
                dve.wait_ge(s.hg_x, u + 1)
                if n == 0:
                    dve.wait_ge(s.zeroed, l + 1)
                for hh, b in enumerate((b0, b1)):
                    if steps[n] == "far":
                        last = dve.tensor_copy(scores_far[:, hh, :, :], b[:, 0:2 * P].rearrange("p (b t) -> p b t", b=2))
                    else:
                        m = lvl_u[:, NL + 1 if steps[n] is None else n, :].unsqueeze(1).broadcast_to([P, 4, P])
                        last = dve.copy_predicated(scores_hg[:, hh, :, :], m,
                                                   b[:, :].rearrange("p (b t) -> p b t", b=4))
                last.then_inc(s.hg_sc, 1)

            for n, L in enumerate(steps):
                ada_dve(dve, l, MIX_STEPS + n)
                dve.drain()
                if L is None:
                    take(n - 1)
                    continue
                if L == "far":
                    v = gg.rearrange("p (k c t) -> p k c t", k=2, t=HG_CHUNK)
                    e = ee.rearrange("p (k c t) -> p k c t", k=2, t=HG_CHUNK)
                    end = lambda c: v[:, :, c, HG_CHUNK - 1:HG_CHUNK].broadcast_to([P, 2, HG_CHUNK])
                    dve.tensor_tensor(e[:, :, 0, :], end(0), v[:, :, 0, :], ALU.subtract)
                    dve.tensor_tensor(e[:, :, 1, :], end(1), v[:, :, 1, :], ALU.subtract)
                    dve.tensor_copy(e[:, :, 2, :], v[:, :, 2, :])
                    dve.tensor_tensor(e[:, :, 3, :], end(2), v[:, :, 3, :], ALU.add)
                    dve.drain()
                    dve.tensor_tensor(e[:, :, 0, :], e[:, :, 0, :], end(1), ALU.add).then_inc(s.hg_g, 1)
                else:
                    gl, gr = halves(gg, L)
                    el, er = halves(ee, L)
                    mid = gl[:, :, L - 1:L].broadcast_to(list(gl.shape))
                    dve.tensor_tensor(el, mid, gl, ALU.subtract)
                    if L == HG_CHUNK:
                        dve.tensor_copy(er, gr).then_inc(s.hg_g, 1)
                    else:
                        dve.tensor_tensor(er, gr, mid, ALU.subtract).then_inc(s.hg_g, 1)
                if n >= 1 and steps[n - 1] is not None or L == "far":
                    take(n - 1)
                dve.wait_ge(s.hg_e, hg_decayed(l, n) + 1)
                if L == "far":
                    kl, ql = [t.rearrange("p (k h t) -> p k h t", k=2, h=2)[:, :, i, :] for t, i in ((kc, 0), (q8, 1))]
                    eh = ee.rearrange("p (k h t) -> p k h t", k=2, h=2)
                    dst = qk.rearrange("p (k h t) -> p k h t", k=2, h=2)
                    el, er, dl, dr = eh[:, :, 0, :], eh[:, :, 1, :], dst[:, :, 0, :], dst[:, :, 1, :]
                else:
                    kl, ql = halves(kc, L)[0], halves(q8, L)[1]
                    dl, dr = halves(qk, L)
                dve.tensor_tensor(dl, el, kl, ALU.mult)
                dve.tensor_tensor(dr, er, ql, ALU.mult).then_inc(s.hg_qk, 1)
            take(HG_STEPS - 1)
            dve.wait_ge(s.hg_ors, l + 1)
            dve.scalar_tensor_tensor(out=gg, in0=bank[4][:, :], scalar=param(f"onorm@{l}"), in1=ee,
                                     op0=ALU.mult, op1=ALU.mult)
            dve.tensor_tensor(sg, proj_b[:, 16 * T:18 * T], sga, ALU.mult)
            dve.drain()
            dve.tensor_tensor(mix_b[:, 0:2 * T], gg, sg, ALU.mult).then_inc(s.mixa, 1)

        def hg_act(act, l):
            act.wait_ge(s.hg_f, l + 1)
            act.activation(ee, ee, ACT.Ln)
            act.activation(gg, gg, ACT.Ln).then_inc(s.hg_ln, 1)
            for n in range(HG_STEPS - 1):
                ada_act(act, l, MIX_STEPS + n)
                u = l * (HG_STEPS - 1) + n
                act.wait_ge(s.hg_g, u + 1)
                act.activation(ee, ee, ACT.Exp).then_inc(s.hg_e, 1)
            act.wait_ge(s.hg_o, l + 1)
            act.activation(ee, bank[4][:, :], ACT.Square).then_inc(s.hg_osq, 1)
            act.wait_ge(s.hg_oms, l + 1)
            act.activation(qk, bank[5][:, :], ACT.Ln, bias=eps_col)
            act.drain()
            act.activation(ee, qk, ACT.Exp, scale=-0.5).then_inc(s.hg_ors, 1)

        def input_product(pe, lin, g, c, dst, norm, w):
            if lin.split:
                def wait_part(part, k):
                    if c == 0:
                        pe.wait_ge((s.norm_hi, s.split_normed)[part], KT * (norm - 2 * DEPTH) + k + 1)

                split_product(pe, lin, g, c, dst, wait_part, w)
                return
            wait_weights(pe, lin, g, c)
            for k in range(KT):
                if g.at == 0 and c == 0:
                    wait_normed(pe, norm, k)
                mm = pe.matmul(dst, ring[:, slot_of(lin, g, c), k * P:(k + 1) * P], sq[:, k, 0:w],
                               start=(k == 0), stop=(k == KT - 1))
            mm.then_inc(used[slot_of(lin, g, c)], 1)

        def dense_t(pe, lin, norm):
            w = norm_width(norm)
            for g in turns(pe, lin):
                wait_banks(pe, lin, g)
                input_product(pe, lin, g, 0, bank[2 * parity(lin, g)][:, 0:w], norm, w)

        def hid_split_number(lin):
            return [x for x in PLAN.values() if x.split and x.tiles == lin.tiles].index(lin)

        def hidden_product(pe, lin, g, x, w):
            last, row = sum(lin.tiles) - 1, 0
            for c in range(lin.cpg):
                if c in lin.split:
                    split_product(pe, lin, g, c, bank[2 * parity(lin, g)][:, 0:w],
                                  lambda part, k: pe.wait_ge((s.hid_hi, s.hid_lo)[part], KT * hid_split_number(lin) + k + 1),
                                  w, start=False, stop=False)
                    row += lin.tiles[c]
                    continue
                wait_weights(pe, lin, g, c)
                for k in range(lin.tiles[c]):
                    mm = pe.matmul(bank[2 * parity(lin, g)][:, 0:w], ring[:, slot_of(lin, g, c), k * P:(k + 1) * P],
                                   x(row), start=(row == 0), stop=(row == last))
                    row += 1
                mm.then_inc(used[slot_of(lin, g, c)], 1)

        def block1_pe(pe, l):
            norm_pe(pe, 2 * l)
            dense_t(pe, PLAN["in_t", l], 2 * l)
            lin = PLAN["in_a", l]
            for g in turns(pe, lin):
                wait_banks(pe, lin, g)
                wait_weights(pe, lin, g, 0)
                for tt in range(TT):
                    q = slice(tt * P, (tt + 1) * P)
                    for k in range(KT):
                        mm = pe.matmul(bank[2 * parity(lin, g)][:, q], sq[:, k, q],
                                       ring[:, slot_of(lin, g, 0), k * P:(k + 1) * P],
                                       start=(k == 0), stop=(k == KT - 1))
                mm.then_inc(used[slot_of(lin, g, 0)], 1)
            pe.wait_ge(s.consts1, 16)
            pe.wait_ge(s.hn_sq, l + 1)
            for u in range(5):
                if u >= 2:
                    pe.wait_ge(s.hn_ln, 5 * l + u - 1)
                pe.matmul(bank[4 + u % 2][:, :], blk64, sq_b[:, u * 2 * T:(u + 1) * 2 * T],
                          start=True, stop=True).then_inc(s.hn_ms, 1)
            pe.wait_ge(s.qkn, l + 1)
            pe.matmul(bank[4][:, :], rot, qkn_b[:, 2 * T:4 * T], start=True, stop=True).then_inc(s.rotated, 1)
            pe.matmul(bank[5][:, :], rot, qkn_b[:, 4 * T:6 * T], start=True, stop=True).then_inc(s.rotated, 1)
            for g in range(2):
                if g == 1:
                    pe.wait_ge(s.rope, 4 * l + 3)
                pe.matmul(bank[6][:, :], dup[:, g, :], qkn_b[:, 0:2 * T], start=True, stop=True)
                pe.matmul(bank[7][:, :], rotdup[:, g, :], qkn_b[:, 0:2 * T],
                          start=True, stop=True).then_inc(s.rotated, 1)
            lin = PLAN["cmp", l]
            for g in turns(pe, lin):
                wait_banks(pe, lin, g)
                pe.wait_ge(s.blocks, 2 * l + g.m + 1)
                for c in range(4):
                    wait_weights(pe, lin, g, c)
                    for i in range(8):
                        mm = pe.matmul(bank[2 * parity(lin, g)][:, 0:2 * N_CMP],
                                       ring[:, slot_of(lin, g, c), i * P:(i + 1) * P],
                                       bc_b[:, (g.m * CMP_L + 8 * c + i) * 2 * N_CMP:(g.m * CMP_L + 8 * c + i + 1) * 2 * N_CMP],
                                       start=(c == 0 and i == 0), stop=(c == 3 and i == 7))
                    mm.then_inc(used[slot_of(lin, g, c)], 1)
            pe.wait_ge(s.rope, 4 * l + 4)
            wait_drained(pe, lin, 0)
            pe.matmul(bank[4][:, 0:2 * N_CMP], param(f"w2k@{l}"), hk, start=True, stop=True).then_inc(s.cmp_raw, 1)
            wait_drained(pe, lin, 1)
            for g in range(2):
                mm = pe.matmul(bank[5][0:N_CMP, g * DH:(g + 1) * DH], hv[:, g * N_CMP:(g + 1) * N_CMP],
                               param(f"w2v@{l}"), start=True, stop=True)
            mm.then_inc(s.cmp_raw, 1)
            pe.wait_ge(s.kc_sq, l + 1)
            pe.matmul(bank[6][:, 0:2 * N_CMP], blk64, krot, start=True, stop=True).then_inc(s.kc_ms, 1)
            pe.wait_ge(s.kc_n, l + 1)
            pe.matmul(bank[7][:, 0:2 * N_CMP], rot, kcn, start=True, stop=True).then_inc(s.kc_rot, 1)
            pe.wait_ge(s.kc_done, l + 1)
            pe.wait_ge(s.vc_done, l + 1)
            pe.wait_ge(s.fa, l + 1)
            attention_pe(pe, l, units_block1(l))
            pe.wait_ge(s.att_o, N_OUTS1 // DEPTH * (l + 1))
            hg_pe(pe, l)
            lin = PLAN["wo", l]
            pe.wait_ge(s.mixa, l + 1)
            for g in turns(pe, lin):
                wait_banks(pe, lin, g)
                wait_weights(pe, lin, g, 0)
                for k in range(KT):
                    mm = pe.matmul(bank[2 * parity(lin, g)][:, 0:T], ring[:, slot_of(lin, g, 0), k * P:(k + 1) * P],
                                   mixt[:, k, :], start=(k == 0), stop=(k == KT - 1))
                mm.then_inc(used[slot_of(lin, g, 0)], 1)
            norm_pe(pe, 2 * l + 1)
            dense_t(pe, PLAN["up", l], 2 * l + 1)
            lin = PLAN["down", l]
            wait_all_drained(pe, PLAN["up", l])
            for g in turns(pe, lin):
                wait_banks(pe, lin, g)
                hidden_product(pe, lin, g, lambda k: hid1[:, k, :], T)

        def block1_act(act, l):
            norm_act(act, 2 * l)
            if l == 0:
                act.wait_ge(s.lb, 1)
                act.activation(lb, lb, ACT.Exp).then_inc(s.lb, 1)
            lin = PLAN["in_t", l]
            for g in turns(act, lin, tail=2):
                wait_products(act, lin, g)
                act.activation(proj[:, g.m, :], bank[2 * parity(lin, g)][:, 0:T],
                               ACT.Copy).then_inc(drained[parity(lin, g)], 1)
            lin = PLAN["in_a", l]
            for g in turns(act, lin, tail=2):
                wait_products(act, lin, g)
                act.activation(vtok[:, :, g.m * P:(g.m + 1) * P],
                               bank[2 * parity(lin, g)][:, 0:T].rearrange("p (t c) -> p t c", t=TT),
                               ACT.Copy).then_inc(drained[parity(lin, g)], 1)
            act.drain()
            act.activation(sq_b, proj_b[:, 4 * T:14 * T], ACT.Square).then_inc(s.hn_sq, 1)
            for u in range(5):
                act.wait_ge(s.hn_ms, 5 * l + u + 1)
                act.activation(sq_b[:, u * 2 * T:(u + 1) * 2 * T], bank[4 + u % 2][:, :], ACT.Ln,
                               bias=eps_col).then_inc(s.hn_ln, 1)
            act.drain()
            act.activation(sq_b, sq_b, ACT.Exp, scale=-0.5).then_inc(s.hn_rs, 1)
            act.wait_ge(s.fox_in, l + 1)
            act.activation(lx, lx, ACT.Exp, scale=-1.0)
            act.drain()
            act.activation(ly, lx, ACT.Ln, bias=one_col).then_inc(s.fox_e, 1)
            act.activation(sg, proj_b[:, 0:2 * T], ACT.Sigmoid)
            act.activation(kc, proj_b[:, 0:2 * T], ACT.Sigmoid, scale=-1.0)
            act.activation(sga, proj_b[:, 16 * T:18 * T], ACT.Sigmoid)
            act.activation(gate, vtok[:, :, 0:24], ACT.Sigmoid).then_inc(s.sig, 1)
            lin = PLAN["cmp", l]
            for g, dst in zip(turns(act, lin), (hk, hv)):
                wait_products(act, lin, g)
                act.activation(dst, bank[2 * parity(lin, g)][:, 0:2 * N_CMP],
                               ACT.Gelu_apprx_tanh).then_inc(drained[parity(lin, g)], 1)
            act.wait_ge(s.cmp_raw, 2 * l + 1)
            act.activation(krot, bank[4][:, 0:2 * N_CMP], ACT.Square).then_inc(s.kc_sq, 1)
            act.wait_ge(s.kc_ms, l + 1)
            act.activation(kcb, bank[6][:, 0:2 * N_CMP], ACT.Ln, bias=eps_col)
            act.drain()
            act.activation(kcb, kcb, ACT.Exp, scale=-0.5).then_inc(s.kc_rs, 1)
            attention_act(act, l, units_block1(l))
            hg_act(act, l)
            norm_act(act, 2 * l + 1)
            lin = PLAN["up", l]
            for g in turns(act, lin, tail=2):
                wait_products(act, lin, g)
                q = parity(lin, g)
                act.activation(tmp2[:, q, 0:T], bank[2 * q][:, 0:T], ACT.Relu)
                act.drain()
                act.activation(hid1[:, g.m, :], tmp2[:, q, 0:T], ACT.Square).then_inc(drained[q], 1)
            if l == DEPTH - 1 and 2 in blocks:
                first_split(split_high, act, PLAN["ffn1", 0])

        def norm1_dve(dve, n, gain):
            dve.wait_ge(s.rstd, n + 1)
            for k in range(KT):
                dve.scalar_tensor_tensor(out=sq[:, k, 0:T], in0=res[:, k, 0:T], scalar=gain[:, k:k + 1],
                                         in1=rstd[:, 0:T], op0=ALU.mult, op1=ALU.mult).then_inc(s.normed, 1)

        def square(dve, k, c0, c1):
            dve.tensor_tensor(sq[:, 0, c0:c1], res[:, k, c0:c1], res[:, k, c0:c1], ALU.mult)
            dve.drain()
            return dve.tensor_tensor(sumsq[:, c0:c1], sumsq[:, c0:c1], sq[:, 0, c0:c1], ALU.add)

        def add_to_residual(dve, lin, following, context=False):
            dve.drain()
            dve.memset(sumsq, 0.0)
            dve.drain()
            if context:
                for k in range(KT):
                    square(dve, k, T, 2 * T)
                    dve.drain()
            for g in turns(dve, lin, tail=2):
                split_following(dve, lin, g, following)
                wait_products(dve, lin, g)
                dve.tensor_tensor(res[:, g.m, 0:T], bank[2 * parity(lin, g)][:, 0:T], res[:, g.m, 0:T],
                                  ALU.add).then_inc(drained[parity(lin, g)], 1)
                dve.drain()
                square(dve, g.m, 0, T).then_inc(s.squares, 1)

        def split_following(dve, lin, g, following):
            if lin.split:
                splits_ahead(split_low, dve, lin, g, following)
            elif following and isinstance(g.m, int) and g.m == lin.n - 1:
                first_split(split_low, dve, following)

        def bounds_dve(dve):
            a, b = param("lb")[:, 0:2], param("lb")[:, 2:4]
            dve.tensor_tensor(lb_u[:, 0:2], a, b, ALU.max)
            dve.drain()
            dve.tensor_tensor(lb[:, 0:2], a, lb_u[:, 0:2], ALU.subtract)
            dve.tensor_tensor(lb[:, 2:4], b, lb_u[:, 0:2], ALU.subtract).then_inc(s.lb, 1)
            dve.wait_ge(s.lb, 2)
            dve.tensor_tensor(lb_u[:, 0:2], lb[:, 0:2], lb[:, 2:4], ALU.add)
            dve.drain()
            dve.reciprocal(lb_u[:, 2:4], lb_u[:, 0:2])
            dve.drain()
            dve.tensor_tensor(lb[:, 0:2], lb[:, 0:2], lb_u[:, 2:4], ALU.mult)
            dve.tensor_tensor(lb[:, 2:4], lb[:, 2:4], lb_u[:, 2:4], ALU.mult)
            dve.drain()
            dve.tensor_tensor(lb_t[:, 0:2], lb[:, 0:2], lb[:, 0:2], ALU.subtract)
            dve.tensor_tensor(lb_t[:, 2:4], lb[:, 0:2], lb[:, 2:4], ALU.add)
            dve.drain()
            dve.tensor_tensor(lb_t[:, 2:4], lb_t[:, 2:4], lb[:, 0:2], ALU.subtract)
            dve.drain()
            dve.tensor_scalar(lb_u[:, 0:4], lb_t[:, 0:4], -1.0, 1.0, ALU.mult, ALU.add)
            dve.drain()

        def block1_dve(dve, l):
            norm1_dve(dve, 2 * l, param(f"norm1@{l}"))
            if l == 0:
                bounds_dve(dve)
            wait_drained(dve, PLAN["in_a", l], 0)
            for tt in range(TT):
                dve.tensor_tensor(lx[:, 4 * tt:4 * tt + 4], vtok[:, tt, 24:28], param(f"fb@{l}"), ALU.add)
            dve.drain()
            dve.tensor_scalar(lz, lx, 0.0, None, ALU.min)
            dve.tensor_scalar(ly, lx, -1.0, None, ALU.mult)
            dve.drain()
            dve.tensor_tensor(lx, lx, ly, ALU.max).then_inc(s.fox_in, 1)
            dve.tensor_copy(qkg, param(f"qkg@{l}"))
            dve.drain()
            dve.tensor_scalar(qkg[:, 6:8], qkg[:, 6:8], DH ** -0.5, None, ALU.mult)
            dve.drain()
            dve.wait_ge(s.hn_rs, l + 1)
            for j in range(10):
                last = dve.scalar_tensor_tensor(out=qkn[:, j, :], in0=proj[:, 4 + j, :], scalar=qkg[:, j:j + 1],
                                                in1=sqh[:, j, :], op0=ALU.mult, op1=ALU.mult)
            last.then_inc(s.qkn, 1)
            dve.drain()
            dve.wait_ge(s.consts1, 16)
            cos2 = cos.unsqueeze(1).broadcast_to([P, 2, T])
            sin2 = sin.unsqueeze(1).broadcast_to([P, 2, T])
            tmp = ee.rearrange("p (m t) -> p m t", m=2)
            for u in range(2):
                dve.wait_ge(s.rotated, 4 * l + u + 1)
                dve.tensor_tensor(qr[:, 2 * u:2 * u + 2, :], qkn[:, 2 + 2 * u:4 + 2 * u, :], cos2, ALU.mult)
                dve.tensor_tensor(tmp, bank[4 + u][:, :].rearrange("p (m t) -> p m t", m=2), sin2, ALU.mult)
                dve.drain()
                dve.tensor_tensor(qr[:, 2 * u:2 * u + 2, :], qr[:, 2 * u:2 * u + 2, :], tmp,
                                  ALU.add).then_inc(s.rope, 1)
                dve.drain()
            for g in range(2):
                dve.wait_ge(s.rotated, 4 * l + 3 + g)
                dve.tensor_tensor(kd[:, g, :, :], bank[6][:, :].rearrange("p (m t) -> p m t", m=2), cos2, ALU.mult)
                dve.tensor_tensor(tmp, bank[7][:, :].rearrange("p (m t) -> p m t", m=2), sin2, ALU.mult)
                dve.drain()
                dve.tensor_tensor(kd[:, g, :, :], kd[:, g, :, :], tmp, ALU.add).then_inc(s.rope, 1)
                dve.drain()
            dve.wait_ge(s.fox_e, l + 1)
            dve.tensor_tensor(lf, lz, ly, ALU.subtract)
            dve.drain()
            for st in range(TT):
                for h in range(4):
                    last = dve.tensor_scalar(fa[:, st, h, :], tri[:, st, :], lf[:, 4 * st + h:4 * st + h + 1], None,
                                             ALU.mult)
            last.then_inc(s.fa, 1)
            dve.wait_ge(s.kc_rs, l + 1)
            dve.scalar_tensor_tensor(out=kcn, in0=bank[4][:, 0:2 * N_CMP], scalar=param(f"kng@{l}"), in1=kcb,
                                     op0=ALU.mult, op1=ALU.mult).then_inc(s.kc_n, 1)
            dve.drain()
            dve.wait_ge(s.cmp_raw, 2 * l + 2)
            dve.tensor_copy(vc_b[0:N_CMP, :], bank[5][0:N_CMP, 0:2 * DH]).then_inc(s.vc_done, 1)
            dve.wait_ge(s.kc_rot, l + 1)
            dve.tensor_tensor(kcb, kcn, const(1, "ccos"), ALU.mult)
            dve.tensor_tensor(krot, bank[7][:, 0:2 * N_CMP], const(1, "csin"), ALU.mult)
            dve.drain()
            dve.tensor_tensor(kcb, kcb, krot, ALU.add).then_inc(s.kc_done, 1)
            dve.wait_ge(s.sig, l + 1)
            attention_dve(dve, l, units_block1(l))
            hg_dve(dve, l)
            add_to_residual(dve, PLAN["wo", l], None)
            norm1_dve(dve, 2 * l + 1, param(f"norm2@{l}"))
            last = l == DEPTH - 1
            if last:
                dve.wait_ge(s.ctx_in, 16)
            add_to_residual(dve, PLAN["down", l], PLAN["ffn1", 0] if last and 2 in blocks else None, context=last)

        def block1_pool(pool, l):
            if l >= 1:
                pool.wait_ge(s.mixa, l)
            wait_all_drained(pool, PLAN["in_t", l])
            if l >= 1:
                wait_all_drained(pool, PLAN["down", l - 1])
                pool.wait_ge(s.blocks, 2 * l)
            pool.memset(bc_b, 0.0).then_inc(s.cleared, 1)
            pool.memset(sc_b, 0.0).then_inc(s.zeroed, 1)
            pool.wait_ge(s.cleared, l + 1)
            pool.wait_ge(s.zeroed, l + 1)
            pos = param(f"pos@{l}").rearrange("p (w l) -> p w l", w=2)
            for w in range(2):
                for g in range(2):
                    rows = slice(g * DH, g * DH + DH)
                    for h in range(2):
                        src = proj[rows, 14 + w, 16 * h:16 * h + 16 * N_CMP].rearrange("p (n l) -> p l n", l=16)
                        add = pos[rows, w, 16 * h:16 * h + 16].unsqueeze(2).broadcast_to([DH, 16, N_CMP])
                        last = pool.tensor_tensor(bc[rows, w, 16 * h:16 * h + 16, g, :], src, add, ALU.add)
                last.then_inc(s.blocks, 1)


        gs = gate_b.rearrange("p (n k c) -> p n k c", n=3, c=2)
        tmp4 = (rstd2, lnb2)

        def seqs(l):
            return 2 if l < DEPTH - 1 else 1

        def both(ap, w):
            return ap[:, 0:w].rearrange("p (s t) -> p s t", t=T)

        def units_block2(l):
            out = [Unit("lat", tt, h=h) for tt in range(TT) for h in range(QH)]
            if seqs(l) == 2:
                out += [Unit("ctx", TT + tt, h=2 * x) for tt in range(TT) for x in range(QH // 2)]
            u0 = N_UNITS1 + sum(len(units_block2(i)) for i in range(l))
            o0 = N_OUTS1 + sum(len(units_block2(i)) for i in range(l))
            for n, x in enumerate(out):
                x.u, x.o = u0 + n, o0 + n
                x.heads = 1 if x.kind == "lat" else 2
                x.keys = 4 * P // x.heads
                x.key0 = 0 if x.kind == "lat" else T
            return out

        def latent_scores(pe, x):
            pe.wait_ge(s.att_e, x.u - 1)
            for j in range(x.heads):
                mm = pe.matmul(scores(x)[:, j * x.keys:(j + 1) * x.keys],
                               q2[0:QK, x.h + j, x.tt * P:(x.tt + 1) * P],
                               k2[0:QK, x.h + j, x.key0:x.key0 + x.keys], start=True, stop=True)
            mm.then_inc(s.att_s, 1)

        def latent_turn(pe, x):
            pe.wait_ge(s.att_p, x.u + 1)
            pe.wait_ge(s.att_c, x.u)
            for k in range(4):
                mm = pe.transpose(bank[6][:, k * P:(k + 1) * P], pr[:, x.u % 2, k * P:(k + 1) * P], ident)
            mm.then_inc(s.att_t, 1)

        def latent_values(pe, x):
            pe.wait_ge(s.att_c, x.u + 1)
            pe.wait_ge(s.att_o, x.o - 1 if x.heads == 1 else x.o)
            kt = 4 // x.heads
            for j in range(x.heads):
                h = x.h + j
                rows = slice((h % 2) * DH, (h % 2) * DH + DH)
                for k in range(kt):
                    mm = pe.matmul(bank[7][rows, 0:P], v2[:, x.key0 // P + k, h * DH:(h + 1) * DH],
                                   pt[:, x.u % 2, (j * kt + k) * P:(j * kt + k + 1) * P],
                                   start=(k == 0), stop=(k == kt - 1), skip_group_check=True)
            mm.then_inc(s.att_v, 1)

        def latent_max(dve, x):
            dve.wait_ge(s.att_s, x.u + 1)
            dve.wait_ge(s.att_e, x.u - 1)
            at = 2 * (x.u % 2)
            dve.tensor_reduce(mx[:, at:at + x.heads], scores(x)[:, :].rearrange("p (j k) -> p j k", j=x.heads),
                              AX_X, ALU.max)
            dve.drain()
            dve.tensor_scalar(negmx[:, at:at + x.heads], mx[:, at:at + x.heads], -ATTN_SCALE, None,
                              ALU.mult).then_inc(s.att_m, 1)

        def latent_norm(dve, x):
            dve.wait_ge(s.att_e, x.u + 1)
            at = 2 * (x.u % 2)
            dve.reciprocal(rcp[:, at:at + x.heads], smu[:, at:at + x.heads])
            dve.drain()
            for j in range(x.heads):
                c = slice(j * x.keys, (j + 1) * x.keys)
                last = dve.tensor_scalar(pr[:, x.u % 2, c], pr[:, x.u % 2, c], rcp[:, at + j:at + j + 1], None,
                                         ALU.mult)
            last.then_inc(s.att_p, 1)

        def latent_exp(act, x):
            act.wait_ge(s.att_m, x.u + 1)
            act.wait_ge(s.att_t, x.u - 1)
            at = 2 * (x.u % 2)
            for j in range(x.heads):
                c = slice(j * x.keys, (j + 1) * x.keys)
                last = act.activation(pr[:, x.u % 2, c], scores(x)[:, c], ACT.Exp, scale=ATTN_SCALE,
                                      bias=negmx[:, at + j:at + j + 1], accum_out=smu[:, at + j:at + j + 1])
            last.then_inc(s.att_e, 1)

        def latent_copy(act, x):
            act.wait_ge(s.att_t, x.u + 1)
            act.wait_ge(s.att_v, x.u - 1)
            act.activation(pt[:, x.u % 2, :], bank[6][:, :], ACT.Copy).then_inc(s.att_c, 1)

        def latent_out(act, x):
            act.wait_ge(s.att_v, x.u + 1)
            rows = slice((x.h % 2) * DH, (x.h % 2) * DH + DH) if x.heads == 1 else slice(0, P)
            act.activation(att[rows, x.h // 2, x.tt * P:(x.tt + 1) * P], bank[7][rows, 0:P],
                           ACT.Copy).then_inc(s.att_o, 1)

        def gated_norm_dve(dve, l, which):
            n = 2 * DEPTH + 3 * l + which
            w = norm_width(n)
            mod = modulation(l)
            dve.wait_ge(s.rstd, n + 1)
            if is_split(n):
                for k in range(KT):
                    for c in range(w // T):
                        t = slice(c * T, (c + 1) * T)
                        last = dve.scalar_tensor_tensor(out=sq[:, k, t], in0=res[:, k, t], scalar=gs[:, which, k, c:c + 1],
                                                        in1=rstd[:, t], op0=ALU.mult, op1=ALU.mult)
                    last.then_inc(s.norm_value, 1)
                for k in range(KT):
                    norm_low(dve, n, k)
                return
            for k in range(KT):
                dve.tensor_tensor(sq[:, k, 0:w], res[:, k, 0:w], rstd[:, 0:w], ALU.mult)
                dve.drain()
                for c in range(w // T):
                    last = dve.tensor_scalar(sq[:, k, c * T:(c + 1) * T], sq[:, k, c * T:(c + 1) * T],
                                             gs[:, which, k, c:c + 1], mod[:, SHIFT[which], k, c:c + 1],
                                             ALU.mult, ALU.add)
                last.then_inc(s.normed, 1)

        def gated_add(dve, l, lin, which, w, following, w_next):
            mod = modulation(l)
            dve.drain()
            dve.memset(sumsq, 0.0)
            dve.drain()
            for g in turns(dve, lin, tail=2):
                split_following(dve, lin, g, following)
                wait_products(dve, lin, g)
                for c in range(w // T):
                    t = slice(c * T, (c + 1) * T)
                    last = dve.scalar_tensor_tensor(out=res[:, g.m, t], in0=bank[2 * parity(lin, g)][:, t],
                                                    scalar=mod[:, GATE[which], g.m, c:c + 1], in1=res[:, g.m, t],
                                                    op0=ALU.mult, op1=ALU.add)
                last.then_inc(drained[parity(lin, g)], 1)
                dve.drain()
                square(dve, g.m, 0, w_next).then_inc(s.squares, 1)

        def ffn_pe(pe, l, which):
            n = 2 * DEPTH + 3 * l + which
            w = norm_width(n)
            lin = PLAN["ffn1" if which == 0 else "ffn2", l]
            norm_pe(pe, n)
            gated_pair(pe, lin, n, w)
            wait_all_drained(pe, lin)
            lin = PLAN["ffn1_out" if which == 0 else "ffn2_out", l]
            for g in turns(pe, lin):
                wait_banks(pe, lin, g)
                hidden_product(pe, lin, g, lambda k: hid2[:, k, 0:w], w)

        def gated_pair(pe, lin, n, w):
            for g in turns(pe, lin):
                wait_banks(pe, lin, g)
                for c in range(2):
                    input_product(pe, lin, g, c, bank[2 * parity(lin, g) + c][:, 0:w], n, w)

        def ffn_act(act, l, which):
            n = 2 * DEPTH + 3 * l + which
            norm_act(act, n)
            lin = PLAN["ffn1" if which == 0 else "ffn2", l]
            for g in turns(act, lin, tail=2):
                splits_ahead(split_high, act, lin, g)
                act.wait_ge(used[slot_of(lin, g, 0)], turn_of(lin, g, 0) + 1)
                act.activation(tmp2[:, parity(lin, g), 0:norm_width(n)],
                               bank[2 * parity(lin, g)][:, 0:norm_width(n)], ACT.Silu).then_inc(s.silu, 1)
            out = PLAN["ffn1_out" if which == 0 else "ffn2_out", l]
            if not out.split:
                return
            first_split(split_high, act, out)
            wait_drained(act, lin, lin.n - 1)
            for k in range(KT):
                act.activation(hn_hi[:, k, 0:norm_width(n)], hid2[:, KT + k, 0:norm_width(n)],
                               ACT.Copy).then_inc(s.hid_hi, 1)
            for g in turns(act, out, tail=2):
                splits_ahead(split_high, act, out, g, after_ffn(l, which))

        def after_ffn(l, which):
            if which == 0:
                return PLAN["conv_in", l]
            return PLAN["ffn1", l + 1] if l < DEPTH - 1 else None

        def ffn_dve(dve, l, which):
            w = norm_width(2 * DEPTH + 3 * l + which)
            gated_norm_dve(dve, l, which)
            lin = PLAN["ffn1" if which == 0 else "ffn2", l]
            before = FF2 * (2 * l + which // 2)
            out = PLAN["ffn1_out" if which == 0 else "ffn2_out", l]
            for g in turns(dve, lin, tail=2):
                splits_ahead(split_low, dve, lin, g)
                wait_products(dve, lin, g)
                dve.wait_ge(s.silu, g.m + (before + 1))
                q = parity(lin, g)
                dve.tensor_tensor(hid2[:, g.m, 0:w], bank[2 * q + 1][:, 0:w], tmp2[:, q, 0:w],
                                  ALU.mult).then_inc(drained[q], 1)
            if out.split:
                first_split(split_low, dve, out)
                for k in range(KT):
                    dve.wait_ge(s.hid_hi, KT * hid_split_number(out) + k + 1)
                    dve.tensor_tensor(hn_lo[:, k, 0:w], hid2[:, KT + k, 0:w], hn_hi[:, k, 0:w].bitcast(F32),
                                      ALU.subtract).then_inc(s.hid_lo, 1)
            n = 2 * DEPTH + 3 * l + which
            gated_add(dve, l, out, which, w, after_ffn(l, which), norm_width(n + 1))

        def fourier_steps(l):
            first = [(1, c, tt, gp) for c in range(seqs(l)) for tt in range(TT) for gp in range(2)]
            steps = first + [(2, g, 0, 0) for g in range(G4)]
            u0 = sum(len(fourier_steps(i)) for i in range(l))
            return [(u0 + n,) + x for n, x in enumerate(steps)]

        def fourier_pe(pe, l):
            wait_all_drained(pe, PLAN["lat_in", l])
            for u, stage, a, tt, gp in fourier_steps(l):
                b = bank[4 + u % 2]
                if u >= 2:
                    pe.wait_ge(s.f_sb, u - 1)
                if stage == 1:
                    for j in range(2):
                        mm = pe.matmul(b[:, j * T:(j + 1) * T],
                                       z[:, 6 + 2 * gp + j, a * T + tt * P:a * T + (tt + 1) * P], dft_c,
                                       start=True, stop=True)
                else:
                    if a == 0:
                        pe.wait_ge(s.f_sb, u)
                    for c in range(seqs(l)):
                        for i in range(4):
                            mm = pe.matmul(b[:, c * T:(c + 1) * T],
                                           f1[:, c, i // 2, a, (i % 2) * P:(i % 2 + 1) * P],
                                           dft_t[:, i // 2, i % 2, :], start=(i == 0), stop=(i == 3))
                mm.then_inc(s.f_mm, 1)

        def fourier_act(act, l):
            for u, stage, a, tt, gp in fourier_steps(l):
                act.wait_ge(s.f_mm, u + 1)
                b = bank[4 + u % 2]
                if stage == 1:
                    act.activation(f1[:, a, tt, 2 * gp:2 * gp + 2, :], b[:, :].rearrange("p (g c) -> p g c", g=2),
                                   ACT.Copy).then_inc(s.f_sb, 1)
                else:
                    act.activation(four[:, a, 0:seqs(l) * T], b[:, 0:seqs(l) * T], ACT.Copy).then_inc(s.f_sb, 1)

        BRANCHES = (("mrg_conv", 3, 0), ("mrg_four", 4, 16), ("mrg_mla", 4, 8))

        def branch_pe(pe, l, b, g):
            name, kt, _ = BRANCHES[b]
            w = seqs(l) * T
            lin = PLAN[name, l]
            src = (cvo, four, att)[b]
            wait_banks(pe, lin, g)
            for k in range(kt):
                if k == 0:
                    wait_weights(pe, lin, g, 0)
                mm = pe.matmul(bank[2 * parity(lin, g)][:, 0:w], ring[:, slot_of(lin, g, 0), k * P:(k + 1) * P],
                               src[:, k, 0:w], start=(k == 0), stop=(k == kt - 1))
            mm.then_inc(used[slot_of(lin, g, 0)], 1)
            input_product(pe, lin, g, 1, bank[2 * parity(lin, g) + 1][:, 0:w], 2 * DEPTH + 3 * l + 1, w)

        def after_branch(l, b):
            return PLAN[BRANCHES[b + 1][0], l] if b < 2 else None

        def branch_act(act, l, b, g):
            name, _, tile0 = BRANCHES[b]
            w = seqs(l) * T
            lin = PLAN[name, l]
            bias = param(f"bbg@@{l}").rearrange("p (m c) -> p m c", c=1)
            splits_ahead(split_high, act, lin, g, after_branch(l, b))
            wait_products(act, lin, g)
            act.activation(tmp2[:, parity(lin, g), 0:w], bank[2 * parity(lin, g) + 1][:, 0:w], ACT.Sigmoid,
                           bias=bias[:, g.m + tile0, :]).then_inc(s.sig_g, 1)

        def branch_dve(dve, l, b, g):
            w = seqs(l) * T
            lin = PLAN[BRANCHES[b][0], l]
            q = parity(lin, g)
            splits_ahead(split_low, dve, lin, g, after_branch(l, b))
            dve.wait_ge(s.sig_g, g.m + (KT * (3 * l + b) + 1))
            if b < 2:
                bias = param((f"bpw@@{l}", f"bfour@@{l}")[b]).rearrange("p (m c) -> p m c", c=1)[:, g.m, :]
            else:
                bias = 0.0
            dst = mrg[:, g.m, 0:w] if b == 0 else tmp4[q][:, 0:w]
            one = dve.scalar_tensor_tensor(out=dst, in0=bank[2 * q][:, 0:w], scalar=bias, in1=tmp2[:, q, 0:w],
                                           op0=ALU.add, op1=ALU.mult)
            if b == 0:
                one.then_inc(drained[q], 1)
            else:
                dve.drain()
                dve.tensor_tensor(mrg[:, g.m, 0:w], mrg[:, g.m, 0:w], tmp4[q][:, 0:w],
                                  ALU.add).then_inc(drained[q], 1)

        def between_units(branch, eng, l, n):
            if 0 <= n < 2 * KT:
                branch(eng, l, n // KT, Group(n % KT, n % KT, 0, period(2)))

        def block2_pe(pe, l):
            n = 2 * DEPTH + 3 * l
            if l == 0:
                pe.wait_ge(s.consts2, 32)
            ffn_pe(pe, l, 0)
            norm_pe(pe, n + 1)
            w = seqs(l) * T
            gated_pair(pe, PLAN["conv_in", l], n + 1, w)
            lin = PLAN["lat_in", l]
            for m in range(lin.n):
                g, wg = Group(m, m, 0, lin.n), 2 * T if m < 3 else w
                wait_banks(pe, lin, g)
                input_product(pe, lin, g, 0, bank[2 * parity(lin, g)][:, 0:wg], n + 1, wg)
            pe.wait_ge(s.c_sq, l + 1)
            for k in range(3):
                mm = pe.matmul(bank[6][:, 0:w], const(2, "ones_ct"), q2[:, 3 + k, 0:w], start=(k == 0), stop=(k == 2))
            mm.then_inc(s.c_ms, 1)
            for k in range(2):
                mm = pe.matmul(bank[7][:, :], const(2, "ones_kv"), q2[:, 6 + k, :], start=(k == 0), stop=(k == 1))
            mm.then_inc(s.c_ms, 1)
            fourier_pe(pe, l)
            pe.wait_ge(s.cv_done, l + 1)
            pe.wait_ge(s.f_sb, fourier_steps(l)[-1][0] + 1)
            for k in range(CT):
                mm = pe.matmul(bank[4][:, 0:w], const(2, "ones_ct"), cvo[:, k, 0:w], start=(k == 0), stop=(k == CT - 1))
            mm.then_inc(s.ln_ms, 1)
            pe.wait_ge(s.c_n, l + 1)
            pe.matmul(bank[6][:, 0:T], const(2, "rot96"), z[:, 2, 0:T], start=True, stop=True).then_inc(s.kr_rot, 1)
            lin = PLAN["uq", l]
            for g in turns(pe, lin):
                wait_banks(pe, lin, g)
                wait_weights(pe, lin, g, 0)
                for k in range(3):
                    mm = pe.matmul(bank[2 * parity(lin, g)][:, 0:w], ring[:, slot_of(lin, g, 0), k * P:(k + 1) * P],
                                   z[:, 3 + k, 0:w], start=(k == 0), stop=(k == 2))
                mm.then_inc(used[slot_of(lin, g, 0)], 1)
            pe.wait_ge(s.ln_sq, l + 1)
            for k in range(CT):
                mm = pe.matmul(bank[5][:, 0:w], const(2, "ones_ct"), cvq[:, k, 0:w], start=(k == 0), stop=(k == CT - 1))
            mm.then_inc(s.ln_ms, 1)
            lin = PLAN["uk", l]
            for g in turns(pe, lin):
                wait_banks(pe, lin, g)
                wait_weights(pe, lin, g, 0)
                for k in range(2):
                    mm = pe.matmul(bank[2 * parity(lin, g)][:, :], ring[:, slot_of(lin, g, 0), k * P:(k + 1) * P],
                                   z[:, k, :], start=(k == 0), stop=(k == 1))
                mm.then_inc(used[slot_of(lin, g, 0)], 1)
            pe.wait_ge(s.kr_done, l + 1)
            pe.wait_ge(s.ln_n, l + 1)
            lin = PLAN["uv", l]
            for g in turns(pe, lin):
                wait_weights(pe, lin, g, 0)
                for tt in range(4):
                    for k in range(2):
                        mm = pe.matmul(bank[4 + tt][:, :], z[:, k, tt * P:(tt + 1) * P],
                                       ring[:, slot_of(lin, g, 0), k * 4 * P:(k + 1) * 4 * P],
                                       start=(k == 0), stop=(k == 1))
                mm.then_inc(used[slot_of(lin, g, 0)], 1)
            wait_all_drained(pe, PLAN["uq", l])
            pe.wait_ge(s.v_done, 4 * (l + 1))
            for u in range(4):
                if u >= 2:
                    pe.wait_ge(s.q_done, 4 * l + u - 1)
                pe.matmul(bank[4 + u % 2][:, :], const(2, "rot96"), q2[:, 2 * u:2 * u + 2, 0:T],
                          start=True, stop=True).then_inc(s.q_rot, 1)
            wait_all_drained(pe, PLAN["uk", l])
            pe.wait_ge(s.q_done, 4 * (l + 1))
            units = units_block2(l)
            pe.wait_ge(s.ln_out, l + 1)
            for i in range(len(units) + 2):
                between_units(branch_pe, pe, l, i)
                if i < len(units):
                    latent_scores(pe, units[i])
                if 1 <= i <= len(units):
                    latent_turn(pe, units[i - 1])
                if i >= 2:
                    latent_values(pe, units[i - 2])
            pe.wait_ge(s.att_o, units[-1].o + 1)
            for g in turns(pe, PLAN["mrg_mla", l]):
                branch_pe(pe, l, 2, g)
            wait_all_drained(pe, PLAN["mrg_mla", l])
            lin = PLAN["mix_out", l]
            for g in turns(pe, lin):
                wait_banks(pe, lin, g)
                wait_weights(pe, lin, g, 0)
                for k in range(KT):
                    mm = pe.matmul(bank[2 * parity(lin, g)][:, 0:w], ring[:, slot_of(lin, g, 0), k * P:(k + 1) * P],
                                   mrg[:, k, 0:w], start=(k == 0), stop=(k == KT - 1))
                mm.then_inc(used[slot_of(lin, g, 0)], 1)
            ffn_pe(pe, l, 2)

        def block2_act(act, l):
            n = 2 * DEPTH + 3 * l
            w = seqs(l) * T
            ffn_act(act, l, 0)
            norm_act(act, n + 1)
            lin = PLAN["conv_in", l]
            for g in turns(act, lin, tail=2):
                splits_ahead(split_high, act, lin, g, PLAN["lat_in", l])
                wait_products(act, lin, g)
                act.activation(tmp2[:, parity(lin, g), 0:w], bank[2 * parity(lin, g) + 1][:, 0:w],
                               ACT.Sigmoid).then_inc(s.cv_in, 1)
            lin = PLAN["lat_in", l]
            for g in range(lin.n):
                g = Group(g, g, 0, period(1))
                splits_ahead(split_high, act, lin, g)
                wait_products(act, lin, g)
                wg = 2 * T if g.m < 3 else w
                act.activation(z[:, g.m, 0:wg], bank[2 * parity(lin, g)][:, 0:wg],
                               ACT.Copy).then_inc(drained[parity(lin, g)], 1)
                if g.m == 5:
                    act.drain()
                    act.activation(q2[:, 3:6, 0:w], z[:, 3:6, 0:w], ACT.Square)
                    act.activation(q2[:, 6:8, :], z[:, 0:2, :], ACT.Square).then_inc(s.c_sq, 1)
            for i, (b, wi) in enumerate(((6, w), (7, 2 * T))):
                act.wait_ge(s.c_ms, 2 * l + i + 1)
                act.activation(tmp3[:, i, 0:wi], bank[b][:, 0:wi], ACT.Ln, bias=eps_col)
                act.drain()
                last = act.activation(tmp3[:, i, 0:wi], tmp3[:, i, 0:wi], ACT.Exp, scale=-0.5)
            last.then_inc(s.c_rs, 1)
            fourier_act(act, l)
            act.wait_ge(s.ln_cen, l + 1)
            act.activation(cvq[:, :, 0:w], cvo[:, :, 0:w], ACT.Square).then_inc(s.ln_sq, 1)
            lin = PLAN["uq", l]
            for g in turns(act, lin):
                wait_products(act, lin, g)
                act.activation(q2[:, g.m, 0:w], bank[2 * parity(lin, g)][:, 0:w],
                               ACT.Copy).then_inc(drained[parity(lin, g)], 1)
            act.wait_ge(s.ln_ms, 2 * l + 2)
            act.activation(lnb2[:, 0:w], bank[5][:, 0:w], ACT.Ln, bias=eps_col)
            act.drain()
            act.activation(rstd2[:, 0:w], lnb2[:, 0:w], ACT.Exp, scale=-0.5).then_inc(s.ln_rs, 1)
            act.wait_ge(s.ln_n, l + 1)
            for k in range(CT):
                last = act.activation(cvo[:, k, 0:w], cvo[:, k, 0:w], ACT.Silu, bias=param(f"lnb@@{l}")[:, k:k + 1])
            last.then_inc(s.ln_out, 1)
            lin = PLAN["uv", l]
            for g in turns(act, lin):
                wait_products(act, lin, g)
                for tt in range(4):
                    act.activation(v2[:, tt, :], bank[4 + tt][:, :], ACT.Copy).then_inc(s.v_done, 1)
            units = units_block2(l)
            first_split(split_high, act, PLAN["mrg_conv", l])
            for i in range(len(units) + 2):
                between_units(branch_act, act, l, i)
                if i < len(units):
                    latent_exp(act, units[i])
                if 1 <= i <= len(units):
                    latent_copy(act, units[i - 1])
                if i >= 2:
                    latent_out(act, units[i - 2])
            for g in turns(act, PLAN["mrg_mla", l], tail=2):
                branch_act(act, l, 2, g)
            if PLAN["ffn2", l].split:
                first_split(split_high, act, PLAN["ffn2", l])
            ffn_act(act, l, 2)

        def block2_dve(dve, l):
            w = seqs(l) * T
            if l == 0:
                dve.wait_ge(s.consts2, 32)
            dve.drain()
            mod = modulation(l)
            for i, name in enumerate(("g1", "gm", "g2")):
                dve.scalar_tensor_tensor(out=gs[:, i, :, :], in0=mod[:, SCALE[i], :, :], scalar=1.0,
                                         in1=param(f"{name}@@{l}").unsqueeze(2).broadcast_to([P, KT, 2]),
                                         op0=ALU.add, op1=ALU.mult)
            for i in (0, 2):
                dve.tensor_scalar(mod[:, GATE[i], :, :], mod[:, GATE[i], :, :], 0.5, None, ALU.mult)
            dve.drain()
            ffn_dve(dve, l, 0)
            gated_norm_dve(dve, l, 1)
            lin = PLAN["conv_in", l]
            dve.wait_ge(s.padded, l + 1)
            for g in turns(dve, lin, tail=2):
                splits_ahead(split_low, dve, lin, g)
                wait_products(dve, lin, g)
                dve.wait_ge(s.cv_in, CT * l + g.m + 1)
                dve.tensor_tensor(cvp[:, g.m, 0:seqs(l), PAD:PAD + T], both(bank[2 * parity(lin, g)], w),
                                  both(tmp2[:, parity(lin, g), :], w), ALU.mult).then_inc(drained[parity(lin, g)], 1)
            taps = param(f"dw@@{l}").rearrange("p (m k) -> p m k", k=CONV_K)
            dve.drain()
            for k in range(CONV_K):
                for m in range(CT):
                    src = cvp[:, m, 0:seqs(l), k:k + T]
                    dst = both(cvo[:, m, :], w)
                    if k == 0:
                        last = dve.tensor_scalar(dst, src, taps[:, m, 0:1], param(f"bdw@@{l}")[:, m:m + 1],
                                                 ALU.mult, ALU.add)
                    else:
                        last = dve.scalar_tensor_tensor(out=dst, in0=src, scalar=taps[:, m, k:k + 1], in1=dst,
                                                        op0=ALU.mult, op1=ALU.add)
                if k < CONV_K - 1:
                    dve.drain()
            last.then_inc(s.cv_done, 1)
            dve.wait_ge(s.c_rs, l + 1)
            for k in range(3):
                dve.scalar_tensor_tensor(out=z[:, 3 + k, 0:w], in0=z[:, 3 + k, 0:w], scalar=param(f"gq@@{l}")[:, k:k + 1],
                                         in1=tmp3[:, 0, 0:w], op0=ALU.mult, op1=ALU.mult)
            for k in range(2):
                last = dve.scalar_tensor_tensor(out=z[:, k, :], in0=z[:, k, :], scalar=param(f"gkv@@{l}")[:, k:k + 1],
                                                in1=tmp3[:, 1, :], op0=ALU.mult, op1=ALU.mult)
            last.then_inc(s.c_n, 1)
            dve.wait_ge(s.ln_ms, 2 * l + 1)
            for k in range(CT):
                last = dve.tensor_tensor(cvo[:, k, 0:w], cvo[:, k, 0:w], bank[4][:, 0:w], ALU.subtract)
            last.then_inc(s.ln_cen, 1)
            dve.wait_ge(s.kr_rot, l + 1)
            mcos, msin = const(2, "mcos"), const(2, "msin")
            dve.tensor_tensor(tmp3[:, 0, 0:T], bank[6][:, 0:T], msin, ALU.mult)
            dve.tensor_tensor(z[:, 2, 0:T], z[:, 2, 0:T], mcos, ALU.mult)
            dve.drain()
            dve.tensor_tensor(z[:, 2, 0:T], z[:, 2, 0:T], tmp3[:, 0, 0:T], ALU.add).then_inc(s.kr_done, 1)
            dve.wait_ge(s.ln_rs, l + 1)
            for k in range(CT):
                last = dve.scalar_tensor_tensor(out=cvo[:, k, 0:w], in0=cvo[:, k, 0:w],
                                                scalar=param(f"lng@@{l}")[:, k:k + 1], in1=rstd2[:, 0:w],
                                                op0=ALU.mult, op1=ALU.mult)
            last.then_inc(s.ln_n, 1)
            dve.drain()
            lin = PLAN["uk", l]
            for g in turns(dve, lin):
                wait_products(dve, lin, g)
                dve.tensor_tensor(k2[:, g.m, :], bank[2 * parity(lin, g)][:, :], z[:, 2, :],
                                  ALU.add).then_inc(drained[parity(lin, g)], 1)
            for u in range(4):
                dve.wait_ge(s.q_rot, 4 * l + u + 1)
                dst = q2[:, 2 * u:2 * u + 2, 0:T]
                b = both(bank[4 + u % 2], 2 * T)
                t3 = both(tmp3[:, 0, :], 2 * T)
                dve.tensor_tensor(dst, dst, mcos.unsqueeze(1).broadcast_to([P, 2, T]), ALU.mult)
                dve.tensor_tensor(t3, b, msin.unsqueeze(1).broadcast_to([P, 2, T]), ALU.mult)
                dve.drain()
                dve.tensor_tensor(dst, dst, t3, ALU.add).then_inc(s.q_done, 1)
                dve.drain()
            units = units_block2(l)
            first_split(split_low, dve, PLAN["mrg_conv", l])
            for i in range(len(units) + 2):
                if 1 <= i <= len(units):
                    latent_norm(dve, units[i - 1])
                between_units(branch_dve, dve, l, i)
                if i < len(units):
                    latent_max(dve, units[i])
            for g in turns(dve, PLAN["mrg_mla", l], tail=2):
                branch_dve(dve, l, 2, g)
            gated_add(dve, l, PLAN["mix_out", l], 1, w, PLAN["ffn2", l] if PLAN["ffn2", l].split else None,
                      norm_width(2 * DEPTH + 3 * l + 2))
            ffn_dve(dve, l, 2)

        def pad_pool(pool, l):
            wait_all_drained(pool, PLAN["ffn1_out", l])
            if l >= 1:
                pool.wait_ge(s.padded, l)
            pool.memset(cvp_b, 0.0).then_inc(s.padded, 1)

        block = stack.enter_context(nc.Block())

        @block.sync
        def _(sp):
            for seg in SEGMENTS:
                if seg.chunk >= limit:
                    break
                n_pat = len(seg.pattern)
                per = period(n_pat)
                times = min(seg.times, (limit - seg.chunk) // n_pat)

                def load(k, at, i):
                    for c, w in enumerate(seg.pattern):
                        chunk = seg.chunk + at * n_pat + c
                        slot, turn = chunk % SLOTS, chunk // SLOTS + i * (per * n_pat // SLOTS)
                        if not (isinstance(turn, int) and turn == 0):
                            sp.wait_ge(used[slot], turn)
                        number = k * seg.pattern.count(w) + (seg.at.get(w, 0) + seg.pattern[:c].count(w))
                        sp.dma_start(ring[:, slot, 0:w * P], streams[w][number]).then_inc(landed[slot], 16)

                first = per if seg.chunk < SLOTS else 0
                for k in range(min(first, times)):
                    load(k, k, 0)
                end = times // per
                if end - first // per >= 2:
                    with sp.Fori(first // per, end) as i:
                        for j in range(per):
                            load(i * per + j, j, i)
                    rest = end * per
                else:
                    rest = first
                for k in range(rest, times):
                    load(k, k, 0)
            sp.wait_ge(s.final, KT)
            sp.dma_start(out_cm, sq[:, :, 0:T]).then_inc(s.stored, 16)
            sp.wait_ge(s.stored, 16)

        @block.tensor
        def _(pe):
            pe.wait_ge(s.consts, 48)
            pe.wait_ge(s.csilu, 1)
            for l in range(DEPTH):
                block1_pe(pe, l)
            if 2 in blocks:
                for l in range(DEPTH):
                    block2_pe(pe, l)
                norm_pe(pe, LAST_NORM)

        @block.scalar
        def _(act):
            act.dma_start(res[:, :, 0:T], x_cm).then_inc(s.x_in, 16)
            act.dma_start(con0[:, :], consts[0]).then_inc(s.consts, 16)
            act.dma_start(par0[:, :], params[0]).then_inc(s.consts, 16)
            act.dma_start(par12[:, 0:PARAM_SETS[1][1]], params[1]).then_inc(s.consts, 16)
            act.dma_start(con12[:, 0:CONST_SETS[1][1]], consts[1]).then_inc(s.consts1, 16)
            act.dma_start(res[:, :, T:2 * T], ctx_cm).then_inc(s.ctx_in, 16)
            act.wait_ge(s.consts, 48)
            act.activation(conds[:, :], param("cvec"), ACT.Silu).then_inc(s.csilu, 1)
            for l in range(DEPTH):
                block1_act(act, l)
            if 2 in blocks:
                act.wait_ge(s.mixa, DEPTH)
                act.dma_start(con12[:, 0:CONST_SETS[2][1]], consts[2]).then_inc(s.consts2, 16)
                act.dma_start(par12[:, 0:PARAM_SETS[2][1]], params[2]).then_inc(s.consts2, 16)
                for l in range(DEPTH):
                    block2_act(act, l)
                norm_act(act, LAST_NORM)
            else:
                act.wait_ge(s.ctx_in, 16)

        @block.vector
        def _(dve):
            dve.memset(eps_col, EPS)
            dve.memset(one_col, 1.0)
            dve.drain()
            dve.memset(sumsq, 0.0)
            dve.wait_ge(s.consts, 48)
            for l in range(DEPTH):
                if l == 0:
                    dve.wait_ge(s.x_in, 16)
                    for k in range(KT):
                        square(dve, k, 0, T).then_inc(s.squares, 1)
                        dve.drain()
                block1_dve(dve, l)
            if 2 in blocks:
                for l in range(DEPTH):
                    block2_dve(dve, l)
                dve.wait_ge(s.rstd, LAST_NORM + 1)
                for k in range(KT):
                    dve.scalar_tensor_tensor(out=sq[:, k, 0:T], in0=res[:, k, 0:T], scalar=param("gfin")[:, k:k + 1],
                                             in1=rstd[:, 0:T], op0=ALU.mult, op1=ALU.mult).then_inc(s.final, 1)
            else:
                dve.drain()
                for k in range(KT):
                    dve.tensor_copy(sq[:, k, 0:T], res[:, k, 0:T]).then_inc(s.final, 1)

        @block.gpsimd
        def _(pool):
            pool.wait_ge(s.consts, 48)
            for l in range(DEPTH):
                block1_pool(pool, l)
            if 2 in blocks:
                for l in range(DEPTH):
                    pad_pool(pool, l)
                    for g in turns(pool, PLAN["lat_in", l]):
                        split_low(pool, PLAN["lat_in", l], g, 0)


def kernel(**inputs):
    import numpy as _np
    import concourse.bacc as _bacc
    from concourse import mybir as _mybir
    from concourse.bass_utils import run_bass_kernel_spmd as _run

    a = {name: _np.asarray(v) for name, v in inputs.items()}
    nc = _bacc.Bacc("TRN2", target_bir_lowering=False, num_devices=1)
    arrays = {}

    def given(name, v):
        arrays[name] = _np.ascontiguousarray(v)
        return nc.dram_tensor(name, v.shape, _mybir.dt.from_np(v.dtype), kind="ExternalInput").ap()

    streams = {w: given(f"weights_{w}", v) for w, v in pack_stream(a).items()}
    consts = [given(f"consts_{k}", v) for k, v in enumerate(shape_constants())]
    params = [given(f"params_{k}", v) for k, v in enumerate(pack_params(a))]
    x_cm = given("x_cm", channel_major(a["x"][0]))
    ctx_cm = given("ctx_cm", channel_major(a["ctx_2"][0]))
    out_cm = nc.dram_tensor("out_cm", (P, KT, T), F32, kind="ExternalOutput").ap()
    kernel_program(nc, streams, consts, params, x_cm, ctx_cm, out_cm)
    out = _run(nc, [arrays], core_ids=[0]).results[0]["out_cm"]
    return out.transpose(1, 0, 2).reshape(D, T).T.reshape(1, T, D)
```
